# Optimizing a Trainium2 kernel written in Bass

```python
import math
import jax, jax.numpy as jnp
from jax import lax
import numpy as np

D_MODEL = 1024
BATCH = 1
SEQ = 512
DEPTH = 1

HEAD_DIM = 64
FOX_HEADS = 8
NSA_HEADS = 8
NSA_KV_HEADS = 2
CMP_BLOCK = 32
CMP_STRIDE = 16
CMP_HIDDEN = 256
SLC_BLOCK = 64
SLC_TOPK = 16
WINDOW = 512
Q_BLOCK = 128
N_GROUPS = 4
EXPERTS_PER_GROUP = 4
N_EXPERTS = N_GROUPS * EXPERTS_PER_GROUP
TOP_K_IN_GROUP = 2
D_EXPERT = 512
RMS_EPS = 1e-6
NEG_INF = -1e30
FORCE_SCORE = 1e4

FOX_W = FOX_HEADS * HEAD_DIM
NSA_W = NSA_HEADS * HEAD_DIM
NSA_KV_W = NSA_KV_HEADS * HEAD_DIM
IN_COLS = (FOX_W, FOX_W, FOX_W, FOX_HEADS,
           NSA_W, NSA_KV_W, NSA_KV_W, NSA_KV_W, NSA_KV_W, NSA_KV_W, NSA_KV_W, 3 * NSA_HEADS,
           D_MODEL, D_MODEL)
D_IN = sum(IN_COLS)


def rms_norm(x, g):
    xf = x.astype(jnp.float32)
    y = xf * lax.rsqrt(jnp.mean(xf * xf, axis=-1, keepdims=True) + RMS_EPS)
    return (y * g.astype(jnp.float32)).astype(x.dtype)

def split_cols(z):
    outs, off = [], 0
    for c in IN_COLS:
        outs.append(z[..., off:off + c])
        off += c
    return outs

def to_heads(t, n):
    B, S, _ = t.shape
    return t.reshape(B, S, n, HEAD_DIM).transpose(0, 2, 1, 3)

def from_heads(t):
    B, n, S, dh = t.shape
    return t.transpose(0, 2, 1, 3).reshape(B, S, n * dh)

def alibi_slopes(n):
    return jnp.asarray([2.0 ** (-8.0 * (h + 1) / n) for h in range(n)], jnp.float32)

def fox_attention(q, k, v, log_f):
    B, H, S, dh = q.shape
    cum = jnp.cumsum(log_f, axis=-1)
    scale = dh ** -0.5
    kpos = jnp.arange(S)

    def block(i):
        q0 = i * Q_BLOCK
        qpos = q0 + jnp.arange(Q_BLOCK)
        qb = lax.dynamic_slice_in_dim(q, q0, Q_BLOCK, axis=2)
        cb = lax.dynamic_slice_in_dim(cum, q0, Q_BLOCK, axis=2)
        s = jnp.einsum('bhqd,bhkd->bhqk', qb, k, preferred_element_type=jnp.float32) * scale
        s = s + cb[..., :, None] - cum[..., None, :]
        s = jnp.where(kpos[None, :] <= qpos[:, None], s, NEG_INF)
        p = jax.nn.softmax(s, axis=-1)
        return jnp.einsum('bhqk,bhkd->bhqd', p.astype(v.dtype), v)

    o = lax.map(block, jnp.arange(S // Q_BLOCK))
    return jnp.moveaxis(o, 0, 2).reshape(B, H, S, dh)

def compress_blocks(t, w1, w2, pos):
    B, S, G, dh = t.shape
    n_cmp = (S - CMP_BLOCK) // CMP_STRIDE + 1
    idx = jnp.arange(n_cmp)[:, None] * CMP_STRIDE + jnp.arange(CMP_BLOCK)[None, :]
    blk = t[:, idx] + pos[None, None, :, None, :]
    blk = jnp.moveaxis(blk, 3, 1).reshape(B, G, n_cmp, CMP_BLOCK * dh)
    return jax.nn.gelu(blk @ w1) @ w2

def nsa_attention(q, k_cmp, v_cmp, k_slc, v_slc, k_win, v_win, gates):
    B, H, S, dh = q.shape
    G = k_slc.shape[1]
    R = H // G
    n_cmp = k_cmp.shape[2]
    n_slc = S // SLC_BLOCK
    top_n = min(SLC_TOPK, n_slc)
    scale = dh ** -0.5
    slopes = alibi_slopes(H).reshape(G, R)[None, :, :, None, None]

    cmp_start = jnp.arange(n_cmp) * CMP_STRIDE
    cmp_end = cmp_start + CMP_BLOCK - 1
    slc_start = jnp.arange(n_slc) * SLC_BLOCK
    ov = jnp.minimum(cmp_start[:, None] + CMP_BLOCK, slc_start[None, :] + SLC_BLOCK) - \
        jnp.maximum(cmp_start[:, None], slc_start[None, :])
    overlap = jnp.clip(ov, 0, None).astype(jnp.float32) / CMP_BLOCK
    slc_ids = jnp.arange(n_slc)

    k_sb = k_slc.reshape(B, G, n_slc, SLC_BLOCK, dh)
    v_sb = v_slc.reshape(B, G, n_slc, SLC_BLOCK, dh)
    pad = ((0, 0), (0, 0), (WINDOW, 0), (0, 0))
    k_wp = jnp.pad(k_win, pad)
    v_wp = jnp.pad(v_win, pad)
    gather = jax.vmap(jax.vmap(lambda blocks, idx: blocks[idx]))

    def block(i):
        q0 = i * Q_BLOCK
        qpos = q0 + jnp.arange(Q_BLOCK)
        qb = lax.dynamic_slice_in_dim(q, q0, Q_BLOCK, axis=2).reshape(B, G, R, Q_BLOCK, dh)

        s = jnp.einsum('bgrqd,bgnd->bgrqn', qb, k_cmp, preferred_element_type=jnp.float32) * scale
        dist = (qpos[:, None] - cmp_end[None, :]).astype(jnp.float32)
        valid = dist >= 0
        s = jnp.where(valid, s - slopes * dist, NEG_INF)
        p_cmp = jax.nn.softmax(s, axis=-1) * jnp.any(valid, axis=-1)[:, None].astype(jnp.float32)
        o_cmp = jnp.einsum('bgrqn,bgnd->bgrqd', p_cmp.astype(v_cmp.dtype), v_cmp)

        imp = jnp.einsum('bgrqn,nj->bgqj', p_cmp, overlap)
        qblk = qpos // SLC_BLOCK
        forced = (slc_ids[None, :] == 0) | (slc_ids[None, :] == qblk[:, None]) | \
            (slc_ids[None, :] == qblk[:, None] - 1)
        future = slc_ids[None, :] * SLC_BLOCK > qpos[:, None]
        score = jnp.where(future, -1.0, jnp.where(forced, FORCE_SCORE, imp))
        _, idx = lax.top_k(score, top_n)
        n_tok = top_n * SLC_BLOCK
        ks_g = gather(k_sb, idx).reshape(B, G, Q_BLOCK, n_tok, dh)
        vs_g = gather(v_sb, idx).reshape(B, G, Q_BLOCK, n_tok, dh)
        spos = (idx[..., None] * SLC_BLOCK + jnp.arange(SLC_BLOCK)).reshape(B, G, Q_BLOCK, n_tok)
        dist = (qpos[:, None] - spos).astype(jnp.float32)[:, :, None]
        s = jnp.einsum('bgrqd,bgqkd->bgrqk', qb, ks_g, preferred_element_type=jnp.float32) * scale
        s = jnp.where(dist >= 0, s - slopes * dist, NEG_INF)
        o_slc = jnp.einsum('bgrqk,bgqkd->bgrqd', jax.nn.softmax(s, axis=-1).astype(vs_g.dtype), vs_g)

        kw_b = lax.dynamic_slice_in_dim(k_wp, q0, WINDOW + Q_BLOCK, axis=2)
        vw_b = lax.dynamic_slice_in_dim(v_wp, q0, WINDOW + Q_BLOCK, axis=2)
        wpos = q0 - WINDOW + jnp.arange(WINDOW + Q_BLOCK)
        dist = (qpos[:, None] - wpos[None, :]).astype(jnp.float32)
        valid = (dist >= 0) & (dist < WINDOW) & (wpos[None, :] >= 0)
        s = jnp.einsum('bgrqd,bgkd->bgrqk', qb, kw_b, preferred_element_type=jnp.float32) * scale
        s = jnp.where(valid, s - slopes * dist, NEG_INF)
        o_win = jnp.einsum('bgrqk,bgkd->bgrqd', jax.nn.softmax(s, axis=-1).astype(vw_b.dtype), vw_b)

        gb = lax.dynamic_slice_in_dim(gates, q0, Q_BLOCK, axis=2).reshape(B, G, R, Q_BLOCK, 3)
        o = gb[..., 0:1] * o_cmp + gb[..., 1:2] * o_slc + gb[..., 2:3] * o_win
        return o.reshape(B, H, Q_BLOCK, dh)

    o = lax.map(block, jnp.arange(S // Q_BLOCK))
    return jnp.moveaxis(o, 0, 2).reshape(B, H, S, dh)

def hierarchical_moe(x, w_group, b_group, w_router, b_router, w_gate, w_up, w_down):
    B, S, D = x.shape
    t = x.reshape(B * S, D)
    g_logits = (t @ w_group).astype(jnp.float32) + b_group.astype(jnp.float32)
    p_g, g_top = lax.top_k(jax.nn.softmax(g_logits, axis=-1), 1)
    e_logits = ((t @ w_router).astype(jnp.float32) + b_router.astype(jnp.float32)).reshape(-1, N_GROUPS, EXPERTS_PER_GROUP)
    e_in = jnp.take_along_axis(e_logits, g_top[:, :, None], axis=1)[:, 0]
    top_p, top_i = lax.top_k(jax.nn.softmax(e_in, axis=-1), TOP_K_IN_GROUP)
    w = top_p / jnp.sum(top_p, axis=-1, keepdims=True) * p_g
    expert_id = g_top * EXPERTS_PER_GROUP + top_i
    combine = jnp.sum(jax.nn.one_hot(expert_id, N_EXPERTS, dtype=jnp.float32) * w[..., None], axis=1)
    hid = jax.nn.silu(jnp.einsum('td,edf->etf', t, w_gate)) * jnp.einsum('td,edf->etf', t, w_up)
    hid = hid * combine.T.astype(hid.dtype)[:, :, None]
    y = jnp.einsum('etf,efd->td', hid, w_down)
    return y.reshape(B, S, D)

def first_inputs(seed: int = 0) -> dict:
    key = jax.random.key(seed)
    ks = jax.random.split(key, 26)
    L = DEPTH

    def nrm(k, shape, scale):
        return jax.random.normal(k, shape, jnp.float32) * scale

    def gain(k, shape):
        return 1.0 + 0.02 * jax.random.normal(k, shape, jnp.float32)

    cmp_in = CMP_BLOCK * HEAD_DIM
    return {
        "x": nrm(ks[0], (BATCH, SEQ, D_MODEL), 1.0),
        "norm_mix_g": gain(ks[1], (L, D_MODEL)),
        "w_in": nrm(ks[2], (L, D_MODEL, D_IN), D_MODEL ** -0.5),
        "b_forget": jnp.linspace(1.0, 6.0, FOX_HEADS, dtype=jnp.float32)[None, :] + nrm(ks[3], (L, FOX_HEADS), 0.1),
        "fox_q_g": gain(ks[4], (L, HEAD_DIM)),
        "fox_k_g": gain(ks[5], (L, HEAD_DIM)),
        "nsa_q_g": gain(ks[6], (L, HEAD_DIM)),
        "nsa_k_g": gain(ks[7], (L, HEAD_DIM)),
        "cmp_k_w1": nrm(ks[8], (L, cmp_in, CMP_HIDDEN), cmp_in ** -0.5),
        "cmp_k_w2": nrm(ks[9], (L, CMP_HIDDEN, HEAD_DIM), CMP_HIDDEN ** -0.5),
        "cmp_k_pos": nrm(ks[10], (L, CMP_BLOCK, HEAD_DIM), 0.1),
        "cmp_v_w1": nrm(ks[11], (L, cmp_in, CMP_HIDDEN), cmp_in ** -0.5),
        "cmp_v_w2": nrm(ks[12], (L, CMP_HIDDEN, HEAD_DIM), CMP_HIDDEN ** -0.5),
        "cmp_v_pos": nrm(ks[13], (L, CMP_BLOCK, HEAD_DIM), 0.1),
        "w_fox_up": nrm(ks[14], (L, FOX_W, D_MODEL), FOX_W ** -0.5),
        "w_nsa_up": nrm(ks[15], (L, NSA_W, D_MODEL), NSA_W ** -0.5),
        "w_out": nrm(ks[16], (L, D_MODEL, D_MODEL), D_MODEL ** -0.5),
        "norm_ffn_g": gain(ks[17], (L, D_MODEL)),
        "w_group": nrm(ks[18], (L, D_MODEL, N_GROUPS), D_MODEL ** -0.5),
        "b_group": nrm(ks[19], (L, N_GROUPS), 0.01),
        "w_router": nrm(ks[20], (L, D_MODEL, N_EXPERTS), D_MODEL ** -0.5),
        "b_router": nrm(ks[21], (L, N_EXPERTS), 0.01),
        "w_gate": nrm(ks[22], (L, N_EXPERTS, D_MODEL, D_EXPERT), D_MODEL ** -0.5),
        "w_up": nrm(ks[23], (L, N_EXPERTS, D_MODEL, D_EXPERT), D_MODEL ** -0.5),
        "w_down": nrm(ks[24], (L, N_EXPERTS, D_EXPERT, D_MODEL), D_EXPERT ** -0.5),
    }

def first_block(x, norm_mix_g, w_in, b_forget, fox_q_g, fox_k_g, nsa_q_g, nsa_k_g,
              cmp_k_w1, cmp_k_w2, cmp_k_pos, cmp_v_w1, cmp_v_w2, cmp_v_pos,
              w_fox_up, w_nsa_up, w_out, norm_ffn_g, w_group, b_group, w_router, b_router,
              w_gate, w_up, w_down):
    B, S, D = x.shape
    for l in range(DEPTH):
        h = rms_norm(x, norm_mix_g[l])
        (f_q, f_k, f_v, f_f, n_q, k_c, v_c, k_s, v_s, k_w, v_w, n_g, g_a, g_b) = split_cols(h @ w_in[l])

        qa = rms_norm(to_heads(f_q, FOX_HEADS), fox_q_g[l])
        ka = rms_norm(to_heads(f_k, FOX_HEADS), fox_k_g[l])
        va = to_heads(f_v, FOX_HEADS)
        log_f = jax.nn.log_sigmoid(f_f.astype(jnp.float32) + b_forget[l].astype(jnp.float32)).transpose(0, 2, 1)
        out_a = from_heads(fox_attention(qa, ka, va, log_f)) @ w_fox_up[l]

        qb = rms_norm(to_heads(n_q, NSA_HEADS), nsa_q_g[l])
        kc = compress_blocks(k_c.reshape(B, S, NSA_KV_HEADS, HEAD_DIM), cmp_k_w1[l], cmp_k_w2[l], cmp_k_pos[l])
        kc = rms_norm(kc, nsa_k_g[l])
        vc = compress_blocks(v_c.reshape(B, S, NSA_KV_HEADS, HEAD_DIM), cmp_v_w1[l], cmp_v_w2[l], cmp_v_pos[l])
        ks_ = rms_norm(to_heads(k_s, NSA_KV_HEADS), nsa_k_g[l])
        vs_ = to_heads(v_s, NSA_KV_HEADS)
        kw_ = rms_norm(to_heads(k_w, NSA_KV_HEADS), nsa_k_g[l])
        vw_ = to_heads(v_w, NSA_KV_HEADS)
        gates = jax.nn.sigmoid(n_g.reshape(B, S, NSA_HEADS, 3)).transpose(0, 2, 1, 3)
        out_b = from_heads(nsa_attention(qb, kc, vc, ks_, vs_, kw_, vw_, gates)) @ w_nsa_up[l]

        mix = jax.nn.sigmoid(g_a) * out_a + jax.nn.sigmoid(g_b) * out_b
        x = x + mix @ w_out[l]

        x = x + hierarchical_moe(rms_norm(x, norm_ffn_g[l]), w_group[l], b_group[l], w_router[l], b_router[l],
                                 w_gate[l], w_up[l], w_down[l])
    return x


GRID_W = 64
EPS = 1e-6
NEG_INF_2 = -1e30

NA_HEADS = 8
NA_HEAD_DIM = 64
NA_WIN_H = 8
NA_WIN_W = 16
NA_QBLOCK_W = 16
NA_BAND_W = NA_QBLOCK_W + NA_WIN_W
NA_WIDTH = NA_HEADS * NA_HEAD_DIM

MLA_HEADS = 8
MLA_QK_NOPE = 64
MLA_QK_ROPE = 32
MLA_V_DIM = 64
MLA_Q_LORA = 256
MLA_KV_LORA = 128
MLA_QBLOCK = 128
MLA_WIDTH = MLA_HEADS * MLA_V_DIM
ROPE_THETA = 10000.0

MIX_WIDTH = NA_WIDTH + MLA_WIDTH
D_IN_2 = 3 * NA_WIDTH + MLA_Q_LORA + MLA_KV_LORA + MLA_QK_ROPE
D_FF = 2816


def rms_norm_2(x, g):
    xf = x.astype(jnp.float32)
    y = xf * lax.rsqrt(jnp.mean(xf * xf, axis=-1, keepdims=True) + EPS)
    return (y * g.astype(jnp.float32)).astype(x.dtype)

def swiglu(h, w_gu, w_down):
    gate, up = jnp.split(h @ w_gu, 2, axis=-1)
    return (jax.nn.silu(gate) * up) @ w_down

def grid_rope_tables(seq):
    t = jnp.arange(seq)
    row = (t // GRID_W).astype(jnp.float32)
    col = (t % GRID_W).astype(jnp.float32)
    n_freq = MLA_QK_ROPE // 4
    inv_freq = 1.0 / (ROPE_THETA ** (jnp.arange(n_freq, dtype=jnp.float32) / n_freq))
    ang = jnp.concatenate([row[:, None] * inv_freq[None, :], col[:, None] * inv_freq[None, :]], axis=-1)
    return jnp.cos(ang), jnp.sin(ang)

def apply_rope(x, cos, sin):
    xf = x.astype(jnp.float32)
    x1, x2 = jnp.split(xf, 2, axis=-1)
    return jnp.concatenate([x1 * cos - x2 * sin, x2 * cos + x1 * sin], axis=-1).astype(x.dtype)

def neighbourhood_attention(q, k, v, rpb):
    B, S, H, D = q.shape
    R = S // GRID_W
    KH = min(NA_WIN_H, R)
    NCB = GRID_W // NA_QBLOCK_W
    rows = jnp.arange(R)
    row_start = jnp.clip(rows - KH // 2, 0, R - KH)
    key_rows = row_start[:, None] + jnp.arange(KH)
    c0 = jnp.arange(NCB) * NA_QBLOCK_W
    band_start = jnp.clip(c0 - NA_WIN_W // 2, 0, GRID_W - NA_BAND_W)
    key_cols = band_start[:, None] + jnp.arange(NA_BAND_W)
    q_cols = c0[:, None] + jnp.arange(NA_QBLOCK_W)
    win_start = jnp.clip(q_cols - NA_WIN_W // 2, 0, GRID_W - NA_WIN_W)
    kc = key_cols[:, None, :]
    col_mask = (kc >= win_start[..., None]) & (kc < win_start[..., None] + NA_WIN_W)
    row_off = key_rows - rows[:, None] + (NA_WIN_H - 1)
    col_off = jnp.clip(kc - q_cols[:, :, None] + (NA_WIN_W - 1), 0, 2 * NA_WIN_W - 2)
    bias = rpb.astype(jnp.float32)[:, row_off[:, None, None, :, None], col_off[None, :, :, None, :]]
    bias = bias.transpose(1, 2, 0, 3, 4, 5)
    bias = jnp.where(col_mask[:, None, :, None, :], bias, NEG_INF_2)
    qg = q.reshape(B, R, NCB, NA_QBLOCK_W, H, D)
    ridx = key_rows[:, None, :, None]
    cidx = key_cols[None, :, None, :]
    kg = k.reshape(B, R, GRID_W, H, D)[:, ridx, cidx]
    vg = v.reshape(B, R, GRID_W, H, D)[:, ridx, cidx]
    s = jnp.einsum('brnqhd,brnijhd->brnhqij', qg, kg).astype(jnp.float32) * (D ** -0.5)
    s = s + bias[None]
    sh = s.shape
    p = jax.nn.softmax(s.reshape(sh[:-2] + (sh[-2] * sh[-1],)), axis=-1).reshape(sh)
    o = jnp.einsum('brnhqij,brnijhd->brnqhd', p.astype(v.dtype), vg)
    return o.reshape(B, S, H * D)

def latent_attention(c_q, c_kv, k_rope, q_norm_g, w_uq, kv_norm_g, w_ukv, cos, sin):
    B, S, _ = c_q.shape
    H = MLA_HEADS
    q = (rms_norm_2(c_q, q_norm_g) @ w_uq).reshape(B, S, H, MLA_QK_NOPE + MLA_QK_ROPE)
    q_nope, q_rot = jnp.split(q, [MLA_QK_NOPE], axis=-1)
    kv = (rms_norm_2(c_kv, kv_norm_g) @ w_ukv).reshape(B, S, H, MLA_QK_NOPE + MLA_V_DIM)
    k_nope, v = jnp.split(kv, [MLA_QK_NOPE], axis=-1)
    q_rot = apply_rope(q_rot, cos[:, None, :], sin[:, None, :])
    k_rot = apply_rope(k_rope, cos, sin)
    scale = (MLA_QK_NOPE + MLA_QK_ROPE) ** -0.5
    nqb = S // MLA_QBLOCK

    def block(args):
        qn, qr = args
        s = (jnp.einsum('bqhd,bkhd->bhqk', qn, k_nope)
             + jnp.einsum('bqhd,bkd->bhqk', qr, k_rot)).astype(jnp.float32) * scale
        p = jax.nn.softmax(s, axis=-1)
        return jnp.einsum('bhqk,bkhd->bqhd', p.astype(v.dtype), v)

    qn_b = q_nope.reshape(B, nqb, MLA_QBLOCK, H, MLA_QK_NOPE).swapaxes(0, 1)
    qr_b = q_rot.reshape(B, nqb, MLA_QBLOCK, H, MLA_QK_ROPE).swapaxes(0, 1)
    o = lax.map(block, (qn_b, qr_b))
    return o.swapaxes(0, 1).reshape(B, S, H * MLA_V_DIM)

def second_inputs(seed: int = 0) -> dict:
    key = jax.random.key(seed)
    ks = iter(jax.random.split(key, 32))

    def w(shape, fan_in):
        return jax.random.normal(next(ks), shape, jnp.float32) * (fan_in ** -0.5)

    def gain(n):
        return 1.0 + 0.05 * jax.random.normal(next(ks), (DEPTH, n), jnp.float32)

    L = DEPTH
    return {
        "x": jax.random.normal(next(ks), (BATCH, SEQ, D_MODEL), jnp.float32),
        "ffn1_pre_g": gain(D_MODEL),
        "ffn1_w_gu": w((L, D_MODEL, 2 * D_FF), D_MODEL),
        "ffn1_w_down": w((L, D_FF, D_MODEL), D_FF),
        "ffn1_post_g": gain(D_MODEL),
        "mix_pre_g": gain(D_MODEL),
        "w_in": w((L, D_MODEL, D_IN_2), D_MODEL),
        "na_rpb": 0.1 * jax.random.normal(next(ks), (L, NA_HEADS, 2 * NA_WIN_H - 1, 2 * NA_WIN_W - 1), jnp.float32),
        "mla_q_norm_g": gain(MLA_Q_LORA),
        "mla_w_uq": w((L, MLA_Q_LORA, MLA_HEADS * (MLA_QK_NOPE + MLA_QK_ROPE)), MLA_Q_LORA),
        "mla_kv_norm_g": gain(MLA_KV_LORA),
        "mla_w_ukv": w((L, MLA_KV_LORA, MLA_HEADS * (MLA_QK_NOPE + MLA_V_DIM)), MLA_KV_LORA),
        "na_out_norm_g": gain(NA_WIDTH),
        "mla_out_norm_g": gain(MLA_WIDTH),
        "w_out": w((L, MIX_WIDTH, D_MODEL), MIX_WIDTH),
        "mix_post_g": gain(D_MODEL),
        "ffn2_pre_g": gain(D_MODEL),
        "ffn2_w_gu": w((L, D_MODEL, 2 * D_FF), D_MODEL),
        "ffn2_w_down": w((L, D_FF, D_MODEL), D_FF),
        "ffn2_post_g": gain(D_MODEL),
    }

def second_block(x, ffn1_pre_g, ffn1_w_gu, ffn1_w_down, ffn1_post_g, mix_pre_g, w_in, na_rpb,
              mla_q_norm_g, mla_w_uq, mla_kv_norm_g, mla_w_ukv, na_out_norm_g, mla_out_norm_g,
              w_out, mix_post_g, ffn2_pre_g, ffn2_w_gu, ffn2_w_down, ffn2_post_g):
    B, S, _ = x.shape
    cos, sin = grid_rope_tables(S)
    split_at = [NA_WIDTH, 2 * NA_WIDTH, 3 * NA_WIDTH,
                3 * NA_WIDTH + MLA_Q_LORA, 3 * NA_WIDTH + MLA_Q_LORA + MLA_KV_LORA]
    h = x
    for l in range(DEPTH):
        f = swiglu(rms_norm_2(h, ffn1_pre_g[l]), ffn1_w_gu[l], ffn1_w_down[l])
        h = h + 0.5 * rms_norm_2(f, ffn1_post_g[l])
        z = rms_norm_2(h, mix_pre_g[l]) @ w_in[l]
        q_na, k_na, v_na, c_q, c_kv, k_rope = jnp.split(z, split_at, axis=-1)
        hs = (B, S, NA_HEADS, NA_HEAD_DIM)
        o_na = neighbourhood_attention(q_na.reshape(hs), k_na.reshape(hs), v_na.reshape(hs), na_rpb[l])
        o_mla = latent_attention(c_q, c_kv, k_rope, mla_q_norm_g[l], mla_w_uq[l],
                                 mla_kv_norm_g[l], mla_w_ukv[l], cos, sin)
        mixed = jnp.concatenate([rms_norm_2(o_na, na_out_norm_g[l]),
                                 rms_norm_2(o_mla, mla_out_norm_g[l])], axis=-1) @ w_out[l]
        h = h + rms_norm_2(mixed, mix_post_g[l])
        f = swiglu(rms_norm_2(h, ffn2_pre_g[l]), ffn2_w_gu[l], ffn2_w_down[l])
        h = h + 0.5 * rms_norm_2(f, ffn2_post_g[l])
    return h


def setup_inputs(seed=0):
    out = dict(first_inputs(seed))
    for name, value in second_inputs(seed + 1).items():
        if name != "x":
            out[name + "_2"] = value
    return out


def reference(
    x, norm_mix_g, w_in, b_forget, fox_q_g, fox_k_g, nsa_q_g, nsa_k_g, cmp_k_w1, cmp_k_w2,
    cmp_k_pos, cmp_v_w1, cmp_v_w2, cmp_v_pos, w_fox_up, w_nsa_up, w_out, norm_ffn_g, w_group,
    b_group, w_router, b_router, w_gate, w_up, w_down, ffn1_pre_g_2, ffn1_w_gu_2, ffn1_w_down_2,
    ffn1_post_g_2, mix_pre_g_2, w_in_2, na_rpb_2, mla_q_norm_g_2, mla_w_uq_2, mla_kv_norm_g_2,
    mla_w_ukv_2, na_out_norm_g_2, mla_out_norm_g_2, w_out_2, mix_post_g_2, ffn2_pre_g_2,
    ffn2_w_gu_2, ffn2_w_down_2, ffn2_post_g_2,
):
    x = first_block(
        x, norm_mix_g, w_in, b_forget, fox_q_g, fox_k_g, nsa_q_g, nsa_k_g, cmp_k_w1, cmp_k_w2,
        cmp_k_pos, cmp_v_w1, cmp_v_w2, cmp_v_pos, w_fox_up, w_nsa_up, w_out, norm_ffn_g,
        w_group, b_group, w_router, b_router, w_gate, w_up, w_down,
    )
    return second_block(
        x, ffn1_pre_g_2, ffn1_w_gu_2, ffn1_w_down_2, ffn1_post_g_2, mix_pre_g_2, w_in_2,
        na_rpb_2, mla_q_norm_g_2, mla_w_uq_2, mla_kv_norm_g_2, mla_w_ukv_2, na_out_norm_g_2,
        mla_out_norm_g_2, w_out_2, mix_post_g_2, ffn2_pre_g_2, ffn2_w_gu_2, ffn2_w_down_2,
        ffn2_post_g_2,
    )


_drawn_inputs = setup_inputs


def setup_inputs(seed=0):
    import zlib

    import numpy as np

    out = dict(_drawn_inputs(seed))
    spreads = {}
    factors = {'fox_q_g': 8.0,
     'fox_k_g': 4.316,
     'nsa_q_g': 8.0,
     'nsa_k_g': 7.517,
     'cmp_k_pos': 2.889,
     'b_group': 2.86,
     'b_router': 8.0,
     'mla_q_norm_g_2': 2.893,
     'ffn2_post_g_2': 3.368}
    for name, (base, spread) in spreads.items():
        noise = np.random.default_rng([zlib.crc32(name.encode()), seed]).standard_normal(out[name].shape)
        drawn = base * np.exp(spread * noise) if base else spread * noise
        out[name] = __import__('jax').numpy.asarray(drawn.astype(out[name].dtype))
    for name, factor in factors.items():
        out[name] = (out[name] * factor).astype(out[name].dtype)
    return out
```

```python
import numpy as np

P = 128
T, D = 512, 1024
NT = T // P
KD = D // P
H, DH = 8, 64
NE, NG, EPG, FE = 16, 4, 4, 512
NSLOT_BLOCKS = (2 * T + NE * (P - 1)) // P
F = 2816
NF = F // P
NCMP = 31
NEG = -1e30
RING = 3
SLOT = 4096
LAG = 3

CONSTS = {}


def _place(name, width):
    CONSTS[name] = (sum(w for _, w in CONSTS.values()), width)


for _name, _width in (("ident", P), ("flip", P), ("ones_upper", 896), ("dist", T), ("diag_mask", P),
                      ("cmp_dist", NT * NCMP), ("cmp_valid", 1), ("tri16", 256), ("iota_block", 24),
                      ("iota4", 4), ("cos", NT * 16), ("sin", NT * 16), ("na_mask", 3 * 256)):
    _place(_name, _width)
NCONST = sum(w for _, w in CONSTS.values())


def shape_constants():
    f = np.float32
    p = np.arange(P)[:, None]
    tab = {}
    tab["ident"] = np.eye(P)
    tab["flip"] = np.eye(P)[::-1]
    tab["ones_upper"] = (p <= np.arange(896)[None] - 384)
    off = np.arange(T)[None] - 384 - p
    tab["dist"] = np.where(off <= 0, off, NEG)
    tab["diag_mask"] = np.where(np.arange(P)[None] <= p, 0.0, NEG)
    tok = np.arange(NT)[None, :, None] * P + np.arange(P)[:, None, None]
    cd = tok - (np.arange(NCMP) * 16 + 31)[None, None, :]
    tab["cmp_dist"] = np.where(cd >= 0, -cd, NEG).reshape(P, -1)
    tab["cmp_valid"] = (p >= 31)
    e = np.arange(16)
    tab["tri16"] = np.broadcast_to((e[None, :] <= e[:, None]).reshape(1, 256), (P, 256))
    tab["iota_block"] = np.broadcast_to(np.arange(24)[None], (P, 24))
    tab["iota4"] = np.broadcast_to(np.arange(4)[None] - 99.0, (P, 4))
    t = np.arange(T)
    inv = (f(1.0) / (f(10000.0) ** (np.arange(8, dtype=f) / f(8)))).astype(f)
    ang = np.concatenate([(t // 64).astype(f)[:, None] * inv, (t % 64).astype(f)[:, None] * inv], axis=-1)
    for name, fn in (("cos", np.cos), ("sin", np.sin)):
        tab[name] = fn(ang).astype(f).reshape(NT, P, 16).transpose(1, 0, 2).reshape(P, -1)
    masks = []
    for c0, band in ((0, 0), (16, 8), (48, 32)):
        col = c0 + np.arange(16)
        start = np.clip(col - 8, 0, 48)
        key = band + np.arange(32)
        ok = (key[None] >= start[:, None]) & (key[None] < start[:, None] + 16)
        m = np.where(ok, 0.0, NEG)
        masks.append(np.broadcast_to(m[None, :, None, :], (8, 16, 8, 32)).reshape(P, 256))
    tab["na_mask"] = np.concatenate(masks, axis=1)
    return np.concatenate([np.asarray(tab[n], f).reshape(P, w) for n, (_, w) in CONSTS.items()], axis=1)


def weight_blocks(w):
    def chunks(m, c0, c1, cols):
        return m[c0 * P:c1 * P, cols].rearrange("(c p) n -> p c n", p=P)

    blocks = {}
    w_in, w_in2 = w["w_in"][0], w["w_in_2"][0]
    first = []
    for lo in (0, 512, 1024, 1544, 2056):
        first.append([(0, 512, chunks(w_in, 0, 8, slice(lo, lo + 512)))])
    first.append([(0, 288, chunks(w_in, 0, 8, slice(2568, 2848))), (280, 288, chunks(w_in, 0, 8, slice(1536, 1544)))])
    for n in ("cmp_k_w1", "cmp_v_w1"):
        first.append([(0, 256, chunks(w[n][0], 0, 16, slice(0, 256)))])
    for lo in (2848, 3360):
        first.append([(0, 512, chunks(w_in, 0, 8, slice(lo, lo + 512)))])
    first.append([(0, 1024, chunks(w["w_fox_up"][0], 0, 4, slice(0, 1024)))])
    for lo in (3872, 4384):
        first.append([(0, 512, chunks(w_in, 0, 8, slice(lo, lo + 512)))])
    first.append([(0, 1024, chunks(w["w_nsa_up"][0], 0, 4, slice(0, 1024)))])
    for lo in (0, 512):
        first.append([(0, 512, chunks(w["w_out"][0], 0, 8, slice(lo, lo + 512)))])
    blocks["first"] = first
    mid = []
    for lo, hi in ((0, 512), (512, 1024), (1024, 1536), (1536, 1952)):
        mid.append([(0, hi - lo, chunks(w_in2, 0, 8, slice(lo, hi)))])
    mid.append([(0, 768, chunks(w["mla_w_uq_2"][0], 0, 2, slice(0, 768))),
                (1536, 1024, chunks(w["mla_w_ukv_2"][0], 0, 1, slice(0, 1024)))])
    for lo in (0, 512):
        mid.append([(0, 512, chunks(w["w_out_2"][0], 0, 8, slice(lo, lo + 512)))])
    blocks["mid"] = mid
    for n in ("1", "2"):
        blocks["down" + n] = [[(0, 512, chunks(w[f"ffn{n}_w_down_2"][0], c0, c1, slice(half, half + 512)))]
                              for half in (0, 512) for c0, c1 in DOWN_SPLIT]
    return blocks


DOWN_SPLIT = ((0, 8), (8, 16), (16, NF))
N_FIRST, N_MID, N_GU, N_DOWN = 16, 7, NF // 2, 6
AT_MOE = N_FIRST
AT_FFN1 = AT_MOE
AT_MID = AT_FFN1 + N_GU + N_DOWN
AT_FFN2 = AT_MID + N_MID


def build_blocks(nc, w, out):
    import concourse.bass as bass
    from concourse import mybir

    f32, i32 = mybir.dt.float32, mybir.dt.int32
    ALU, ACT, AX = mybir.AluOpType, mybir.ActivationFunctionType, mybir.AxisListType
    ds = bass.ds

    def sb(name, shape, dt=f32):
        return nc.alloc_sbuf_tensor(name, shape, dt)

    def view(ap, dims, off=0):
        return bass.AP(tensor=ap.tensor, offset=ap.offset + off, ap=[ap.ap[0]] + dims)

    const = sb("const", [P, NCONST])
    ring = sb("ring", [P, RING, SLOT])
    xres = sb("xres", [P, NT, D])
    hT = sb("hT", [P, KD, T])
    hn = sb("hn", [P, NT, D])
    gain = sb("gain", [P, 2, D])
    ss = sb("ss", [P, 32])
    rstd = sb("rstd", [P, 32])
    small = sb("small", [P, 1000])
    isml = sb("isml", [P, 64], i32)
    sums = sb("sums", [P, 8])
    nmax = sb("nmax", [P, 8])
    rr = sb("rr", [P, 8])
    cmp_w2 = sb("cmp_w2", [P, 2, 2, DH])
    w_route = sb("w_route", [P, KD, 20])
    AR = 21880
    arena = sb("arena", [P, AR])

    def carve(at, *shape):
        n = int(np.prod(shape))
        assert at + n <= AR, (at, shape)
        ap = arena[:, at:at + n]
        if len(shape) == 2:
            ap = ap.rearrange("p (a b) -> p a b", a=shape[0])
        if len(shape) == 3:
            ap = ap.rearrange("p (a b c) -> p a b c", a=shape[0], b=shape[1])
        return ap

    def c_(name):
        at, width = CONSTS[name]
        return const[:, at:at + width]

    ident, flip, upper, dist, diag_mask = (c_(n) for n in ("ident", "flip", "ones_upper", "dist", "diag_mask"))
    one_col = upper[:, 895:896]

    qT, kT = carve(0, 4, T), carve(2048, 4, T)
    nqT, kkT = carve(4096, 4, T), carve(6144, 4, T)
    vf = carve(8192, NT, 512)
    zc = carve(10240, NT, 512)
    zd = carve(12288, NT, 288)
    OaT, ObT = carve(13440, 4, T), carve(15488, 4, T)
    zs = [OaT, ObT, carve(17536, 4, T)]
    K2 = carve(19584, 4, T)
    PB = carve(17536, 4, T)
    tab = carve(19584, 2, 768)
    zk, sq = hn[:, 0:2, :].rearrange("p a b -> p (a b)").rearrange("p (t n) -> p t n", t=NT), \
        hn[:, 2:4, :].rearrange("p a b -> p (a b)").rearrange("p (t n) -> p t n", t=NT)
    PT = hn[:, :, :].rearrange("p (u a) b -> p u (a b)", u=2).rearrange("p u (j q) -> p u j q", j=4)
    lf, forget = small[:, 0:32], small[:, 32:40]
    tmp32 = small[:, 40:72]
    gates = small[:, 72:168]
    gcol = small[:, 168:172]
    posT = small[:, 172:204]
    pos_bias = small[:, 204:208]
    kcT = small[:, 208:270].rearrange("p (g n) -> p g n", g=2)
    vcmp = small[0:NCMP, 270:398]
    kcn = carve(17792, 2 * P)[0:NCMP]
    kcs, kcs_sq = carve(17536, P)[0:NCMP], carve(17664, P)[0:NCMP]
    hidc = carve(21632, 2, 2, 62)
    cumT = carve(21120, T)
    pos_raw = hn[0:32, 0, 0:P]
    gate_sig = carve(0, NT, D)
    mixtmp = carve(4096, 2, 512)
    Xb, XT = carve(0, D), carve(1024, KD, P)
    sg, hb, HTs, Yb = carve(2048, 512), carve(2560, 512), carve(3072, 4, P), carve(3584, D)
    Yg = carve(4608, 4, D)
    rt = carve(8704, 2048)
    zeros = cmp_w2[:, :, :, :].rearrange("p a b c -> p (a b c)")
    hid = carve(0, NF, T)
    sgb = carve(NF * T, 2, T)
    qT2, kT2, Vband = carve(0, 4, T), carve(2048, 4, T), carve(4096, 4, 1024)
    v2 = carve(8192, NT, 512)
    xrev = carve(10240, H, 384)
    z3 = carve(13312, NT, 416)
    PB2 = carve(14976, 4, T)
    tab2 = carve(17024, 2, 768)
    sq_na = carve(18560, 4, T)
    rpbs = carve(20608, 64)
    qTm, kTm, vm = carve(0, H, T), carve(4096, H, T), carve(8192, NT, 512)
    cT, PBm, zero_tab = carve(10240, 3, T), carve(10240, 4, T), carve(12288, T)
    ropes = hn[:, 0, :].rearrange("p (a b) -> p a b", a=2)
    qz, kf = carve(14976, NT, 768), carve(18048, NT, 768)
    sq_mla = carve(14976, 4, T)

    psum = nc.alloc_psum_tensor("psum", [P, 8, 512], f32)
    ps = [psum[:, i, :] for i in range(8)]
    Xs = nc.dram_tensor("x_slots", (24 * P, D), f32, kind="Internal").ap()
    Ys = nc.dram_tensor("y_slots", (NSLOT_BLOCKS * P, D), f32, kind="Internal").ap()
    Rp = nc.dram_tensor("rpb_padded", (H * 15, 64), f32, kind="Internal").ap()

    names = """x_in const_in moe_load0 moe_load1 moe_load2 y_stored load0 load1 load2 load3 gain_in0 gain_in1 gain_used head_gain_in pos_in misc_in cn_gain_in
        route_in hn_ready ht_psum ht_ready var_ready root_ready dve_step act_step pool_step
        sumsq z_psum z_evac sq_done sq_used head_ready tr_psum tr_evac k2_ready pos_psum pos_evac cmp_psum
        pos_bias_ready gelu_done cmp2_psum kcn_ready kcn_psum kct_ready
        fox_u fox_l lf_ready gate_raw gates_ready cum_psum cum_ready
        tab_psum fox_tab nsa_tab na_tab mla_tab score_psum scored expd recd scaled pt_psum pt_ready pv_psum o_evac o_sq
        mix_psum mix_sig mixed res_ready route_psum chosen exp_in exp_out routed zero_ready zero_out scattered x_slot xtr_psum xt_ready
        gu_psum silu_done hb_ready htr_psum hts_ready y_psum yb_ready y_out y_back0 y_back1 y_back2 y_back3 y_used
        ff_psum ff_silu ff_hid fd_block fd_psum f_evac
        z2_psum z2_evac rpb_in rpb_pad rpb_out rpb_zero xrev_in band_in cn_ready cn_psum ct_ready
        mla_psum mla_evac roped mt_psum mt_act mt_dve nrm_psum o2_psum out_dma vm_free""".split()
    s = {n: nc.alloc_semaphore(n) for n in names}
    loaded = [s[f"load{i}"] for i in range(RING)]
    blocks = weight_blocks(w)

    def place(n):
        return n % RING, n // RING

    def released(n, i=0):
        if n < 6:
            return s["z_psum"], 4 * n + 4
        if n < 8:
            return s["cmp_psum"], 2 * (n - 5)
        if n < N_FIRST:
            return s["mix_psum"], (4, 8, 16, 20, 24, 32, 36, 40)[n - 8]
        for f, at in ((0, AT_FFN1), (1, AT_FFN2)):
            k = n - at
            if 0 <= k < N_GU:
                return s["ff_psum"], NF * f + 2 * k + 2
            if N_GU <= k < N_GU + N_DOWN:
                half, part = divmod(k - N_GU, 3)
                return (s["fd_block"], 4 * f + 2 * half + part + 1) if part < 2 else (s["fd_psum"], 8 * f + 4 * half + 4)
        k = n - AT_MID
        if k < 4:
            return s["z2_psum"], 4 * k + 4
        return (s["mla_psum"], 16) if k == 4 else (s["o2_psum"], 8 * (k - 4))

    def arrived(pe, n, i=0):
        slot, use = place(n)
        pe.wait_ge(loaded[slot], 32 * (use + 1) + 32 * i)

    moe_loaded = [s[f"moe_load{i}"] for i in range(RING)]

    def moe_arrived(pe, k, i=0):
        pe.wait_ge(moe_loaded[k % RING], 32 * (k // RING + 1) + 32 * i)

    def slot_view(n, chunks, width, at=0):
        slot = place(n)[0]
        return ring[:, slot, at:at + chunks * width].rearrange("p (c n) -> p c n", c=chunks)

    def half(ap, h):
        return ap[64 * (h % 2):64 * (h % 2) + 64]

    def make_phase(name):
        units, steps, groups, pairs = [], [], [], []
        if name == "first":
            heads = [("fox", h) for h in range(H)] + [("nsa", h) for h in range(H)]
        else:
            heads = [(name, h) for h in range(H)]
        for g, (kind, h) in enumerate(heads):
            groups.append(dict(kind=kind, h=h, first=len(steps)))
            branches = {"fox": ("fox",), "nsa": ("slc", "win", "cmp"), "na": ("na",), "mla": ("mla",)}[kind]
            for br in branches:
                u = len(units)
                unit = dict(pair=g // 2, pv=[], last_of_pair=(br == branches[-1] and h % 2 == 1))
                units.append(unit)
                kv = h // 4
                first_br, last_br = br == branches[0], br == branches[-1]
                if kind in ("fox", "nsa") and br != "cmp":
                    v_of = {"fox": lambda j: vf[:, j, 64 * h:64 * h + 64],
                            "slc": lambda j: zc[:, j, 384 + 64 * kv:448 + 64 * kv],
                            "win": lambda j: zd[:, j, 128 + 64 * kv:192 + 64 * kv]}[br]
                    k_of = {"fox": lambda: half(kT, h)[:, h // 2, :], "slc": lambda: half(kkT, h)[:, kv, :],
                            "win": lambda: half(kkT, h)[:, 2 + kv, :]}[br]()
                    q_of = half(qT if kind == "fox" else nqT, h)[:, h // 2, :]
                    for i in range(NT):
                        n = P * (i + 1)
                        steps.append(dict(
                            u=u, g=g, lhsT=q_of[:, P * i:P * i + P], rhs=k_of[:, 0:n], keys=n, out=(n,),
                            mask=kind == "fox", tab=(0, n) if kind == "fox" else None,
                            const_tab=None, shift=384 - P * i if kind == "nsa" else 0, first=i == 0, last=i == NT - 1,
                            gate=None if kind == "fox" else gates[:, 24 * i + 3 * h + (1 if br == "slc" else 2):][:, 0:1],
                            blocks=[(P * j, P) for j in range(i + 1)], rows=P, dst=P * i))
                    for j in range(NT):
                        unit["pv"].append((v_of(j), (j, P * j, T), (P * j, T), first_br and j == 0, last_br and j == NT - 1))
                elif br == "cmp":
                    for i in range(NT):
                        steps.append(dict(
                            u=u, g=g, lhsT=half(nqT, h)[:, h // 2, P * i:P * i + P], rhs=half(kcT, h)[:, kv, :],
                            keys=NCMP, mask=False, tab=None, const_tab=None, shift=512 + NCMP * i, first=i == 0,
                            last=i == NT - 1, gate=gates[:, 24 * i + 3 * h:24 * i + 3 * h + 1],
                            blocks=[(0, NCMP)], rows=NCMP, dst=P * i))
                    unit["pv"].append((vcmp[:, 64 * kv:64 * kv + 64], (0, 0, T), (0, T), False, True))
                elif kind == "na":
                    q_of = half(qT2, h)[:, h // 2, :]
                    k_of = half(kT2, h)[:, h // 2, :].rearrange("p (r c) -> p r c", r=8)
                    for b in range(4):
                        band = (0, 8, 24, 32)[b]
                        steps.append(dict(
                            u=u, g=g, lhsT=q_of[:, P * b:P * b + P], rhs=k_of[:, :, band:band + 32], keys=256,
                            mask=False, tab=None, const_tab=None, shift=256 * (0, 1, 1, 2)[b], first=b == 0,
                            last=b == 3, gate=None, blocks=[(0, P), (P, P)], rows=P, dst=P * b))
                        for j in range(2):
                            unit["pv"].append((Vband[:, b, 512 * j + 64 * h:512 * j + 64 * h + 64],
                                               (j, P * b, P * b + P), (P * b, P * b + P), j == 0, j == 1))
                else:
                    for i in range(NT):
                        steps.append(dict(
                            u=u, g=g, lhsT=qTm[0:96, h, P * i:P * i + P], rhs=kTm[0:96, h, :], keys=T, mask=False,
                            tab=None, const_tab=zero_tab, shift=0, first=i == 0, last=i == NT - 1, gate=None,
                            blocks=[(P * j, P) for j in range(NT)], rows=P, dst=P * i))
                    for j in range(NT):
                        unit["pv"].append((vm[:, j, 64 * h:64 * h + 64], (j, 0, T), (0, T), j == 0, j == NT - 1))
        for unit in units:
            unit["h"] = 0
        at = 0
        for g, (kind, h) in enumerate(heads):
            for _ in range(3 if kind == "nsa" else 1):
                units[at]["h"] = h
                at += 1
        return dict(name=name, units=units, steps=steps, groups=groups, pb={"first": PB, "na": PB2, "mla": PBm}[name],
                    tab={"first": tab, "na": tab2, "mla": None}[name], n_pairs=len(heads) // 2)

    phases = [make_phase("first"), make_phase("na"), make_phase("mla")]
    n_steps = n_units = n_pairs = 0
    for ph in phases:
        ph.update(n0=n_steps, u0=n_units, p0=n_pairs)
        n_steps += len(ph["steps"])
        n_units += len(ph["units"])
        n_pairs += ph["n_pairs"]

    def bias_of(ph, st):
        if st["const_tab"] is not None:
            return st["const_tab"][:, 0:st["keys"]]
        t = ph["tab"][:, st["g"] % 2, st["shift"]:st["shift"] + st["keys"]]
        return t

    def attend_pe(pe, ph, tables=None):
        steps, units, n0, u0 = ph["steps"], ph["units"], ph["n0"], ph["u0"]
        if tables:
            tables(0)
        for m in range(len(steps) + LAG + 1):
            if m < len(steps):
                st = steps[m]
                if tables and ph["groups"][st["g"]]["first"] == m:
                    tables(st["g"] + 1)
                if n0 + m >= 3:
                    pe.wait_ge(s["scored"], n0 + m - 2)
                bank = ps[(n0 + m) % 3]
                out = bank[:, 0:st["keys"]]
                mm = nc.tensor.matmul(out, st["lhsT"], st["rhs"], start=True, stop=not st["mask"])
                if st["mask"]:
                    mm = nc.tensor.matmul(bank[:, st["keys"] - P:st["keys"]], ident, diag_mask, start=False, stop=True)
                mm.then_inc(s["score_psum"], 1)
            if 0 <= m - LAG < len(steps):
                n = m - LAG
                st = steps[n]
                if n0 + n >= 2:
                    pe.wait_ge(s["pt_ready"], n0 + n - 1)
                pe.wait_ge(s["scaled"], n0 + n + 1)
                bank, pbuf = ps[3 + (n0 + n) % 2], ph["pb"][:, (n0 + n) % 4, :]
                for j, (c0, rows) in enumerate(st["blocks"]):
                    mm = nc.tensor.transpose(bank[0:rows, P * j:P * j + P], pbuf[:, c0:c0 + rows], ident)
                mm.then_inc(s["pt_psum"], 1)
            n = m - LAG - 1
            if n >= 0 and steps[n]["last"]:
                u = steps[n]["u"]
                unit = units[u]
                pair = ph["p0"] + unit["pair"]
                pe.wait_ge(s["pt_ready"], n0 + n + 1)
                if unit["h"] % 2 == 0 and pair >= 2:
                    pe.wait_ge(s["o_evac"], pair - 1)
                bank = ps[5 + pair % 2]
                last = None
                for lhsT, (j, a, b), (c, d), start, stop in unit["pv"]:
                    rows = lhsT.shape[0]
                    last = nc.tensor.matmul(half(bank, unit["h"])[:, c:d], lhsT, PT[0:rows, (u0 + u) % 2, j, a:b],
                                            start=start, stop=stop)
                last.then_inc(s["pv_psum"], 1)

    def attend_dve(dve, ph, evac, tables=None):
        steps, n0 = ph["steps"], ph["n0"]

        def recip(n):
            dve.wait_ge(s["expd"], n0 + n + 1)
            if n0 + n >= 8:
                dve.wait_ge(s["scaled"], n0 + n - 7)
            k = (n0 + n) % 8
            nc.vector.reciprocal(rr[:, k:k + 1], sums[:, k:k + 1]).then_inc(s["recd"], 1)

        if tables:
            tables(0)
        for m in range(len(steps) + LAG + 1):
            if m < len(steps):
                st = steps[m]
                if tables and ph["groups"][st["g"]]["first"] == m:
                    tables(st["g"] + 1)
                if st["first"] and st["const_tab"] is None:
                    kind, h = ph["groups"][st["g"]]["kind"], ph["groups"][st["g"]]["h"]
                    dve.wait_ge(s[f"{kind}_tab"], h + 1)
                dve.wait_ge(s["score_psum"], n0 + m + 1)
                if n0 + m >= 4:
                    dve.wait_ge(s["pt_psum"], n0 + m - 3)
                k = (n0 + m) % 8
                n = st["keys"]
                nc.vector.tensor_tensor_reduce(
                    out=ph["pb"][:, (n0 + m) % 4, 0:n], in0=ps[(n0 + m) % 3][:, 0:n], in1=bias_of(ph, st), scale=-1.0,
                    scalar=3e38, op0=ALU.add, op1=ALU.min, accum_out=nmax[:, k:k + 1]).then_inc(s["scored"], 1)
            if 0 <= m - 1 < len(steps):
                recip(m - 1)
            n = m - LAG - 1
            if n >= 0 and steps[n]["last"] and ph["units"][steps[n]["u"]]["last_of_pair"]:
                evac(steps[n]["u"])

    def attend_act(act, ph, evac=None, tables=None):
        steps, n0, u0 = ph["steps"], ph["n0"], ph["u0"]
        if tables:
            tables(0)
        for m in range(len(steps) + LAG + 1):
            if m < len(steps):
                st = steps[m]
                if tables and ph["groups"][st["g"]]["first"] == m:
                    tables(st["g"] + 1)
                act.wait_ge(s["scored"], n0 + m + 1)
                if n0 + m >= 8:
                    act.wait_ge(s["recd"], n0 + m - 7)
                k = (n0 + m) % 8
                p = ph["pb"][:, (n0 + m) % 4, 0:st["keys"]]
                nc.scalar.activation(p, p, ACT.Exp, bias=nmax[:, k:k + 1], scale=-1.0,
                                     accum_out=sums[:, k:k + 1]).then_inc(s["expd"], 1)
            if 0 <= m - LAG < len(steps):
                n = m - LAG
                st = steps[n]
                u = u0 + st["u"]
                act.wait_ge(s["pt_psum"], n0 + n + 1)
                if st["first"] and u >= 2:
                    act.wait_ge(s["pv_psum"], u - 1)
                nj, rows = len(st["blocks"]), st["rows"]
                src = ps[3 + (n0 + n) % 2][0:rows, 0:P * nj].rearrange("p (j q) -> p j q", j=nj)
                nc.scalar.activation(PT[0:rows, u % 2, 0:nj, st["dst"]:st["dst"] + P], src, ACT.Copy)\
                    .then_inc(s["pt_ready"], 1)
            n = m - LAG - 1
            if evac and n >= 0 and steps[n]["last"] and ph["units"][steps[n]["u"]]["last_of_pair"]:
                evac(steps[n]["u"])

    def attend_pool(pool, ph, tables=None):
        steps, n0 = ph["steps"], ph["n0"]
        if tables:
            tables(0)
        for m, st in enumerate(steps):
            if tables and ph["groups"][st["g"]]["first"] == m:
                tables(st["g"] + 1)
            pool.wait_ge(s["recd"], n0 + m + 1)
            k = (n0 + m) % 8
            p = ph["pb"][:, (n0 + m) % 4, 0:st["keys"]]
            if st["gate"] is None:
                ins = nc.gpsimd.tensor_scalar(p, p, rr[:, k:k + 1], None, ALU.mult)
            else:
                ins = nc.gpsimd.tensor_scalar(p, p, rr[:, k:k + 1], st["gate"], ALU.mult, ALU.mult)
            ins.then_inc(s["scaled"], 1)

    first, na, mla = phases

    def free_tab(eng, ph, g):
        if g >= 2:
            eng.wait_ge(s["scored"], ph["n0"] + ph["groups"][g - 1]["first"])

    def counter():
        return [0]

    def last_block(eng):
        return eng.value_load(isml[0:1, 32:33], min_val=2 * T // P - 1, max_val=NSLOT_BLOCKS - 1)

    block = nc.Block()
    with block, nc.allow_non_contiguous_dma(reason="gains of heads and outputs, a column each"):

        @block.sync
        def _(sp):
            def load(n, pieces, wait=None, sem_of=loaded):
                slot = place(n)[0]
                landed = sem_of[slot] if sem_of is loaded else moe_loaded[(n - AT_MOE) % RING]
                if n >= RING:
                    sem, value = wait or released(n - RING)
                    sp.wait_ge(sem, value)
                if len(pieces) == 1:
                    at, width, src = pieces[0]
                    k = src.shape[1] // 2
                    pieces = [(at, width, src[:, 0:k, :]), (at + k * width, width, src[:, k:, :])]
                for at, width, src in pieces:
                    k, cols = src.shape[1], src.shape[2]
                    if width == 288 and cols == 8:
                        dst = ring[:, slot, 0:k * width].rearrange("p (c n) -> p c n", c=k)[:, :, at:at + cols]
                    else:
                        dst = ring[:, slot, at:at + k * width].rearrange("p (c n) -> p c n", c=k)[:, :, 0:cols]
                    sp.dma_start(dst, src).then_inc(landed, 16)

            def load_gu(n, name, b, wait=None):
                gu = w[name][0]
                load(n, [(2048 * g, 256, gu[:, ds(b * 256 + g * F, 256)].rearrange("(c p) n -> p c n", p=P))
                         for g in range(2)], wait=wait)

            for t in range(NT):
                sp.dma_start(xres[:, t, :], w["x"][0, t * P:(t + 1) * P, :]).then_inc(s["x_in"], 16)
            sp.dma_start(const[:, :], w["consts"]).then_inc(s["const_in"], 16)
            for n, pieces in enumerate(blocks["first"]):
                load(n, pieces)

            def expert(b):
                return sp.value_load(isml[0:1, ds(8 + b, 1)] if not isinstance(b, int) else isml[0:1, 8 + b:9 + b],
                                     min_val=0, max_val=NE - 1)

            def expert_weights(k, name, e, wait):
                load(AT_MOE + k, [(0, 512 if name != "w_down" else 1024,
                                   w[name][0][ds(e, 1), :, :].rearrange("o (c p) f -> p (o c) f", p=P))],
                     wait=wait, sem_of=moe_loaded)

            sp.wait_ge(s["routed"], 1)
            last = last_block(sp)
            e0 = expert(0)
            expert_weights(0, "w_gate", e0, released(AT_MOE - 3))
            expert_weights(1, "w_up", e0, released(AT_MOE - 2))
            e1 = expert(1)
            expert_weights(2, "w_gate", e1, released(AT_MOE - 1))
            expert_weights(3, "w_up", e1, (s["gu_psum"], 1))
            expert_weights(4, "w_down", e0, (s["gu_psum"], 2))
            with sp.Fori(2, last + 1) as b:
                e = expert(b)
                expert_weights(5, "w_gate", e, (s["gu_psum"], 2 * b - 1))
                expert_weights(6, "w_up", e, (s["gu_psum"], 2 * b))
                before = expert(b - 1)
                expert_weights(7, "w_down", before, (s["y_psum"], 2 * b - 2))
            expert_weights(5, "w_down", expert(last), (s["gu_psum"], 2 * last + 1))

            def ffn(f, at, name):
                for b in range(3):
                    load_gu(at + b, name + "_w_gu_2", b,
                            ((s["gu_psum"], 2 * last + 2), (s["y_psum"], 2 * last), (s["y_psum"], 2 * last + 2))[b] if f == 0 else None)
                with sp.Fori(0, 2) as i:
                    for q in range(3):
                        load_gu(at + 3 + q, name + "_w_gu_2", 3 * i + (3 + q), (s["ff_psum"], 6 * i + (NF * f + 2 * q + 2)))
                for b in (9, 10):
                    load_gu(at + b, name + "_w_gu_2", b)
                for k, pieces in enumerate(blocks["down" + name[-1]]):
                    load(at + N_GU + k, pieces)

            ffn(0, AT_FFN1, "ffn1")
            for k, pieces in enumerate(blocks["mid"]):
                load(AT_MID + k, pieces)
            ffn(1, AT_FFN2, "ffn2")
            for t in range(NT):
                sp.wait_ge(s["res_ready"], 4 * 4 + t + 1)
                sp.dma_start(out[0, t * P:(t + 1) * P, :], xres[:, t, :]).then_inc(s["out_dma"], 16)
            sp.wait_ge(s["out_dma"], 16 * NT)

        @block.gpsimd
        def _(pool):
            steps_done = counter()

            def chained(ins):
                steps_done[0] += 1
                ins.then_inc(s["pool_step"], 1)
                pool.wait_ge(s["pool_step"], steps_done[0])

            gains = ["norm_mix_g", "norm_ffn_g", "ffn1_pre_g_2", "ffn1_post_g_2", "mix_pre_g_2", "mix_post_g_2",
                     "ffn2_pre_g_2", "ffn2_post_g_2"]

            def load_gain(k):
                if k >= 2:
                    pool.wait_ge(s["gain_used"], k - 1)
                pool.dma_start(gain[:, k % 2, :], w[gains[k]].partition_broadcast(P)[:, 0, :])\
                    .then_inc(s[f"gain_in{k % 2}"], 16)

            load_gain(0)
            load_gain(1)
            for k, name in enumerate(("fox_q_g", "fox_k_g", "nsa_q_g", "nsa_k_g")):
                for a in (0, 64):
                    pool.dma_start(gcol[a:a + 64, k:k + 1], w[name].rearrange("a d -> d a")).then_inc(s["head_gain_in"], 16)
            for k, name in enumerate(("cmp_k_pos", "cmp_v_pos")):
                pool.dma_start(sq[16 * k:16 * k + 16, 0, 0:P], w[name][0].rearrange("(c two) d -> c (two d)", two=2))\
                    .then_inc(s["pos_in"], 16)
            pool.dma_start(forget, w["b_forget"].partition_broadcast(P)[:, 0, :]).then_inc(s["misc_in"], 16)
            pool.dma_start(small[:, 526:526 + 4], w["b_group"].partition_broadcast(P)[:, 0, :]).then_inc(s["misc_in"], 16)
            pool.dma_start(small[:, 530:530 + 16], w["b_router"].partition_broadcast(P)[:, 0, :]).then_inc(s["misc_in"], 16)
            for k, name in enumerate(("cmp_k_w2", "cmp_v_w2")):
                pool.dma_start(cmp_w2[:, k, :, :], w[name][0].rearrange("(c p) d -> p c d", p=P)).then_inc(s["misc_in"], 16)
            pool.dma_start(small[:, 600:856], w["mla_q_norm_g_2"].partition_broadcast(P)[:, 0, :]).then_inc(s["misc_in"], 16)
            pool.dma_start(small[:, 856:984], w["mla_kv_norm_g_2"].partition_broadcast(P)[:, 0, :]).then_inc(s["misc_in"], 16)
            for k, name in enumerate(("na_out_norm_g_2", "mla_out_norm_g_2")):
                pool.dma_start(small[:, 984 + 4 * k:988 + 4 * k], w[name].rearrange("a (c p) -> p (a c)", p=P))\
                    .then_inc(s["misc_in"], 16)
            pool.dma_start(w_route[:, :, 0:4], w["w_group"][0].rearrange("(c p) n -> p c n", p=P)).then_inc(s["route_in"], 16)
            pool.dma_start(w_route[:, :, 4:20], w["w_router"][0].rearrange("(c p) n -> p c n", p=P))\
                .then_inc(s["route_in"], 16)

            pool.wait_ge(s["pos_evac"], 1)
            for g, last in enumerate((4, 8, 16, 24)):
                pool.wait_ge(s["z_evac"], last)
                if g:
                    pool.wait_ge(s["sq_used"], g)
                if g < 3:
                    nc.gpsimd.tensor_tensor(sq, zs[g], zs[g], ALU.mult).then_inc(s["sq_done"], 1)
                else:
                    chained(nc.gpsimd.tensor_tensor(sq[:, :, 0:P], zc[:, :, 256:384], zc[:, :, 256:384], ALU.mult))
                    nc.gpsimd.tensor_tensor(sq[:, :, P:2 * P], zd[:, :, 0:P], zd[:, :, 0:P], ALU.mult)\
                        .then_inc(s["sq_done"], 1)

            pool.wait_ge(s["cmp2_psum"], 1)
            nc.gpsimd.memset(zeros, 0.0).then_inc(s["zero_ready"], 1)
            pool.wait_ge(s["zero_ready"], 1)
            for k in range(4):
                pool.dma_start(Xs.rearrange("(a p) (k n) -> k p a n", p=P, k=4)[k],
                               view(zeros, [[0, 24], [1, 256]])).then_inc(s["zero_out"], 16)
                pool.dma_start(Ys.rearrange("(a p) (k n) -> k p a n", p=P, k=4)[k],
                               view(zeros, [[0, NSLOT_BLOCKS], [1, 256]])).then_inc(s["zero_out"], 16)

            def alibi(g):
                if g < H or g >= 2 * H:
                    return
                h = g - H
                free_tab(pool, first, g)
                slope = 2.0 ** (-(h + 1))
                chained(nc.gpsimd.tensor_scalar(tab[:, g % 2, 0:T], dist, slope, None, ALU.mult))
                nc.gpsimd.tensor_scalar(tab[:, g % 2, T:T + NT * NCMP], c_("cmp_dist"), slope, None, ALU.mult)\
                    .then_inc(s["nsa_tab"], 1)

            attend_pool(pool, first, alibi)

            pool.wait_ge(s["routed"], 1)
            pool.wait_ge(s["zero_out"], 128)
            for k in range(2):
                for t in range(NT):
                    pool.indirect_dma_start(Xs[:, :], bass.IndirectOffsetOnAxis(ap=isml[:, 4 * k + t:4 * k + t + 1], axis=0),
                                            hn[:, t, :], None).then_inc(s["scattered"], 16)
            pool.wait_ge(s["scattered"], 16 * 8)
            pool.dma_start(Xb, Xs[0:P, :]).then_inc(s["x_slot"], 16)
            pool.wait_ge(s["xtr_psum"], 2)
            pool.dma_start(Xb, Xs[P:2 * P, :]).then_inc(s["x_slot"], 16)
            last = last_block(pool)
            with pool.Fori(1, last + 1) as b:
                pool.wait_ge(s["xtr_psum"], 2 * b + 2)
                pool.dma_start(Xb, Xs[ds(P * b + P, P), :]).then_inc(s["x_slot"], 16)
                pool.wait_ge(s["yb_ready"], b)
                pool.dma_start(Ys[ds(P * b - P, P), :], Yb).then_inc(s["y_out"], 16)
            pool.wait_ge(s["yb_ready"], last + 1)
            pool.dma_start(Ys[ds(P * last, P), :], Yb).then_inc(s["y_out"], 16)
            pool.wait_ge(s["y_stored"], 1)
            for t in range(NT):
                for k in range(2):
                    n = 2 * t + k
                    if n >= 4:
                        pool.wait_ge(s["res_ready" if k else "y_used"], (4 if k else 0) + t - 1)
                    pool.indirect_dma_start(Yg[:, n % 4, :], None, Ys[:, :], bass.IndirectOffsetOnAxis(
                        ap=isml[:, 4 * k + t:4 * k + t + 1], axis=0)).then_inc(s[f"y_back{n % 4}"], 16)

            for k in range(2, 5):
                load_gain(k)
            pool.wait_ge(s["fd_psum"], 8)
            nc.gpsimd.memset(rpbs[0:120, :], 0.0).then_inc(s["rpb_zero"], 1)
            pool.wait_ge(s["rpb_zero"], 1)
            pool.dma_start(rpbs[0:120, 16:47], w["na_rpb_2"][0].rearrange("h a b -> (h a) b")).then_inc(s["rpb_in"], 16)
            pool.wait_ge(s["rpb_in"], 16)
            pool.dma_start(Rp, rpbs[0:120, :]).then_inc(s["rpb_out"], 16)
            pool.wait_ge(s["rpb_out"], 16)
            for h in range(H):
                for r in range(8):
                    src = bass.AP(tensor=Rp.tensor, offset=Rp.offset + 64 * (15 * h + r), ap=[[1, 16], [64, 8], [1, 48]])
                    pool.dma_start(xrev[16 * r:16 * r + 16, h, :].rearrange("p (j u) -> p j u", j=8), src)\
                        .then_inc(s["xrev_in"], 16)
            load_gain(5)
            pool.wait_ge(s["z2_evac"], 12)
            for b, band in enumerate((0, 8, 24, 32)):
                for r in range(8):
                    pool.dma_start(Vband[32 * (r % 4):32 * (r % 4) + 32, b, 512 * (r // 4):512 * (r // 4) + 512],
                                   v2[64 * (r % 2) + band:64 * (r % 2) + band + 32, r // 2, :]).then_inc(s["band_in"], 16)
            attend_pool(pool, na)
            nc.gpsimd.memset(zero_tab, 0.0).then_inc(s["mla_tab"], 1)
            attend_pool(pool, mla)
            load_gain(6)
            load_gain(7)

        @block.tensor
        def _(pe):
            def to_features(k, ready=None):
                for t in range(NT):
                    pe.wait_ge(s["hn_ready"], 4 * k + t + 1)
                    for half_ in range(2):
                        for c in range(4):
                            mm = nc.tensor.transpose(ps[2 * t + half_][:, P * c:P * c + P],
                                                     hn[:, t, P * (4 * half_ + c):P * (4 * half_ + c) + P], ident)
                        mm.then_inc(s["ht_psum"], 1)

            pe.wait_ge(s["const_in"], 16)
            pe.wait_ge(s["pos_in"], 32)
            nc.tensor.transpose(ps[7][:, 0:32], sq[0:32, 0, 0:P], ident[0:32, 0:32]).then_inc(s["pos_psum"], 1)
            pe.wait_ge(s["pos_evac"], 1)
            to_features(0)
            pe.wait_ge(s["ht_ready"], 8)

            def project(n, sem, cols, job):
                arrived(pe, n)
                wv = slot_view(n, 8, cols)
                for t in range(NT):
                    j = job + t
                    if j >= 4:
                        pe.wait_ge(s["z_evac"], j - 3)
                    for c in range(KD):
                        mm = nc.tensor.matmul(ps[j % 4][:, 0:cols], hT[:, c, P * t:P * t + P], wv[:, c, :],
                                              start=c == 0, stop=c == KD - 1)
                    mm.then_inc(sem, 1)

            def heads_to_features(g, src):
                if g < 4:
                    pe.wait_ge(s["head_ready"], g + 1)
                for p_ in range(4 if g < 4 else 2):
                    if g:
                        pe.wait_ge(s["tr_evac"], 4 * (g - 1) + p_ + 1)
                    for t in range(NT):
                        mm = nc.tensor.transpose(ps[4 + p_][:, P * t:P * t + P], src[:, t, P * p_:P * p_ + P], ident)
                    mm.then_inc(s["tr_psum"], 1)

            project(0, s["z_psum"], 512, 0)
            project(1, s["z_psum"], 512, 4)
            heads_to_features(0, zs[0])
            project(2, s["z_psum"], 512, 8)
            heads_to_features(1, zs[1])
            project(3, s["z_psum"], 512, 12)
            project(4, s["z_psum"], 512, 16)
            heads_to_features(2, zs[2])
            project(5, s["z_psum"], 288, 20)
            heads_to_features(3, zk)
            heads_to_features(4, zc)

            pe.wait_ge(s["k2_ready"], 8)
            pe.wait_ge(s["z_evac"], 24)
            for kv in range(2):
                arrived(pe, 6 + kv)
                w1 = slot_view(6 + kv, 16, 256)
                for hc in range(2):
                    k = 2 * kv + hc
                    for c in range(16):
                        nc.tensor.matmul(ps[6][:, k:k + 1], w1[:, c, P * hc:P * hc + P],
                                         posT[:, 16 * kv + c:16 * kv + c + 1], start=c == 0, stop=c == 15)
                    for c in range(16):
                        mm = nc.tensor.matmul(ps[k][:, 0:62], w1[:, c, P * hc:P * hc + P],
                                              view(K2[:, 2 * kv, :], [[T, 2], [16, NCMP]], 2 * c), start=c == 0, stop=c == 15)
                    mm.then_inc(s["cmp_psum"], 1)
            pe.wait_ge(s["lf_ready"], 1)
            for j in range(NT):
                mm = nc.tensor.matmul(ps[4][0:8, :], lf[:, 8 * j:8 * j + 8], upper[:, 384 - P * j:896 - P * j],
                                      start=j == 0, stop=j == NT - 1)
            mm.then_inc(s["cum_psum"], 1)
            pe.wait_ge(s["gelu_done"], 4)
            pe.wait_ge(s["misc_in"], 16 * 9)
            for kv in range(2):
                for g in range(2):
                    for hc in range(2):
                        mm = nc.tensor.matmul(ps[7][0:NCMP, 128 * kv + 64 * g:128 * kv + 64 * g + 64],
                                              hidc[:, kv, hc, NCMP * g:NCMP * g + NCMP], cmp_w2[:, kv, hc, :],
                                              start=hc == 0, stop=hc == 1)
            mm.then_inc(s["cmp2_psum"], 1)
            pe.wait_ge(s["kcn_ready"], 1)
            for g in range(2):
                mm = nc.tensor.transpose(ps[5][:, 32 * g:32 * g + NCMP], kcn[:, P * g:P * g + P], ident[0:NCMP, 0:NCMP])
            mm.then_inc(s["kcn_psum"], 1)
            pe.wait_ge(s["kct_ready"], 1)
            pe.wait_ge(s["gates_ready"], 1)
            pe.wait_ge(s["cum_ready"], 1)

            def fox_table(g):
                if g >= H:
                    return
                if g:
                    pe.wait_ge(s["fox_tab"], g)
                nc.tensor.matmul(ps[7], view(ident[0:8, :], [[0, P]], g), cumT[0:8, :], start=True, stop=True)\
                    .then_inc(s["tab_psum"], 1)

            attend_pe(pe, first, fox_table)

            pe.wait_ge(s["pt_ready"], len(first["steps"]))
            pe.wait_ge(s["o_evac"], 8)

            def mix_job(job, bank, lhs, wv, cols, kc):
                for c in range(kc):
                    mm = nc.tensor.matmul(ps[bank], lhs[:, c, :], wv[:, c, cols:cols + 512], start=c == 0, stop=c == kc - 1)
                mm.then_inc(s["mix_psum"], 1)

            for stage, (blocks_, lhs) in enumerate((((8, 9), hT), ((10,), OaT), ((11, 12), hT), ((13,), ObT))):
                for q in range(8):
                    hf, t = divmod(q, 4)
                    n = blocks_[min(hf, len(blocks_) - 1)]
                    if q in (0, 4):
                        arrived(pe, n)
                    kc = 8 if len(blocks_) == 2 else 4
                    wv = slot_view(n, kc, 512 if kc == 8 else 1024)
                    if stage:
                        sem, value = ((s["mix_sig"], 0), (s["mixed"], 0), (s["mix_sig"], 8))[stage - 1]
                        pe.wait_ge(sem, value + q + 1)
                    mix_job(q, q, lhs[:, :, P * t:P * t + P], wv, 512 * hf if kc == 4 else 0, kc)
            to_features(1)
            pe.wait_ge(s["ht_ready"], 16)
            for hf in range(2):
                arrived(pe, 14 + hf)
                wv = slot_view(14 + hf, 8, 512)
                for t in range(NT):
                    mix_job(0, 4 * hf + t, hT[:, :, P * t:P * t + P], wv, 0, 8)

            pe.wait_ge(s["res_ready"], 4)
            to_features(2)
            pe.wait_ge(s["ht_ready"], 24)
            pe.wait_ge(s["route_in"], 32)
            for t in range(NT):
                for c in range(KD):
                    mm = nc.tensor.matmul(ps[0][:, 20 * t:20 * t + 20], hT[:, c, P * t:P * t + P], w_route[:, c, :],
                                          start=c == 0, stop=c == KD - 1)
            mm.then_inc(s["route_psum"], 1)
            pe.wait_ge(s["chosen"], 1)
            for t in range(NT):
                for j in range(t + 1):
                    nc.tensor.matmul(ps[1][:, 16 * t:16 * t + 16], upper[:, 384 + P * (t - j):512 + P * (t - j)],
                                     rt[:, 16 * j:16 * j + 16], start=j == 0, stop=j == t)
            for j in range(NT):
                mm = nc.tensor.matmul(ps[2][:, 0:16], upper[:, 768:896], rt[:, 16 * j:16 * j + 16], start=j == 0, stop=j == NT - 1)
            mm.then_inc(s["route_psum"], 1)

            def slot_features(b):
                pe.wait_ge(s["x_slot"], 16 * b + 16)
                for h_ in range(2):
                    for c in range(4):
                        mm = nc.tensor.transpose(ps[2 + h_][:, P * c:P * c + P], Xb[:, P * (4 * h_ + c):P * (4 * h_ + c) + P], ident)
                    mm.then_inc(s["xtr_psum"], 1)

            def gate_up(k, i=0):
                for g in range(2):
                    moe_arrived(pe, k + g, i)
                    wv = slot_view(AT_MOE + k + g, 8, 512)
                    for c in range(KD):
                        mm = nc.tensor.matmul(ps[g], XT[:, c, :], wv[:, c, :], start=c == 0, stop=c == KD - 1)
                    mm.then_inc(s["gu_psum"], 1)

            def hidden_features(b):
                pe.wait_ge(s["hb_ready"], b + 1)
                for c in range(4):
                    mm = nc.tensor.transpose(ps[6][:, P * c:P * c + P], hb[:, P * c:P * c + P], ident)
                mm.then_inc(s["htr_psum"], 1)

            def down(k, i=0):
                moe_arrived(pe, k, i)
                wv = slot_view(AT_MOE + k, 4, 1024)
                for hf in range(2):
                    for c in range(4):
                        mm = nc.tensor.matmul(ps[4 + hf], HTs[:, c, :], wv[:, c, 512 * hf:512 * hf + 512], start=c == 0, stop=c == 3)
                    mm.then_inc(s["y_psum"], 1)

            pe.wait_ge(s["routed"], 1)
            slot_features(0)
            pe.wait_ge(s["xt_ready"], 2)
            gate_up(0)
            slot_features(1)
            hidden_features(0)

            def gate_up_and_down(b):
                pe.wait_ge(s["xt_ready"], 2 * b + 2)
                gate_up(2, b - 1)
                slot_features(b + 1)
                pe.wait_ge(s["hts_ready"], b)
                if not (isinstance(b, int) and b == 1):
                    pe.wait_ge(s["yb_ready"], b - 1)
                down(4, b - 1)
                hidden_features(b)

            gate_up_and_down(1)
            last = last_block(pe)
            with pe.Fori(2, last + 1) as b:
                gate_up_and_down(b)
            pe.wait_ge(s["hts_ready"], last + 1)
            pe.wait_ge(s["yb_ready"], last)
            down(2, last)
            pe.wait_ge(s["yb_ready"], last + 1)
            pe.wait_ge(s["xt_ready"], 2 * last + 4)

            def ffn(f, at):
                def chunk_pair(n, j, k, i=0):
                    arrived(pe, n, i)
                    wv = ring[:, place(n)[0], :].rearrange("p (g c n) -> p g c n", g=2, c=8)
                    for q in range(2):
                        if k + q >= 3:
                            pe.wait_ge(s["ff_hid"], j + (NF * f + q - 2))
                        for g in range(2):
                            for c in range(KD):
                                mm = nc.tensor.matmul(ps[2 * ((k + q) % 3) + g], wv[:, g, c, P * q:P * q + P], hT[:, c, :],
                                                      start=c == 0, stop=c == KD - 1)
                        mm.then_inc(s["ff_psum"], 1)

                chunk_pair(at, 0, 0)
                chunk_pair(at + 1, 2, 2)
                with pe.Fori(0, 3) as i:
                    for q in range(3):
                        chunk_pair(at + 2 + q, 6 * i + (4 + 2 * q), 4 + 2 * q, i)
                for hf in range(2):
                    for part, (c0, c1) in enumerate(DOWN_SPLIT):
                        n = at + N_GU + 3 * hf + part
                        arrived(pe, n)
                        if part == 0 and hf == 0:
                            pe.wait_ge(s["ff_hid"], NF * f + NF)
                        wv = slot_view(n, c1 - c0, 512)
                        for t in range(NT):
                            for c in range(c0, c1):
                                mm = nc.tensor.matmul(ps[4 * hf + t], hid[:, c, P * t:P * t + P], wv[:, c - c0, :],
                                                      start=c == 0, stop=c == NF - 1)
                            if part == 2:
                                mm.then_inc(s["fd_psum"], 1)
                            elif t == NT - 1:
                                mm.then_inc(s["fd_block"], 1)
                if f == 0:
                    pe.wait_ge(s["f_evac"], 8)

            to_features(3)
            pe.wait_ge(s["ht_ready"], 32)
            ffn(0, AT_FFN1)

            to_features(4)
            pe.wait_ge(s["ht_ready"], 40)
            for q in range(16):
                n = AT_MID + q // 4
                if q % 4 == 0:
                    arrived(pe, n)
                cols = 512 if q < 12 else 416
                wv = slot_view(n, 8, cols)
                if q >= 8:
                    pe.wait_ge(s["z2_evac"], q - 7)
                r = q % 4
                for c in range(KD):
                    if q < 8:
                        mm = nc.tensor.matmul(ps[q % 8], wv[:, c, P * r:P * r + P], hT[:, c, :], start=c == 0, stop=c == KD - 1)
                    else:
                        mm = nc.tensor.matmul(ps[q % 8][:, 0:cols], hT[:, c, P * r:P * r + P], wv[:, c, :],
                                              start=c == 0, stop=c == KD - 1)
                mm.then_inc(s["z2_psum"], 1)
            pe.wait_ge(s["z2_evac"], 16)

            def na_table(g):
                if g >= H:
                    return
                if g == 0:
                    pe.wait_ge(s["xrev_in"], 16 * 8 * H)
                if g:
                    pe.wait_ge(s["na_tab"], g)
                nc.tensor.matmul(ps[7][:, 0:384], flip, xrev[:, g, :], start=True, stop=True).then_inc(s["tab_psum"], 1)

            pe.wait_ge(s["band_in"], 16 * 32)
            attend_pe(pe, na, na_table)

            def norm_sums(k, sq_):
                pe.wait_ge(s["o_sq"], 4 * k + 4)
                for t in range(NT):
                    for c in range(4):
                        mm = nc.tensor.matmul(ps[7][:, 4 * k + t:4 * k + t + 1], sq_[:, c, P * t:P * t + P], one_col,
                                              start=c == 0, stop=c == 3)
                mm.then_inc(s["nrm_psum"], 1)

            norm_sums(0, sq_na)
            pe.wait_ge(s["cn_ready"], 1)
            pe.wait_ge(s["pt_ready"], mla["n0"])
            for c in range(3):
                for t in range(NT):
                    mm = nc.tensor.transpose(ps[c][:, P * t:P * t + P], z3[:, t, P * c:P * c + P], ident)
                mm.then_inc(s["cn_psum"], 1)
            pe.wait_ge(s["ct_ready"], 3)
            pe.wait_ge(s["o_evac"], 12)
            n = AT_MID + 4
            arrived(pe, n)
            uq, ukv = slot_view(n, 2, 768), slot_view(n, 1, 1024, 1536)
            for t in range(NT):
                for q in range(4):
                    j = 4 * t + q
                    if j >= 4:
                        pe.wait_ge(s["mla_evac"], j - 3)
                    bank = ps[3 + q]
                    if q < 2:
                        for c in range(2):
                            mm = nc.tensor.matmul(bank[:, 0:384], cT[:, c, P * t:P * t + P], uq[:, c, 384 * q:384 * q + 384],
                                                  start=c == 0, stop=c == 1)
                    else:
                        mm = nc.tensor.matmul(bank, cT[:, 2, P * t:P * t + P], ukv[:, 0, 512 * (q - 2):512 * (q - 1)],
                                              start=True, stop=True)
                    mm.then_inc(s["mla_psum"], 1)
            pe.wait_ge(s["roped"], 2)
            for j in range(16):
                src, h = (qz, j) if j < 8 else (kf, j - 8)
                if j >= 3:
                    pe.wait_ge(s["mt_dve" if (j - 3) % 2 else "mt_act"], (j - 3) // 2 + 1)
                for t in range(NT):
                    mm = nc.tensor.transpose(ps[j % 3][0:96, P * t:P * t + P], src[:, t, 96 * h:96 * h + 96], ident)
                mm.then_inc(s["mt_psum"], 1)
            pe.wait_ge(s["mt_act"], 8)
            pe.wait_ge(s["mt_dve"], 8)
            pe.wait_ge(s["mla_evac"], 16)
            attend_pe(pe, mla)
            norm_sums(1, sq_mla)
            pe.wait_ge(s["pt_ready"], mla["n0"] + len(mla["steps"]))
            pe.wait_ge(s["o_evac"], 16)
            for hf in range(2):
                arrived(pe, AT_MID + 5 + hf)
                wv = slot_view(AT_MID + 5 + hf, 8, 512)
                for t in range(NT):
                    for k in range(2):
                        j = 8 * hf + 2 * t + k
                        bank = j % 6
                        if j >= 6:
                            pe.wait_ge(s["f_evac"], 8 + (j - 6) // 2 + 1)
                        for c in range(4):
                            mm = nc.tensor.matmul(ps[bank], hT[:, 4 * k + c, P * t:P * t + P], wv[:, 4 * k + c, :],
                                                  start=c == 0, stop=c == 3)
                        mm.then_inc(s["o2_psum"], 1)
            pe.wait_ge(s["f_evac"], 16)
            to_features(5)
            pe.wait_ge(s["ht_ready"], 48)
            ffn(1, AT_FFN2)

        @block.scalar
        def _(act):
            steps_done, roots = counter(), counter()

            def chained(ins):
                steps_done[0] += 1
                ins.then_inc(s["act_step"], 1)
                act.wait_ge(s["act_step"], steps_done[0])

            def root(ap):
                roots[0] += 1
                act.wait_ge(s["var_ready"], roots[0])
                nc.scalar.activation(ap, ap, ACT.Sqrt).then_inc(s["root_ready"], 1)

            def norm_squares(k):
                for t in range(NT):
                    if k == 0:
                        act.wait_ge(s["x_in"], 16 * NT)
                    else:
                        act.wait_ge(s["res_ready"], 4 * (k - 1) + t + 1)
                    nc.scalar.activation(hn[:, t, :], xres[:, t, :], ACT.Square, accum_out=ss[:, t:t + 1])\
                        .then_inc(s["sumsq"], 1)
                root(rstd[:, 0:NT])

            def to_hT(k):
                for m in range(8):
                    act.wait_ge(s["ht_psum"], 8 * k + m + 1)
                    t, h_ = divmod(m, 2)
                    nc.scalar.activation(hT[:, 4 * h_:4 * h_ + 4, P * t:P * t + P],
                                         ps[m].rearrange("p (c q) -> p c q", c=4), ACT.Copy).then_inc(s["ht_ready"], 1)

            def post_squares(base):
                for t in range(NT):
                    act.wait_ge(s["f_evac"], base + 4 + t + 1)
                    nc.scalar.activation(arena[:, t * D:t * D + D], hn[:, t, :], ACT.Square, accum_out=ss[:, t:t + 1])\
                        .then_inc(s["sumsq"], 1)
                root(rstd[:, 0:NT])

            act.wait_ge(s["pos_evac"], 1)
            norm_squares(0)
            to_hT(0)

            def z_copy(blk, dst, cols):
                for t in range(NT):
                    j = 4 * blk + t
                    act.wait_ge(s["z_psum"], j + 1)
                    nc.scalar.activation(dst[:, t, :], ps[j % 4][:, 0:cols], ACT.Copy).then_inc(s["z_evac"], 1)

            z_copy(0, zs[0], 512)
            z_copy(1, zs[1], 512)
            root(rstd[:, 0:32])
            z_copy(2, vf, 512)
            root(rstd[:, 0:32])
            z_copy(3, zs[2], 512)
            z_copy(4, zc, 512)
            root(rstd[:, 0:32])
            z_copy(5, zd, 288)
            root(rstd[:, 0:16])
            act.wait_ge(s["fox_u"], 1)
            chained(nc.scalar.activation(lf, lf, ACT.Exp))
            nc.scalar.activation(lf, lf, ACT.Ln, bias=one_col).then_inc(s["fox_l"], 1)
            act.wait_ge(s["z_evac"], 24)
            nc.scalar.activation(gates.rearrange("p (t n) -> p t n", t=NT), zd[:, :, 256:280], ACT.Sigmoid)\
                .then_inc(s["gate_raw"], 1)
            act.wait_ge(s["pos_bias_ready"], 1)
            for kv in range(2):
                for hc in range(2):
                    k = 2 * kv + hc
                    act.wait_ge(s["cmp_psum"], k + 1)
                    nc.scalar.activation(hidc[:, kv, hc, :], ps[k][:, 0:62], ACT.Gelu_apprx_tanh,
                                         bias=pos_bias[:, k:k + 1]).then_inc(s["gelu_done"], 1)
            root(rstd[0:NCMP, 0:2])

            def fox_table(g):
                if g >= H:
                    return
                free_tab(act, first, g)
                act.wait_ge(s["tab_psum"], g + 1)
                nc.scalar.activation(tab[:, g % 2, 0:T], ps[7], ACT.Copy).then_inc(s["fox_tab"], 1)

            attend_act(act, first, tables=fox_table)

            for stage in range(2):
                for q in range(8):
                    hf, t = divmod(q, 4)
                    act.wait_ge(s["mix_psum"], 16 * stage + q + 1)
                    if stage:
                        act.wait_ge(s["mixed"], q + 1)
                    nc.scalar.activation(gate_sig[:, t, 512 * hf:512 * hf + 512], ps[q], ACT.Sigmoid)\
                        .then_inc(s["mix_sig"], 1)
            to_hT(1)
            norm_squares(1)
            to_hT(2)
            act.wait_ge(s["exp_in"], 1)
            nc.scalar.activation(rt[:, 1024:1044], rt[:, 1024:1044], ACT.Exp).then_inc(s["exp_out"], 1)

            def slot_copy(b):
                for h_ in range(2):
                    act.wait_ge(s["xtr_psum"], 2 * b + (h_ + 1))
                    nc.scalar.activation(XT[:, 4 * h_:4 * h_ + 4, :], ps[2 + h_].rearrange("p (c q) -> p c q", c=4),
                                         ACT.Copy).then_inc(s["xt_ready"], 1)

            def expert_block(b):
                act.wait_ge(s["gu_psum"], 2 * b + 1)
                if not (isinstance(b, int) and b == 0):
                    act.wait_ge(s["hb_ready"], b)
                nc.scalar.activation(sg, ps[0], ACT.Silu).then_inc(s["silu_done"], 1)
                slot_copy(b + 1)
                act.wait_ge(s["htr_psum"], b + 1)
                nc.scalar.activation(HTs, ps[6].rearrange("p (c q) -> p c q", c=4), ACT.Copy).then_inc(s["hts_ready"], 1)

            act.wait_ge(s["routed"], 1)
            slot_copy(0)
            expert_block(0)
            with act.Fori(1, last_block(act) + 1) as b:
                expert_block(b)
            norm_squares(2)
            to_hT(3)

            def ffn(f):
                def chunk(j, k):
                    act.wait_ge(s["ff_psum"], j + (NF * f + 1))
                    if k >= 2:
                        act.wait_ge(s["ff_hid"], j + (NF * f - 1))
                    nc.scalar.activation(sgb[:, k % 2, :], ps[2 * (k % 3)], ACT.Silu).then_inc(s["ff_silu"], 1)

                for j in range(4):
                    chunk(j, j)
                with act.Fori(0, 3) as i:
                    for q in range(6):
                        chunk(6 * i + (4 + q), 4 + q)
                for m in range(8):
                    hf, t = divmod(m, 4)
                    act.wait_ge(s["fd_psum"], 8 * f + m + 1)
                    nc.scalar.activation(hn[:, t, 512 * hf:512 * hf + 512], ps[m], ACT.Copy).then_inc(s["f_evac"], 1)
                post_squares(16 * f)

            ffn(0)
            norm_squares(3)
            to_hT(4)
            for q in range(16):
                act.wait_ge(s["z2_psum"], q + 1)
                r = q % 4
                dst = (qT2, kT2, v2, z3)[q // 4][:, r, :]
                src = ps[q % 8][:, 0:dst.shape[1]]
                if q < 4:
                    dst = dst.rearrange("p (b r c) -> p r b c", b=4, r=8)
                    src = src.rearrange("p (r b c) -> p r b c", r=8, b=4)
                nc.scalar.activation(dst, src, ACT.Copy, scale=0.125 if q < 4 else 1.0)\
                    .then_inc(s["z2_evac"], 1)

            def squares(ph, dst):
                def evac(u):
                    unit = ph["units"][u]
                    bank = ps[5 + (ph["p0"] + unit["pair"]) % 2]
                    act.wait_ge(s["pv_psum"], ph["u0"] + u + 1)
                    o, i = dst[:, unit["pair"], :], bank
                    if ph is na:
                        o = o.rearrange("p (r b c) -> p b r c", r=8, b=4)
                        i = i.rearrange("p (b r c) -> p b r c", b=4, r=8)
                    nc.scalar.activation(o, i, ACT.Square).then_inc(s["o_sq"], 1)
                return evac

            root(rstd[:, 16:24])
            attend_act(act, na, squares(na, sq_na))
            root(rstd[:, 24:28])
            for c in range(3):
                act.wait_ge(s["cn_psum"], c + 1)
                nc.scalar.activation(cT[:, c, :], ps[c], ACT.Copy).then_inc(s["ct_ready"], 1)
            for t in range(NT):
                for q in range(4):
                    act.wait_ge(s["mla_psum"], 4 * t + q + 1)
                    if q < 2:
                        nc.scalar.activation(qz[:, t, 384 * q:384 * q + 384], ps[3 + q][:, 0:384], ACT.Copy,
                                             scale=float(96 ** -0.5)).then_inc(s["mla_evac"], 1)
                    else:
                        kv = ps[3 + q].rearrange("p (h n) -> p h n", h=4)
                        h = 4 * (q - 2)
                        nc.scalar.activation(kf[:, t, :].rearrange("p (h n) -> p h n", h=H)[:, h:h + 4, 0:64],
                                             kv[:, :, 0:64], ACT.Copy)
                        nc.scalar.activation(vm[:, t, :].rearrange("p (h n) -> p h n", h=H)[:, h:h + 4, :],
                                             kv[:, :, 64:128], ACT.Copy).then_inc(s["mla_evac"], 1)
            for j in range(0, 16, 2):
                act.wait_ge(s["mt_psum"], j + 1)
                dst = qTm if j < 8 else kTm
                nc.scalar.activation(dst[0:96, j % 8, :], ps[j % 3][0:96], ACT.Copy).then_inc(s["mt_act"], 1)
            attend_act(act, mla, squares(mla, sq_mla))
            root(rstd[:, 28:32])
            post_squares(8)
            norm_squares(4)
            to_hT(5)
            ffn(1)

        @block.vector
        def _(dve):
            steps_done, roots, gains_used, norms = counter(), counter(), counter(), counter()
            V = nc.vector

            def chained(ins):
                steps_done[0] += 1
                ins.then_inc(s["dve_step"], 1)
                dve.wait_ge(s["dve_step"], steps_done[0])

            def variance(dst, src, n):
                return V.tensor_scalar(dst, src, 1.0 / n, 1e-6, ALU.mult, ALU.add)

            def inverse_root(ap):
                roots[0] += 1
                dve.wait_ge(s["root_ready"], roots[0])
                chained(V.reciprocal(ap, ap))

            def row_rstd():
                norms[0] += 1
                dve.wait_ge(s["sumsq"], 4 * norms[0])
                variance(rstd[:, 0:NT], ss[:, 0:NT], D).then_inc(s["var_ready"], 1)
                inverse_root(rstd[:, 0:NT])

            def norm_rows():
                row_rstd()
                k = gains_used[0]
                dve.wait_ge(s[f"gain_in{k % 2}"], 16 * (k // 2 + 1))
                for t in range(NT):
                    V.scalar_tensor_tensor(out=hn[:, t, :], in0=xres[:, t, :], scalar=rstd[:, t:t + 1], in1=gain[:, k % 2, :],
                                           op0=ALU.mult, op1=ALU.mult).then_inc(s["hn_ready"], 1)
                gains_used[0] += 1

            def free_gain(value):
                dve.wait_ge(s["hn_ready"], value)
                V.memset(nmax[:, 0:1], 0.0).then_inc(s["gain_used"], 1)

            def post_norm(factor):
                row_rstd()
                k = gains_used[0]
                dve.wait_ge(s[f"gain_in{k % 2}"], 16 * (k // 2 + 1))
                for t in range(NT):
                    chained(V.scalar_tensor_tensor(out=hn[:, t, :], in0=hn[:, t, :], scalar=rstd[:, t:t + 1],
                                                   in1=gain[:, k % 2, :], op0=ALU.mult, op1=ALU.mult))
                    V.scalar_tensor_tensor(out=xres[:, t, :], in0=hn[:, t, :], scalar=factor, in1=xres[:, t, :],
                                           op0=ALU.mult, op1=ALU.add).then_inc(s["res_ready"], 1)
                gains_used[0] += 1
                V.memset(nmax[:, 0:1], 0.0).then_inc(s["gain_used"], 1)

            dve.wait_ge(s["pos_psum"], 1)
            V.tensor_copy(posT, ps[7][:, 0:32]).then_inc(s["pos_evac"], 1)
            norm_rows()
            free_gain(4)

            dve.wait_ge(s["head_gain_in"], 16 * 8)

            def head_norm(g):
                n = 32 if g < 3 else 16
                src = sq if g < 3 else sq[:, :, 0:256]
                dve.wait_ge(s["sq_done"], g + 1)
                ins = V.tensor_reduce(ss[:, 0:n].rearrange("p (t h) -> p t h", t=NT),
                                      src.rearrange("p t (h d) -> p t h d", d=DH), AX.X, ALU.add)
                ins.then_inc(s["sq_used"], 1)
                dve.wait_ge(s["sq_used"], g + 1)
                variance(rstd[:, 0:n], ss[:, 0:n], DH).then_inc(s["var_ready"], 1)
                inverse_root(rstd[:, 0:n])
                if g < 3:
                    z = zs[g].rearrange("p t (h d) -> p (t h) d", d=DH)
                    V.tensor_tensor(z, z, rstd[:, 0:32].unsqueeze(2).to_broadcast([P, 32, DH]), ALU.mult)\
                        .then_inc(s["head_ready"], 1)
                else:
                    out_ = zk.rearrange("p t (s two d) -> p t s two d", two=2, d=DH)
                    r = rstd[:, 0:16].rearrange("p (t s) -> p t s", t=NT)
                    for k in range(2):
                        src = (zc[:, :, 256:384], zd[:, :, 0:P])[k].rearrange("p t (g d) -> p t g d", d=DH)
                        for two in range(2):
                            ins = V.tensor_tensor(out_[:, :, 2 * k:2 * k + 2, two, :], src,
                                                  r[:, :, 2 * k:2 * k + 2].unsqueeze(3).to_broadcast([P, NT, 2, DH]), ALU.mult)
                    ins.then_inc(s["head_ready"], 1)

            def head_copy(g):
                dst, col, factor = ((qT, 0, 0.125), (kT, 1, 1.0), (nqT, 2, 0.125), (kkT, 3, 1.0))[g]
                for p_ in range(4):
                    dve.wait_ge(s["tr_psum"], 4 * g + p_ + 1)
                    V.tensor_scalar(dst[:, p_, :], ps[4 + p_], gcol[:, col:col + 1], factor, ALU.mult, ALU.mult)\
                        .then_inc(s["tr_evac"], 1)

            head_norm(0)
            head_copy(0)
            head_norm(1)
            head_copy(1)
            head_norm(2)
            head_copy(2)
            head_norm(3)
            head_copy(3)
            dve.wait_ge(s["misc_in"], 16 * 9)
            u = tmp32.rearrange("p (t h) -> p t h", t=NT)
            chained(V.tensor_tensor(u, zd[:, :, 280:288], view(forget, [[0, NT], [1, H]]), ALU.add))
            V.scalar_tensor_tensor(out=lf, in0=tmp32, scalar=-1.0, in1=tmp32, op0=ALU.mult, op1=ALU.min).then_inc(s["fox_u"], 1)
            for kv in range(2):
                dve.wait_ge(s["tr_psum"], 16 + kv + 1)
                for g in range(2):
                    V.tensor_copy(K2[0:64, 2 * kv + g, :], ps[4 + kv][64 * g:64 * g + 64, :]).then_inc(s["k2_ready"], 1)
                    V.tensor_copy(K2[64:128, 2 * kv + g, 0:T - 1], ps[4 + kv][64 * g:64 * g + 64, 1:T])\
                        .then_inc(s["k2_ready"], 1)
            dve.wait_ge(s["fox_l"], 1)
            V.scalar_tensor_tensor(out=lf, in0=tmp32, scalar=0.0, in1=lf, op0=ALU.min, op1=ALU.subtract)\
                .then_inc(s["lf_ready"], 1)
            dve.wait_ge(s["gate_raw"], 1)
            g0 = view(gates, [[3, H]])
            V.tensor_scalar(g0, g0, c_("cmp_valid"), None, ALU.mult).then_inc(s["gates_ready"], 1)
            dve.wait_ge(s["cmp_psum"], 4)
            V.tensor_copy(pos_bias, ps[6][:, 0:4]).then_inc(s["pos_bias_ready"], 1)
            dve.wait_ge(s["cum_psum"], 1)
            V.tensor_scalar(cumT[0:8, :], ps[4][0:8, :], -1.0, None, ALU.mult).then_inc(s["cum_ready"], 1)
            dve.wait_ge(s["cmp2_psum"], 1)
            V.tensor_copy(vcmp, ps[7][0:NCMP, P:2 * P])
            chained(V.tensor_copy(kcs, ps[7][0:NCMP, 0:P]))
            chained(V.tensor_tensor(kcs_sq, kcs, kcs, ALU.mult))
            chained(V.tensor_reduce(ss[0:NCMP, 0:2], kcs_sq.rearrange("p (g d) -> p g d", g=2), AX.X, ALU.add))
            variance(rstd[0:NCMP, 0:2], ss[0:NCMP, 0:2], DH).then_inc(s["var_ready"], 1)
            inverse_root(rstd[0:NCMP, 0:2])
            for two in range(2):
                ins = V.tensor_tensor(kcn.rearrange("p (g two d) -> p g two d", g=2, two=2)[:, :, two, :],
                                      kcs.rearrange("p (g d) -> p g d", g=2),
                                      rstd[0:NCMP, 0:2].unsqueeze(2).to_broadcast([NCMP, 2, DH]), ALU.mult)
            ins.then_inc(s["kcn_ready"], 1)
            dve.wait_ge(s["kcn_psum"], 1)
            V.tensor_scalar(kcT, ps[5][:, 0:64].rearrange("p (g n) -> p g n", g=2)[:, :, 0:NCMP], gcol[:, 3:4], None, ALU.mult)\
                .then_inc(s["kct_ready"], 1)

            def copy_out(ph, dst, gains_=None):
                def evac(u):
                    unit = ph["units"][u]
                    pair = unit["pair"]
                    bank = ps[5 + (ph["p0"] + pair) % 2]
                    dve.wait_ge(s["pv_psum"], ph["u0"] + u + 1)
                    if gains_ is None:
                        o = (OaT if pair < 4 else ObT)[:, pair % 4, :]
                        V.tensor_copy(o, bank).then_inc(s["o_evac"], 1)
                        return
                    dve.wait_ge(s["o_sq"], ph["p0"] - 8 + pair + 1)
                    o, i = dst[:, pair, :], bank
                    if ph is na:
                        o = o.rearrange("p (r b c) -> p b r c", r=8, b=4)
                        i = i.rearrange("p (b r c) -> p b r c", b=4, r=8)
                    V.tensor_scalar(o, i, small[:, gains_ + pair:gains_ + pair + 1], None, ALU.mult).then_inc(s["o_evac"], 1)
                return evac

            attend_dve(dve, first, copy_out(first, None))

            for q in range(8):
                hf, t = divmod(q, 4)
                dve.wait_ge(s["mix_psum"], 8 + q + 1)
                dve.wait_ge(s["mix_sig"], q + 1)
                V.tensor_tensor(hn[:, t, 512 * hf:512 * hf + 512], ps[q], gate_sig[:, t, 512 * hf:512 * hf + 512], ALU.mult)\
                    .then_inc(s["mixed"], 1)
            for q in range(8):
                hf, t = divmod(q, 4)
                dve.wait_ge(s["mix_psum"], 24 + q + 1)
                dve.wait_ge(s["mix_sig"], 8 + q + 1)
                chained(V.tensor_tensor(mixtmp[:, q % 2, :], ps[q], gate_sig[:, t, 512 * hf:512 * hf + 512], ALU.mult))
                V.tensor_tensor(hn[:, t, 512 * hf:512 * hf + 512], mixtmp[:, q % 2, :], hn[:, t, 512 * hf:512 * hf + 512],
                                ALU.add).then_inc(s["hn_ready" if hf else "mixed"], 1)
            for q in range(8):
                hf, t = divmod(q, 4)
                dve.wait_ge(s["mix_psum"], 32 + q + 1)
                x_ = xres[:, t, 512 * hf:512 * hf + 512]
                ins = V.tensor_tensor(x_, ps[q], x_, ALU.add)
                if hf:
                    ins.then_inc(s["res_ready"], 1)

            norm_rows()
            free_gain(12)
            dve.wait_ge(s["route_psum"], 1)
            R = NT

            def r3(at, n):
                return rt[:, at:at + R * n].rearrange("p (t n) -> p t n", t=R)

            logits, gl = r3(64, 20), None
            bias20 = small[:, 526:546]
            chained(V.tensor_tensor(logits, ps[0][:, 0:80].rearrange("p (t n) -> p t n", t=R), view(bias20, [[0, R], [1, 20]]), ALU.add))
            iota = view(c_("iota4"), [[0, R], [1, 4]])

            def bc(ap, n):
                return ap.unsqueeze(2).to_broadcast([P, R, n])

            def first_max(src, top, onehot, scratch, low):
                chained(V.tensor_reduce(top, src, AX.X, ALU.max))
                chained(V.tensor_tensor(scratch, src, bc(top, 4), ALU.is_equal))
                chained(V.tensor_tensor(scratch, scratch, iota, ALU.mult))
                chained(V.tensor_reduce(low, scratch, AX.X, ALU.min))
                chained(V.tensor_tensor(onehot, iota, bc(low, 4), ALU.is_equal))

            top_g, top1, top2, low = rt[:, 160:164], rt[:, 164:168], rt[:, 168:172], rt[:, 172:176]
            oh_g, oh1, oh2, scr = r3(176, 4), r3(192, 4), r3(208, 4), r3(224, 4)
            e_in = r3(240, 4)
            prod = rt[:, 256:320]
            first_max(logits[:, :, 0:4], top_g, oh_g, scr, low)
            lg = view(rt, [[20, R], [4, 4], [1, 4]], 68)
            chained(V.tensor_tensor(prod.rearrange("p (t g e) -> p t g e", t=R, g=4), lg,
                                    oh_g.unsqueeze(3).to_broadcast([P, R, 4, 4]), ALU.mult))
            chained(V.tensor_reduce(e_in, prod.rearrange("p (t g e) -> p t e g", t=R, g=4), AX.X, ALU.add))
            first_max(e_in, top1, oh1, scr, low)
            chained(V.scalar_tensor_tensor(out=e_in, in0=oh1, scalar=-3e38, in1=e_in, op0=ALU.mult, op1=ALU.add))
            first_max(e_in, top2, oh2, scr, low)
            M = [rt[:, 320:384], rt[:, 384:448]]
            for k, oh in enumerate((oh1, oh2)):
                chained(V.tensor_tensor(M[k].rearrange("p (t g e) -> p t g e", t=R, g=4),
                                        oh_g.unsqueeze(3).to_broadcast([P, R, 4, 4]),
                                        oh.unsqueeze(2).to_broadcast([P, R, 4, 4]), ALU.mult))
            V.tensor_tensor(rt[:, 0:64], M[0], M[1], ALU.add).then_inc(s["chosen"], 1)
            gd = rt[:, 1024:1040].rearrange("p (t n) -> p t n", t=R)
            chained(V.tensor_tensor(gd, logits[:, :, 0:4], bc(top_g, 4), ALU.subtract))
            V.tensor_tensor(rt[:, 1040:1044], top2, top1, ALU.subtract).then_inc(s["exp_in"], 1)
            dve.wait_ge(s["exp_out"], 1)
            den, wts = rt[:, 1044:1048], rt[:, 1048:1056]
            chained(V.tensor_reduce(den, gd, AX.X, ALU.add))
            chained(V.tensor_scalar(rt[:, 1056:1060], rt[:, 1040:1044], 1.0, None, ALU.add))
            chained(V.tensor_tensor(den, den, rt[:, 1056:1060], ALU.mult))
            chained(V.reciprocal(wts[:, 0:4], den))
            chained(V.tensor_tensor(wts[:, 4:8], wts[:, 0:4], rt[:, 1040:1044], ALU.mult))
            dve.wait_ge(s["route_psum"], 2)
            count, nblk, off = rt[:, 448:464], rt[:, 464:480], rt[:, 480:496]
            chained(V.tensor_copy(count, ps[2][:, 0:16]))
            chained(V.tensor_scalar(nblk, count, 0.0, None, ALU.is_gt))
            for k in range(1, NT):
                chained(V.scalar_tensor_tensor(out=nblk, in0=count, scalar=float(P * k), in1=nblk, op0=ALU.is_gt, op1=ALU.add))
            tri = rt[:, 512:768].rearrange("p (a b) -> p a b", a=16)
            chained(V.tensor_tensor(tri, c_("tri16").rearrange("p (a b) -> p a b", a=16),
                                    view(nblk, [[0, 16], [1, 16]]), ALU.mult))
            chained(V.tensor_reduce(off, tri, AX.X, ALU.add))
            before = rt[:, 768:1152][:, 0:16]
            chained(V.tensor_tensor(before, off, nblk, ALU.subtract))
            chained(V.tensor_scalar(before, before, float(P), -1.0, ALU.mult, ALU.add))
            slot = rt[:, 800:864]
            chained(V.tensor_tensor(slot.rearrange("p (t e) -> p t e", t=R), ps[1][:, 0:64].rearrange("p (t e) -> p t e", t=R),
                                    view(before, [[0, R], [1, 16]]), ALU.add))
            pos = rt[:, 864:872]
            for k in range(2):
                chained(V.tensor_tensor(rt[:, 880:944], slot, M[k], ALU.mult))
                chained(V.tensor_reduce(pos[:, 4 * k:4 * k + 4], rt[:, 880:944].rearrange("p (t e) -> p t e", t=R), AX.X, ALU.add))
            chained(V.tensor_copy(isml[:, 0:8], pos))
            nmax_blocks = 24
            cmp_ = rt[:, 1152:1152 + 16 * nmax_blocks].rearrange("p (b e) -> p b e", b=nmax_blocks)
            chained(V.tensor_tensor(cmp_, view(off, [[0, nmax_blocks], [1, 16]]),
                                    c_("iota_block").unsqueeze(2).to_broadcast([P, nmax_blocks, 16]), ALU.is_le))
            eb = rt[:, 1600:1600 + nmax_blocks]
            chained(V.tensor_reduce(eb, cmp_, AX.X, ALU.add))
            chained(V.tensor_scalar(eb, eb, float(NE - 1), None, ALU.min))
            V.tensor_scalar(isml[:, 32:33], off[:, 15:16], -1.0, None, ALU.add)
            V.tensor_copy(isml[:, 8:8 + nmax_blocks], eb).then_inc(s["routed"], 1)

            def hidden(b):
                dve.wait_ge(s["silu_done"], b + 1)
                dve.wait_ge(s["gu_psum"], 2 * b + 2)
                V.tensor_tensor(hb, ps[1], sg, ALU.mult).then_inc(s["hb_ready"], 1)

            def y_copy(b):
                dve.wait_ge(s["y_psum"], 2 * b + 2)
                if not (isinstance(b, int) and b == 0):
                    dve.wait_ge(s["y_out"], 16 * b)
                V.tensor_copy(Yb, psum[:, 4:6, :].rearrange("p a b -> p (a b)")).then_inc(s["yb_ready"], 1)

            hidden(0)
            hidden(1)
            y_copy(0)
            last = last_block(dve)
            with dve.Fori(2, last + 1) as b:
                hidden(b)
                y_copy(b - 1)
            y_copy(last)
            dve.wait_ge(s["y_out"], 16 * last + 16)
            V.tensor_copy(Yb[0:1, 0:1], psum[0:1, 4, 0:1]).then_inc(s["y_stored"], 1)
            for t in range(NT):
                for k in range(2):
                    n = 2 * t + k
                    dve.wait_ge(s[f"y_back{n % 4}"], 16 * (n // 4 + 1))
                    if k:
                        dve.wait_ge(s["y_used"], t + 1)
                    V.scalar_tensor_tensor(out=xres[:, t, :], in0=Yg[:, n % 4, :], scalar=wts[:, 4 * k + t:4 * k + t + 1],
                                           in1=xres[:, t, :], op0=ALU.mult, op1=ALU.add)\
                        .then_inc(s["res_ready" if k else "y_used"], 1)
            norm_rows()
            free_gain(16)

            def ffn(f, gain_at):
                def chunk(j, k):
                    dve.wait_ge(s["ff_silu"], j + (NF * f + 1))
                    V.tensor_tensor(hid[:, j, :] if isinstance(j, int) else hid[:, ds(j, 1), :].rearrange("p a q -> p (a q)"),
                                    ps[2 * (k % 3) + 1], sgb[:, k % 2, :], ALU.mult).then_inc(s["ff_hid"], 1)

                for j in range(4):
                    chunk(j, j)
                with dve.Fori(0, 3) as i:
                    for q in range(6):
                        chunk(6 * i + (4 + q), 4 + q)
                post_norm(0.5)

            ffn(0, 3)
            norm_rows()
            free_gain(20)
            dve.wait_ge(s["z2_evac"], 16)
            zsq = carve(20672, 256)
            for t in range(NT):
                for k, (a, b_) in enumerate(((0, 256), (256, 384))):
                    ins = V.tensor_tensor_reduce(out=zsq[:, 0:b_ - a], in0=z3[:, t, a:b_], in1=z3[:, t, a:b_], scale=1.0,
                                                 scalar=0.0, op0=ALU.mult, op1=ALU.add, accum_out=ss[:, 16 + 4 * k + t:17 + 4 * k + t])
                    chained(ins)
            chained(variance(rstd[:, 16:20], ss[:, 16:20], 256))
            variance(rstd[:, 20:24], ss[:, 20:24], 128).then_inc(s["var_ready"], 1)
            inverse_root(rstd[:, 16:24])
            for t in range(NT):
                for k, (a, b_) in enumerate(((0, 256), (256, 384))):
                    chained(V.scalar_tensor_tensor(out=z3[:, t, a:b_], in0=z3[:, t, a:b_], scalar=rstd[:, 16 + 4 * k + t:17 + 4 * k + t],
                                                   in1=small[:, 600 + a:600 + b_], op0=ALU.mult, op1=ALU.mult))
            V.memset(nmax[:, 0:1], 0.0).then_inc(s["cn_ready"], 1)

            def na_table(g):
                if g >= H:
                    return
                dve.wait_ge(s["tab_psum"], H + g + 1)
                free_tab(dve, na, g)
                src = ps[7][:, 0:384].rearrange("p (j u) -> p j u", j=8)
                for v, off_ in enumerate((0, 8, 16)):
                    ins = V.tensor_tensor(tab2[:, g % 2, 256 * v:256 * v + 256].rearrange("p (j c) -> p j c", j=8),
                                          src[:, :, 16 - off_:48 - off_],
                                          c_("na_mask")[:, 256 * v:256 * v + 256].rearrange("p (j c) -> p j c", j=8), ALU.add)
                ins.then_inc(s["na_tab"], 1)

            attend_dve(dve, na, copy_out(na, hT[:, 0:4, :], 984), na_table)
            dve.wait_ge(s["nrm_psum"], 1)
            variance(rstd[:, 24:28], ps[7][:, 0:4], 512).then_inc(s["var_ready"], 1)
            inverse_root(rstd[:, 24:28])

            def rope(x1, x2, cos, sin, shape, n):
                t1, t2 = (ropes[:, k, 0:n] for k in range(2))
                if len(shape) == 4:
                    t1, t2 = (a.rearrange("p (t h f) -> p t h f", t=shape[1], h=shape[2]) for a in (t1, t2))
                    t3, t4 = (a.rearrange("p (t h f) -> p t h f", t=shape[1], h=shape[2])
                              for a in (hn[:, 1, 0:n], hn[:, 1, 512:512 + n]))
                else:
                    t1, t2 = (a.rearrange("p (t f) -> p t f", t=shape[1]) for a in (t1, t2))
                    t3, t4 = (a.rearrange("p (t f) -> p t f", t=shape[1]) for a in (hn[:, 1, 0:n], hn[:, 1, 512:512 + n]))
                V.tensor_tensor(t1, x1, cos, ALU.mult)
                V.tensor_tensor(t2, x2, sin, ALU.mult)
                V.tensor_tensor(t3, x2, cos, ALU.mult)
                chained(V.tensor_tensor(t4, x1, sin, ALU.mult))
                V.tensor_tensor(x1, t1, t2, ALU.subtract)
                chained(V.tensor_tensor(x2, t3, t4, ALU.add))

            dve.wait_ge(s["cn_psum"], 3)
            cos3, sin3 = (c_(n).rearrange("p (t f) -> p t f", t=NT) for n in ("cos", "sin"))
            rope(z3[:, :, 384:400], z3[:, :, 400:416], cos3, sin3, [P, NT, 16], 64)
            for t in range(NT):
                dve.wait_ge(s["mla_evac"], 4 * t + 4)
                ins = V.tensor_copy(kf[:, t, :].rearrange("p (h n) -> p h n", h=H)[:, :, 64:96],
                                    view(z3[:, t, 384:416], [[0, H], [1, 32]]))
            ins.then_inc(s["roped"], 1)
            for t in range(NT):
                q_ = qz[:, t, :].rearrange("p (h n) -> p h n", h=H)
                ct, st_ = (view(c_(n), [[0, H], [1, 16]], 16 * t) for n in ("cos", "sin"))
                rope(q_[:, :, 64:80], q_[:, :, 80:96], ct, st_, [P, H, 16], 128)
            V.memset(nmax[:, 0:1], 0.0).then_inc(s["roped"], 1)
            for j in range(1, 16, 2):
                dve.wait_ge(s["mt_psum"], j + 1)
                dst = qTm if j < 8 else kTm
                V.tensor_copy(dst[0:96, j % 8, :], ps[j % 3][0:96]).then_inc(s["mt_dve"], 1)
            dve.wait_ge(s["mla_tab"], 1)
            attend_dve(dve, mla, copy_out(mla, hT[:, 4:8, :], 988))
            dve.wait_ge(s["nrm_psum"], 2)
            variance(rstd[:, 28:32], ps[7][:, 4:8], 512).then_inc(s["var_ready"], 1)
            inverse_root(rstd[:, 28:32])
            for q in range(8):
                hf, t = divmod(q, 4)
                f_ = hn[:, t, 512 * hf:512 * hf + 512]
                dve.wait_ge(s["o2_psum"], 2 * q + 1)
                chained(V.tensor_scalar(f_, ps[(2 * q) % 6], rstd[:, 24 + t:25 + t], None, ALU.mult))
                dve.wait_ge(s["o2_psum"], 2 * q + 2)
                V.scalar_tensor_tensor(out=f_, in0=ps[(2 * q + 1) % 6], scalar=rstd[:, 28 + t:29 + t], in1=f_,
                                       op0=ALU.mult, op1=ALU.add).then_inc(s["f_evac"], 1)
            post_norm(1.0)
            norm_rows()
            free_gain(24)
            ffn(1, 7)


_INS = ["x", "norm_mix_g", "w_in", "b_forget", "fox_q_g", "fox_k_g", "nsa_q_g", "nsa_k_g", "cmp_k_w1", "cmp_k_w2",
        "cmp_k_pos", "cmp_v_w1", "cmp_v_w2", "cmp_v_pos", "w_fox_up", "w_nsa_up", "w_out", "norm_ffn_g", "w_group",
        "b_group", "w_router", "b_router", "w_gate", "w_up", "w_down", "ffn1_pre_g_2", "ffn1_w_gu_2", "ffn1_w_down_2",
        "ffn1_post_g_2", "mix_pre_g_2", "w_in_2", "na_rpb_2", "mla_q_norm_g_2", "mla_w_uq_2", "mla_kv_norm_g_2",
        "mla_w_ukv_2", "na_out_norm_g_2", "mla_out_norm_g_2", "w_out_2", "mix_post_g_2", "ffn2_pre_g_2",
        "ffn2_w_gu_2", "ffn2_w_down_2", "ffn2_post_g_2"]


def kernel(**inputs):
    import numpy as _np
    import concourse.bacc as _bacc
    from concourse import mybir as _mybir
    from concourse.bass_utils import run_bass_kernel_spmd as _run

    nc = _bacc.Bacc("TRN2", target_bir_lowering=False, num_devices=1)
    arrays, w = {}, {}
    arrays["in_consts"] = shape_constants()
    w["consts"] = nc.dram_tensor("in_consts", arrays["in_consts"].shape, _mybir.dt.float32, kind="ExternalInput").ap()
    for name in _INS:
        a = _np.ascontiguousarray(inputs[name])
        arrays["in_" + name] = a
        w[name] = nc.dram_tensor("in_" + name, a.shape, _mybir.dt.from_np(a.dtype), kind="ExternalInput").ap()
    out = nc.dram_tensor("out_0", (1, T, D), _mybir.dt.float32, kind="ExternalOutput").ap()
    build_blocks(nc, w, out)
    r = _run(nc, [arrays], core_ids=[0])
    return r.results[0]["out_0"]
```

```python
import numpy as np

P = 128
T, D = 512, 1024
NT = T // P
KD = D // P
H, DH = 8, 64
NE, NG, EPG, FE = 16, 4, 4, 512
NSLOT_BLOCKS = (2 * T + NE * (P - 1)) // P
F = 2816
NF = F // P
NCMP = 31
NEG = -1e30
RING = 3
SLOT = 4096
LAG = 3

CONSTS = {}


def _place(name, width):
    CONSTS[name] = (sum(w for _, w in CONSTS.values()), width)


for _name, _width in (("ident", P), ("flip", P), ("ones_upper", 896), ("dist", T), ("diag_mask", P),
                      ("cmp_dist", NT * NCMP), ("cmp_valid", 1), ("tri16", 256), ("iota_block", 24),
                      ("iota4", 4), ("cos", NT * 16), ("sin", NT * 16), ("na_mask", 3 * 256)):
    _place(_name, _width)
NCONST = sum(w for _, w in CONSTS.values())


def shape_constants():
    f = np.float32
    p = np.arange(P)[:, None]
    tab = {}
    tab["ident"] = np.eye(P)
    tab["flip"] = np.eye(P)[::-1]
    tab["ones_upper"] = (p <= np.arange(896)[None] - 384)
    off = np.arange(T)[None] - 384 - p
    tab["dist"] = np.where(off <= 0, off, NEG)
    tab["diag_mask"] = np.where(np.arange(P)[None] <= p, 0.0, NEG)
    tok = np.arange(NT)[None, :, None] * P + np.arange(P)[:, None, None]
    cd = tok - (np.arange(NCMP) * 16 + 31)[None, None, :]
    tab["cmp_dist"] = np.where(cd >= 0, -cd, NEG).reshape(P, -1)
    tab["cmp_valid"] = (p >= 31)
    e = np.arange(16)
    tab["tri16"] = np.broadcast_to((e[None, :] <= e[:, None]).reshape(1, 256), (P, 256))
    tab["iota_block"] = np.broadcast_to(np.arange(24)[None], (P, 24))
    tab["iota4"] = np.broadcast_to(np.arange(4)[None] - 99.0, (P, 4))
    t = np.arange(T)
    inv = (f(1.0) / (f(10000.0) ** (np.arange(8, dtype=f) / f(8)))).astype(f)
    ang = np.concatenate([(t // 64).astype(f)[:, None] * inv, (t % 64).astype(f)[:, None] * inv], axis=-1)
    for name, fn in (("cos", np.cos), ("sin", np.sin)):
        tab[name] = fn(ang).astype(f).reshape(NT, P, 16).transpose(1, 0, 2).reshape(P, -1)
    masks = []
    for c0, band in ((0, 0), (16, 8), (48, 32)):
        col = c0 + np.arange(16)
        start = np.clip(col - 8, 0, 48)
        key = band + np.arange(32)
        ok = (key[None] >= start[:, None]) & (key[None] < start[:, None] + 16)
        m = np.where(ok, 0.0, NEG)
        masks.append(np.broadcast_to(m[None, :, None, :], (8, 16, 8, 32)).reshape(P, 256))
    tab["na_mask"] = np.concatenate(masks, axis=1)
    return np.concatenate([np.asarray(tab[n], f).reshape(P, w) for n, (_, w) in CONSTS.items()], axis=1)


def weight_blocks(w):
    def chunks(m, c0, c1, cols):
        return m[c0 * P:c1 * P, cols].rearrange("(c p) n -> p c n", p=P)

    blocks = {}
    w_in, w_in2 = w["w_in"][0], w["w_in_2"][0]
    first = []
    for lo in (0, 512, 1024, 1544, 2056):
        first.append([(0, 512, chunks(w_in, 0, 8, slice(lo, lo + 512)))])
    first.append([(0, 288, chunks(w_in, 0, 8, slice(2568, 2848))), (280, 288, chunks(w_in, 0, 8, slice(1536, 1544)))])
    for n in ("cmp_k_w1", "cmp_v_w1"):
        first.append([(0, 256, chunks(w[n][0], 0, 16, slice(0, 256)))])
    for lo in (2848, 3360):
        first.append([(0, 512, chunks(w_in, 0, 8, slice(lo, lo + 512)))])
    first.append([(0, 1024, chunks(w["w_fox_up"][0], 0, 4, slice(0, 1024)))])
    for lo in (3872, 4384):
        first.append([(0, 512, chunks(w_in, 0, 8, slice(lo, lo + 512)))])
    first.append([(0, 1024, chunks(w["w_nsa_up"][0], 0, 4, slice(0, 1024)))])
    for lo in (0, 512):
        first.append([(0, 512, chunks(w["w_out"][0], 0, 8, slice(lo, lo + 512)))])
    blocks["first"] = first
    mid = []
    for lo, hi in ((0, 512), (512, 1024), (1024, 1536), (1536, 1952)):
        mid.append([(0, hi - lo, chunks(w_in2, 0, 8, slice(lo, hi)))])
    mid.append([(0, 768, chunks(w["mla_w_uq_2"][0], 0, 2, slice(0, 768))),
                (1536, 1024, chunks(w["mla_w_ukv_2"][0], 0, 1, slice(0, 1024)))])
    for lo in (0, 512):
        mid.append([(0, 512, chunks(w["w_out_2"][0], 0, 8, slice(lo, lo + 512)))])
    blocks["mid"] = mid
    return blocks


N_FIRST = 16
AT_MOE = AT_MID = N_FIRST
HALF = NF // 2
UNITS = HALF + (HALF + 1) // 2
RAW = 4


def build_blocks(nc, w, out):
    import concourse.bass as bass
    from concourse import mybir

    f32, i32, f32r = mybir.dt.float32, mybir.dt.int32, mybir.dt.float32r
    ALU, ACT, AX = mybir.AluOpType, mybir.ActivationFunctionType, mybir.AxisListType
    ds = bass.ds

    def sb(name, shape, dt=f32):
        return nc.alloc_sbuf_tensor(name, shape, dt)

    def view(ap, dims, off=0):
        return bass.AP(tensor=ap.tensor, offset=ap.offset + off, ap=[ap.ap[0]] + dims)

    const = sb("const", [P, NCONST])
    xres = sb("xres", [P, NT, D])
    hn = sb("hn", [P, NT, D])
    gain = sb("gain", [P, 2, D])
    ss = sb("ss", [P, 32])
    rstd = sb("rstd", [P, 32])
    small = sb("small", [P, 1000])
    isml = sb("isml", [P, 64], i32)
    sums = sb("sums", [P, 8])
    nmax = sb("nmax", [P, 8])
    rr = sb("rr", [P, 8])
    cmp_w2 = sb("cmp_w2", [P, 2, 2, DH])
    w_route = sb("w_route", [P, KD, 20])
    AR = 21880
    slab_at = (nc.sbuf_base + 31) // 32 * 32
    slab = sb("slab", [P, RING * SLOT + KD * T + AR])
    ring = slab[:, 0:RING * SLOT].rearrange("p (s n) -> p s n", s=RING)
    hT = slab[:, RING * SLOT:RING * SLOT + KD * T].rearrange("p (k t) -> p k t", k=KD)
    ARENA = RING * SLOT + KD * T
    arena = slab[:, ARENA:]

    def parts(name, at, *shape):
        return nc.alloc_sbuf_tensor_at(name, [P] + list(shape), f32r, offset=slab_at + 4 * at)

    def carve(at, *shape):
        n = int(np.prod(shape))
        assert at + n <= AR, (at, shape)
        ap = arena[:, at:at + n]
        if len(shape) == 2:
            ap = ap.rearrange("p (a b) -> p a b", a=shape[0])
        if len(shape) == 3:
            ap = ap.rearrange("p (a b c) -> p a b c", a=shape[0], b=shape[1])
        return ap

    def c_(name):
        at, width = CONSTS[name]
        return const[:, at:at + width]

    ident, flip, upper, dist, diag_mask = (c_(n) for n in ("ident", "flip", "ones_upper", "dist", "diag_mask"))
    one_col = upper[:, 895:896]

    qT, kT = carve(0, 4, T), carve(2048, 4, T)
    nqT, kkT = carve(4096, 4, T), carve(6144, 4, T)
    vf = carve(8192, NT, 512)
    zc = carve(10240, NT, 512)
    zd = carve(12288, NT, 288)
    OaT, ObT = carve(13440, 4, T), carve(15488, 4, T)
    zs = [OaT, ObT, carve(17536, 4, T)]
    K2 = carve(19584, 4, T)
    PB = carve(17536, 4, T)
    tab = carve(19584, 2, 768)
    zk, sq = hn[:, 0:2, :].rearrange("p a b -> p (a b)").rearrange("p (t n) -> p t n", t=NT), \
        hn[:, 2:4, :].rearrange("p a b -> p (a b)").rearrange("p (t n) -> p t n", t=NT)
    PT = hn[:, :, :].rearrange("p (u a) b -> p u (a b)", u=2).rearrange("p u (j q) -> p u j q", j=4)
    lf, forget = small[:, 0:32], small[:, 32:40]
    tmp32 = small[:, 40:72]
    gates = small[:, 72:168]
    gcol = small[:, 168:172]
    posT = small[:, 172:204]
    pos_bias = small[:, 204:208]
    kcT = small[:, 208:270].rearrange("p (g n) -> p g n", g=2)
    vcmp = small[0:NCMP, 270:398]
    kcn = carve(17792, 2 * P)[0:NCMP]
    kcs, kcs_sq = carve(17536, P)[0:NCMP], carve(17664, P)[0:NCMP]
    hidc = carve(21632, 2, 2, 62)
    cumT = carve(21120, T)
    pos_raw = hn[0:32, 0, 0:P]
    gate_sig = carve(0, NT, D)
    mixtmp = carve(4096, 2, 512)
    Xb, XT = carve(0, D), carve(1024, KD, P)
    sg, hb, HTs, Yb = carve(2048, 512), carve(2560, 512), carve(3072, 4, P), carve(3584, D)
    Yg = carve(4608, 4, D)
    rt = carve(8704, 2048)
    zeros = cmp_w2[:, :, :, :].rearrange("p a b c -> p (a b c)")
    w_hi, w_lo = parts("w_hi", 0, 2, 2048), parts("w_lo", SLOT, 2, 2048)
    hT_hi, hT_lo = parts("hT_hi", 2 * SLOT, KD, T), parts("hT_lo", 3 * SLOT, KD, T)
    hid_hi, hid_lo = parts("hid_hi", ARENA, HALF, T), parts("hid_lo", ARENA + HALF * T, HALF, T)
    sgb = carve(2 * HALF * T, 2, T)
    raw = carve(AR - RAW * 2048, RAW, 2048)
    qT2, kT2, Vband = carve(0, 4, T), carve(2048, 4, T), carve(4096, 4, 1024)
    v2 = carve(8192, NT, 512)
    xrev = carve(10240, H, 384)
    z3 = carve(13312, NT, 416)
    PB2 = carve(14976, 4, T)
    tab2 = carve(17024, 2, 768)
    sq_na = carve(18560, 4, T)
    rpbs = carve(20608, 64)
    qTm, kTm, vm = carve(0, H, T), carve(4096, H, T), carve(8192, NT, 512)
    cT, PBm, zero_tab = carve(10240, 3, T), carve(10240, 4, T), carve(12288, T)
    ropes = hn[:, 0, :].rearrange("p (a b) -> p a b", a=2)
    qz, kf = carve(14976, NT, 768), carve(18048, NT, 768)
    sq_mla = carve(14976, 4, T)

    psum = nc.alloc_psum_tensor("psum", [P, 8, 512], f32)
    ps = [psum[:, i, :] for i in range(8)]
    Xs = nc.dram_tensor("x_slots", (24 * P, D), f32, kind="Internal").ap()
    Ys = nc.dram_tensor("y_slots", (NSLOT_BLOCKS * P, D), f32, kind="Internal").ap()
    Rp = nc.dram_tensor("rpb_padded", (H * 15, 64), f32, kind="Internal").ap()

    names = """x_in const_in moe_load0 moe_load1 moe_load2 y_stored load0 load1 load2 load3 gain_in0 gain_in1 gain_used head_gain_in pos_in misc_in cn_gain_in
        route_in hn_ready ht_psum ht_ready var_ready root_ready dve_step act_step pool_step
        sumsq z_psum z_evac sq_done sq_used head_ready tr_psum tr_evac k2_ready pos_psum pos_evac cmp_psum
        pos_bias_ready gelu_done cmp2_psum kcn_ready kcn_psum kct_ready
        fox_u fox_l lf_ready gate_raw gates_ready cum_psum cum_ready
        tab_psum fox_tab nsa_tab na_tab mla_tab score_psum scored expd recd scaled pt_psum pt_ready pv_psum o_evac o_sq
        mix_psum mix_sig mixed res_ready route_psum chosen exp_in exp_out routed zero_ready zero_out scattered x_slot xtr_psum xt_ready
        gu_psum silu_done hb_ready htr_psum hts_ready y_psum yb_ready y_out y_back0 y_back1 y_back2 y_back3 y_used
        raw0 raw1 raw2 raw3 split_hi split_lo unit_done ff_silu gated hid_high ff_hid fd_psum f_evac hT_low_ready
        z2_psum z2_evac rpb_in rpb_pad rpb_out rpb_zero xrev_in band_in cn_ready cn_psum ct_ready
        mla_psum mla_evac roped mt_psum mt_act mt_dve nrm_psum o2_psum out_dma vm_free""".split()
    s = {n: nc.alloc_semaphore(n) for n in names}
    loaded = [s[f"load{i}"] for i in range(RING)]
    blocks = weight_blocks(w)

    def place(n):
        return n % RING, n // RING

    def released(n, i=0):
        if n < 6:
            return s["z_psum"], 4 * n + 4
        if n < 8:
            return s["cmp_psum"], 2 * (n - 5)
        if n < N_FIRST:
            return s["mix_psum"], (4, 8, 16, 20, 24, 32, 36, 40)[n - 8]
        k = n - AT_MID
        if k < 4:
            return s["z2_psum"], 4 * k + 4
        return (s["mla_psum"], 16) if k == 4 else (s["o2_psum"], 8 * (k - 4))

    def arrived(pe, n, i=0):
        slot, use = place(n)
        pe.wait_ge(loaded[slot], 32 * (use + 1) + 32 * i)

    moe_loaded = [s[f"moe_load{i}"] for i in range(RING)]

    def moe_arrived(pe, k, i=0):
        pe.wait_ge(moe_loaded[k % RING], 32 * (k // RING + 1) + 32 * i)

    raw_in = [s[f"raw{i}"] for i in range(RAW)]

    def unit_used(eng, g, v, i=0):
        if v == UNITS - 1:
            eng.wait_ge(s["fd_psum"], 8 * g + 8)
        else:
            eng.wait_ge(s["unit_done"], i + ((UNITS - 1) * g + v + 1))

    def split_high(g, v, i=0):
        act, u = nc.scalar, UNITS * g + v
        act.wait_ge(raw_in[u % RAW], 32 * (u // RAW + 1) + (i * 8))
        if v >= 2:
            unit_used(act, g, v - 2, i)
        elif g % 2:
            unit_used(act, g - 1, UNITS + v - 2)
        act.activation(w_hi[:, u % 2, :], raw[:, u % RAW, :], ACT.Copy).then_inc(s["split_hi"], 1)

    def split_low(g, v, i=0):
        dve, u = nc.vector, UNITS * g + v
        dve.wait_ge(s["split_hi"], i + (u + 1))
        dve.tensor_tensor(w_lo[:, u % 2, :], raw[:, u % RAW, :], w_hi[:, u % 2, :].bitcast(f32), ALU.subtract)\
            .then_inc(s["split_lo"], 1)

    def products(out, high, low, by_high, by_low, first, last):
        nc.tensor.matmul(out, high, by_high, start=first, stop=False)
        nc.tensor.matmul(out, high, by_low, start=False, stop=False)
        return nc.tensor.matmul(out, low, by_high, start=False, stop=last)

    def slot_view(n, chunks, width, at=0):
        slot = place(n)[0]
        return ring[:, slot, at:at + chunks * width].rearrange("p (c n) -> p c n", c=chunks)

    def half(ap, h):
        return ap[64 * (h % 2):64 * (h % 2) + 64]

    def make_phase(name):
        units, steps, groups, pairs = [], [], [], []
        if name == "first":
            heads = [("fox", h) for h in range(H)] + [("nsa", h) for h in range(H)]
        else:
            heads = [(name, h) for h in range(H)]
        for g, (kind, h) in enumerate(heads):
            groups.append(dict(kind=kind, h=h, first=len(steps)))
            branches = {"fox": ("fox",), "nsa": ("slc", "win", "cmp"), "na": ("na",), "mla": ("mla",)}[kind]
            for br in branches:
                u = len(units)
                unit = dict(pair=g // 2, pv=[], last_of_pair=(br == branches[-1] and h % 2 == 1))
                units.append(unit)
                kv = h // 4
                first_br, last_br = br == branches[0], br == branches[-1]
                if kind in ("fox", "nsa") and br != "cmp":
                    v_of = {"fox": lambda j: vf[:, j, 64 * h:64 * h + 64],
                            "slc": lambda j: zc[:, j, 384 + 64 * kv:448 + 64 * kv],
                            "win": lambda j: zd[:, j, 128 + 64 * kv:192 + 64 * kv]}[br]
                    k_of = {"fox": lambda: half(kT, h)[:, h // 2, :], "slc": lambda: half(kkT, h)[:, kv, :],
                            "win": lambda: half(kkT, h)[:, 2 + kv, :]}[br]()
                    q_of = half(qT if kind == "fox" else nqT, h)[:, h // 2, :]
                    for i in range(NT):
                        n = P * (i + 1)
                        steps.append(dict(
                            u=u, g=g, lhsT=q_of[:, P * i:P * i + P], rhs=k_of[:, 0:n], keys=n, out=(n,),
                            mask=kind == "fox", tab=(0, n) if kind == "fox" else None,
                            const_tab=None, shift=384 - P * i if kind == "nsa" else 0, first=i == 0, last=i == NT - 1,
                            gate=None if kind == "fox" else gates[:, 24 * i + 3 * h + (1 if br == "slc" else 2):][:, 0:1],
                            blocks=[(P * j, P) for j in range(i + 1)], rows=P, dst=P * i))
                    for j in range(NT):
                        unit["pv"].append((v_of(j), (j, P * j, T), (P * j, T), first_br and j == 0, last_br and j == NT - 1))
                elif br == "cmp":
                    for i in range(NT):
                        steps.append(dict(
                            u=u, g=g, lhsT=half(nqT, h)[:, h // 2, P * i:P * i + P], rhs=half(kcT, h)[:, kv, :],
                            keys=NCMP, mask=False, tab=None, const_tab=None, shift=512 + NCMP * i, first=i == 0,
                            last=i == NT - 1, gate=gates[:, 24 * i + 3 * h:24 * i + 3 * h + 1],
                            blocks=[(0, NCMP)], rows=NCMP, dst=P * i))
                    unit["pv"].append((vcmp[:, 64 * kv:64 * kv + 64], (0, 0, T), (0, T), False, True))
                elif kind == "na":
                    q_of = half(qT2, h)[:, h // 2, :]
                    k_of = half(kT2, h)[:, h // 2, :].rearrange("p (r c) -> p r c", r=8)
                    for b in range(4):
                        band = (0, 8, 24, 32)[b]
                        steps.append(dict(
                            u=u, g=g, lhsT=q_of[:, P * b:P * b + P], rhs=k_of[:, :, band:band + 32], keys=256,
                            mask=False, tab=None, const_tab=None, shift=256 * (0, 1, 1, 2)[b], first=b == 0,
                            last=b == 3, gate=None, blocks=[(0, P), (P, P)], rows=P, dst=P * b))
                        for j in range(2):
                            unit["pv"].append((Vband[:, b, 512 * j + 64 * h:512 * j + 64 * h + 64],
                                               (j, P * b, P * b + P), (P * b, P * b + P), j == 0, j == 1))
                else:
                    for i in range(NT):
                        steps.append(dict(
                            u=u, g=g, lhsT=qTm[0:96, h, P * i:P * i + P], rhs=kTm[0:96, h, :], keys=T, mask=False,
                            tab=None, const_tab=zero_tab, shift=0, first=i == 0, last=i == NT - 1, gate=None,
                            blocks=[(P * j, P) for j in range(NT)], rows=P, dst=P * i))
                    for j in range(NT):
                        unit["pv"].append((vm[:, j, 64 * h:64 * h + 64], (j, 0, T), (0, T), j == 0, j == NT - 1))
        for unit in units:
            unit["h"] = 0
        at = 0
        for g, (kind, h) in enumerate(heads):
            for _ in range(3 if kind == "nsa" else 1):
                units[at]["h"] = h
                at += 1
        return dict(name=name, units=units, steps=steps, groups=groups, pb={"first": PB, "na": PB2, "mla": PBm}[name],
                    tab={"first": tab, "na": tab2, "mla": None}[name], n_pairs=len(heads) // 2)

    phases = [make_phase("first"), make_phase("na"), make_phase("mla")]
    n_steps = n_units = n_pairs = 0
    for ph in phases:
        ph.update(n0=n_steps, u0=n_units, p0=n_pairs)
        n_steps += len(ph["steps"])
        n_units += len(ph["units"])
        n_pairs += ph["n_pairs"]

    def bias_of(ph, st):
        if st["const_tab"] is not None:
            return st["const_tab"][:, 0:st["keys"]]
        t = ph["tab"][:, st["g"] % 2, st["shift"]:st["shift"] + st["keys"]]
        return t

    def attend_pe(pe, ph, tables=None):
        steps, units, n0, u0 = ph["steps"], ph["units"], ph["n0"], ph["u0"]
        if tables:
            tables(0)
        for m in range(len(steps) + LAG + 1):
            if m < len(steps):
                st = steps[m]
                if tables and ph["groups"][st["g"]]["first"] == m:
                    tables(st["g"] + 1)
                if n0 + m >= 3:
                    pe.wait_ge(s["scored"], n0 + m - 2)
                bank = ps[(n0 + m) % 3]
                out = bank[:, 0:st["keys"]]
                mm = nc.tensor.matmul(out, st["lhsT"], st["rhs"], start=True, stop=not st["mask"])
                if st["mask"]:
                    mm = nc.tensor.matmul(bank[:, st["keys"] - P:st["keys"]], ident, diag_mask, start=False, stop=True)
                mm.then_inc(s["score_psum"], 1)
            if 0 <= m - LAG < len(steps):
                n = m - LAG
                st = steps[n]
                if n0 + n >= 2:
                    pe.wait_ge(s["pt_ready"], n0 + n - 1)
                pe.wait_ge(s["scaled"], n0 + n + 1)
                bank, pbuf = ps[3 + (n0 + n) % 2], ph["pb"][:, (n0 + n) % 4, :]
                for j, (c0, rows) in enumerate(st["blocks"]):
                    mm = nc.tensor.transpose(bank[0:rows, P * j:P * j + P], pbuf[:, c0:c0 + rows], ident)
                mm.then_inc(s["pt_psum"], 1)
            n = m - LAG - 1
            if n >= 0 and steps[n]["last"]:
                u = steps[n]["u"]
                unit = units[u]
                pair = ph["p0"] + unit["pair"]
                pe.wait_ge(s["pt_ready"], n0 + n + 1)
                if unit["h"] % 2 == 0 and pair >= 2:
                    pe.wait_ge(s["o_evac"], pair - 1)
                bank = ps[5 + pair % 2]
                last = None
                for lhsT, (j, a, b), (c, d), start, stop in unit["pv"]:
                    rows = lhsT.shape[0]
                    last = nc.tensor.matmul(half(bank, unit["h"])[:, c:d], lhsT, PT[0:rows, (u0 + u) % 2, j, a:b],
                                            start=start, stop=stop)
                last.then_inc(s["pv_psum"], 1)

    def attend_dve(dve, ph, evac, tables=None):
        steps, n0 = ph["steps"], ph["n0"]

        def recip(n):
            dve.wait_ge(s["expd"], n0 + n + 1)
            if n0 + n >= 8:
                dve.wait_ge(s["scaled"], n0 + n - 7)
            k = (n0 + n) % 8
            nc.vector.reciprocal(rr[:, k:k + 1], sums[:, k:k + 1]).then_inc(s["recd"], 1)

        if tables:
            tables(0)
        for m in range(len(steps) + LAG + 1):
            if m < len(steps):
                st = steps[m]
                if tables and ph["groups"][st["g"]]["first"] == m:
                    tables(st["g"] + 1)
                if st["first"] and st["const_tab"] is None:
                    kind, h = ph["groups"][st["g"]]["kind"], ph["groups"][st["g"]]["h"]
                    dve.wait_ge(s[f"{kind}_tab"], h + 1)
                dve.wait_ge(s["score_psum"], n0 + m + 1)
                if n0 + m >= 4:
                    dve.wait_ge(s["pt_psum"], n0 + m - 3)
                k = (n0 + m) % 8
                n = st["keys"]
                nc.vector.tensor_tensor_reduce(
                    out=ph["pb"][:, (n0 + m) % 4, 0:n], in0=ps[(n0 + m) % 3][:, 0:n], in1=bias_of(ph, st), scale=-1.0,
                    scalar=3e38, op0=ALU.add, op1=ALU.min, accum_out=nmax[:, k:k + 1]).then_inc(s["scored"], 1)
            if 0 <= m - 1 < len(steps):
                recip(m - 1)
            n = m - LAG - 1
            if n >= 0 and steps[n]["last"] and ph["units"][steps[n]["u"]]["last_of_pair"]:
                evac(steps[n]["u"])

    def attend_act(act, ph, evac=None, tables=None):
        steps, n0, u0 = ph["steps"], ph["n0"], ph["u0"]
        if tables:
            tables(0)
        for m in range(len(steps) + LAG + 1):
            if m < len(steps):
                st = steps[m]
                if tables and ph["groups"][st["g"]]["first"] == m:
                    tables(st["g"] + 1)
                act.wait_ge(s["scored"], n0 + m + 1)
                if n0 + m >= 8:
                    act.wait_ge(s["recd"], n0 + m - 7)
                k = (n0 + m) % 8
                p = ph["pb"][:, (n0 + m) % 4, 0:st["keys"]]
                nc.scalar.activation(p, p, ACT.Exp, bias=nmax[:, k:k + 1], scale=-1.0,
                                     accum_out=sums[:, k:k + 1]).then_inc(s["expd"], 1)
            if 0 <= m - LAG < len(steps):
                n = m - LAG
                st = steps[n]
                u = u0 + st["u"]
                act.wait_ge(s["pt_psum"], n0 + n + 1)
                if st["first"] and u >= 2:
                    act.wait_ge(s["pv_psum"], u - 1)
                nj, rows = len(st["blocks"]), st["rows"]
                src = ps[3 + (n0 + n) % 2][0:rows, 0:P * nj].rearrange("p (j q) -> p j q", j=nj)
                nc.scalar.activation(PT[0:rows, u % 2, 0:nj, st["dst"]:st["dst"] + P], src, ACT.Copy)\
                    .then_inc(s["pt_ready"], 1)
            n = m - LAG - 1
            if evac and n >= 0 and steps[n]["last"] and ph["units"][steps[n]["u"]]["last_of_pair"]:
                evac(steps[n]["u"])

    def attend_pool(pool, ph, tables=None):
        steps, n0 = ph["steps"], ph["n0"]
        if tables:
            tables(0)
        for m, st in enumerate(steps):
            if tables and ph["groups"][st["g"]]["first"] == m:
                tables(st["g"] + 1)
            pool.wait_ge(s["recd"], n0 + m + 1)
            k = (n0 + m) % 8
            p = ph["pb"][:, (n0 + m) % 4, 0:st["keys"]]
            if st["gate"] is None:
                ins = nc.gpsimd.tensor_scalar(p, p, rr[:, k:k + 1], None, ALU.mult)
            else:
                ins = nc.gpsimd.tensor_scalar(p, p, rr[:, k:k + 1], st["gate"], ALU.mult, ALU.mult)
            ins.then_inc(s["scaled"], 1)

    first, na, mla = phases

    def free_tab(eng, ph, g):
        if g >= 2:
            eng.wait_ge(s["scored"], ph["n0"] + ph["groups"][g - 1]["first"])

    def counter():
        return [0]

    def last_block(eng):
        return eng.value_load(isml[0:1, 32:33], min_val=2 * T // P - 1, max_val=NSLOT_BLOCKS - 1)

    block = nc.Block()
    with block, nc.allow_non_contiguous_dma(reason="gains of heads and outputs, a column each"):

        @block.sync
        def _(sp):
            def load(n, pieces, wait=None, sem_of=loaded):
                slot = place(n)[0]
                landed = sem_of[slot] if sem_of is loaded else moe_loaded[(n - AT_MOE) % RING]
                if n >= RING:
                    sem, value = wait or released(n - RING)
                    sp.wait_ge(sem, value)
                if len(pieces) == 1:
                    at, width, src = pieces[0]
                    k = src.shape[1] // 2
                    pieces = [(at, width, src[:, 0:k, :]), (at + k * width, width, src[:, k:, :])]
                for at, width, src in pieces:
                    k, cols = src.shape[1], src.shape[2]
                    if width == 288 and cols == 8:
                        dst = ring[:, slot, 0:k * width].rearrange("p (c n) -> p c n", c=k)[:, :, at:at + cols]
                    else:
                        dst = ring[:, slot, at:at + k * width].rearrange("p (c n) -> p c n", c=k)[:, :, 0:cols]
                    sp.dma_start(dst, src).then_inc(landed, 16)

            for t in range(NT):
                sp.dma_start(xres[:, t, :], w["x"][0, t * P:(t + 1) * P, :]).then_inc(s["x_in"], 16)
            sp.dma_start(const[:, :], w["consts"]).then_inc(s["const_in"], 16)
            for n, pieces in enumerate(blocks["first"]):
                load(n, pieces)

            def expert(b):
                return sp.value_load(isml[0:1, ds(8 + b, 1)] if not isinstance(b, int) else isml[0:1, 8 + b:9 + b],
                                     min_val=0, max_val=NE - 1)

            def expert_weights(k, name, e, wait):
                load(AT_MOE + k, [(0, 512 if name != "w_down" else 1024,
                                   w[name][0][ds(e, 1), :, :].rearrange("o (c p) f -> p (o c) f", p=P))],
                     wait=wait, sem_of=moe_loaded)

            sp.wait_ge(s["routed"], 1)
            last = last_block(sp)
            e0 = expert(0)
            expert_weights(0, "w_gate", e0, released(AT_MOE - 3))
            expert_weights(1, "w_up", e0, released(AT_MOE - 2))
            e1 = expert(1)
            expert_weights(2, "w_gate", e1, released(AT_MOE - 1))
            expert_weights(3, "w_up", e1, (s["gu_psum"], 1))
            expert_weights(4, "w_down", e0, (s["gu_psum"], 2))
            with sp.Fori(2, last + 1) as b:
                e = expert(b)
                expert_weights(5, "w_gate", e, (s["gu_psum"], 2 * b - 1))
                expert_weights(6, "w_up", e, (s["gu_psum"], 2 * b))
                before = expert(b - 1)
                expert_weights(7, "w_down", before, (s["y_psum"], 2 * b - 2))
            expert_weights(5, "w_down", expert(last), (s["gu_psum"], 2 * last + 1))

            def ffn_half(g, name):
                gu, down, first_chunk = w[name + "_w_gu_2"][0], w[name + "_w_down_2"][0], HALF * (g % 2)

                def unit(v, sources, i=0):
                    u = UNITS * g + v
                    if v >= 3 or g:
                        sp.wait_ge(s["split_lo"], i + max(1, u + 1 - RAW))
                    for at, src in sources:
                        k, cols = src.shape[1], src.shape[2]
                        sp.dma_start(raw[:, u % RAW, at:at + k * cols].rearrange("p (c n) -> p c n", c=k), src)\
                            .then_inc(raw_in[u % RAW], 16)

                def gate_up_unit(v, i=0):
                    unit(v, [(1024 * k, gu[:, ds(i * P + ((first_chunk + v) * P + k * F), P)].rearrange("(c p) n -> p c n", p=P))
                             for k in range(2)], i)

                for v in range(3):
                    gate_up_unit(v)
                with sp.Fori(0, 2) as i:
                    for q in range(4):
                        gate_up_unit(3 + q, 4 * i)
                for j in range(0, HALF, 2):
                    rows = down[(first_chunk + j) * P:(first_chunk + min(j + 2, HALF)) * P, :].rearrange("(c p) n -> p c n", p=P)
                    unit(HALF + j // 2, [(512 * rows.shape[1] * k, rows[:, :, 512 * k:512 * k + 512]) for k in range(2)])

            ffn_half(0, "ffn1")
            ffn_half(1, "ffn1")
            for k, pieces in enumerate(blocks["mid"]):
                load(AT_MID + k, pieces, wait=(s["fd_psum"], 16) if k < RING else None)
            sp.wait_ge(s["nrm_psum"], 2)
            ffn_half(2, "ffn2")
            ffn_half(3, "ffn2")
            for t in range(NT):
                sp.wait_ge(s["res_ready"], 4 * 4 + t + 1)
                sp.dma_start(out[0, t * P:(t + 1) * P, :], xres[:, t, :]).then_inc(s["out_dma"], 16)
            sp.wait_ge(s["out_dma"], 16 * NT)

        @block.gpsimd
        def _(pool):
            steps_done = counter()

            def chained(ins):
                steps_done[0] += 1
                ins.then_inc(s["pool_step"], 1)
                pool.wait_ge(s["pool_step"], steps_done[0])

            gains = ["norm_mix_g", "norm_ffn_g", "ffn1_pre_g_2", "ffn1_post_g_2", "mix_pre_g_2", "mix_post_g_2",
                     "ffn2_pre_g_2", "ffn2_post_g_2"]

            def load_gain(k):
                if k >= 2:
                    pool.wait_ge(s["gain_used"], k - 1)
                pool.dma_start(gain[:, k % 2, :], w[gains[k]].partition_broadcast(P)[:, 0, :])\
                    .then_inc(s[f"gain_in{k % 2}"], 16)

            load_gain(0)
            load_gain(1)
            for k, name in enumerate(("fox_q_g", "fox_k_g", "nsa_q_g", "nsa_k_g")):
                for a in (0, 64):
                    pool.dma_start(gcol[a:a + 64, k:k + 1], w[name].rearrange("a d -> d a")).then_inc(s["head_gain_in"], 16)
            for k, name in enumerate(("cmp_k_pos", "cmp_v_pos")):
                pool.dma_start(sq[16 * k:16 * k + 16, 0, 0:P], w[name][0].rearrange("(c two) d -> c (two d)", two=2))\
                    .then_inc(s["pos_in"], 16)
            pool.dma_start(forget, w["b_forget"].partition_broadcast(P)[:, 0, :]).then_inc(s["misc_in"], 16)
            pool.dma_start(small[:, 526:526 + 4], w["b_group"].partition_broadcast(P)[:, 0, :]).then_inc(s["misc_in"], 16)
            pool.dma_start(small[:, 530:530 + 16], w["b_router"].partition_broadcast(P)[:, 0, :]).then_inc(s["misc_in"], 16)
            for k, name in enumerate(("cmp_k_w2", "cmp_v_w2")):
                pool.dma_start(cmp_w2[:, k, :, :], w[name][0].rearrange("(c p) d -> p c d", p=P)).then_inc(s["misc_in"], 16)
            pool.dma_start(small[:, 600:856], w["mla_q_norm_g_2"].partition_broadcast(P)[:, 0, :]).then_inc(s["misc_in"], 16)
            pool.dma_start(small[:, 856:984], w["mla_kv_norm_g_2"].partition_broadcast(P)[:, 0, :]).then_inc(s["misc_in"], 16)
            for k, name in enumerate(("na_out_norm_g_2", "mla_out_norm_g_2")):
                pool.dma_start(small[:, 984 + 4 * k:988 + 4 * k], w[name].rearrange("a (c p) -> p (a c)", p=P))\
                    .then_inc(s["misc_in"], 16)
            pool.dma_start(w_route[:, :, 0:4], w["w_group"][0].rearrange("(c p) n -> p c n", p=P)).then_inc(s["route_in"], 16)
            pool.dma_start(w_route[:, :, 4:20], w["w_router"][0].rearrange("(c p) n -> p c n", p=P))\
                .then_inc(s["route_in"], 16)

            pool.wait_ge(s["pos_evac"], 1)
            for g, last in enumerate((4, 8, 16, 24)):
                pool.wait_ge(s["z_evac"], last)
                if g:
                    pool.wait_ge(s["sq_used"], g)
                if g < 3:
                    nc.gpsimd.tensor_tensor(sq, zs[g], zs[g], ALU.mult).then_inc(s["sq_done"], 1)
                else:
                    chained(nc.gpsimd.tensor_tensor(sq[:, :, 0:P], zc[:, :, 256:384], zc[:, :, 256:384], ALU.mult))
                    nc.gpsimd.tensor_tensor(sq[:, :, P:2 * P], zd[:, :, 0:P], zd[:, :, 0:P], ALU.mult)\
                        .then_inc(s["sq_done"], 1)

            pool.wait_ge(s["cmp2_psum"], 1)
            nc.gpsimd.memset(zeros, 0.0).then_inc(s["zero_ready"], 1)
            pool.wait_ge(s["zero_ready"], 1)
            for k in range(4):
                pool.dma_start(Xs.rearrange("(a p) (k n) -> k p a n", p=P, k=4)[k],
                               view(zeros, [[0, 24], [1, 256]])).then_inc(s["zero_out"], 16)
                pool.dma_start(Ys.rearrange("(a p) (k n) -> k p a n", p=P, k=4)[k],
                               view(zeros, [[0, NSLOT_BLOCKS], [1, 256]])).then_inc(s["zero_out"], 16)

            def alibi(g):
                if g < H or g >= 2 * H:
                    return
                h = g - H
                free_tab(pool, first, g)
                slope = 2.0 ** (-(h + 1))
                chained(nc.gpsimd.tensor_scalar(tab[:, g % 2, 0:T], dist, slope, None, ALU.mult))
                nc.gpsimd.tensor_scalar(tab[:, g % 2, T:T + NT * NCMP], c_("cmp_dist"), slope, None, ALU.mult)\
                    .then_inc(s["nsa_tab"], 1)

            attend_pool(pool, first, alibi)

            pool.wait_ge(s["routed"], 1)
            pool.wait_ge(s["zero_out"], 128)
            for k in range(2):
                for t in range(NT):
                    pool.indirect_dma_start(Xs[:, :], bass.IndirectOffsetOnAxis(ap=isml[:, 4 * k + t:4 * k + t + 1], axis=0),
                                            hn[:, t, :], None).then_inc(s["scattered"], 16)
            pool.wait_ge(s["scattered"], 16 * 8)
            pool.dma_start(Xb, Xs[0:P, :]).then_inc(s["x_slot"], 16)
            pool.wait_ge(s["xtr_psum"], 2)
            pool.dma_start(Xb, Xs[P:2 * P, :]).then_inc(s["x_slot"], 16)
            last = last_block(pool)
            with pool.Fori(1, last + 1) as b:
                pool.wait_ge(s["xtr_psum"], 2 * b + 2)
                pool.dma_start(Xb, Xs[ds(P * b + P, P), :]).then_inc(s["x_slot"], 16)
                pool.wait_ge(s["yb_ready"], b)
                pool.dma_start(Ys[ds(P * b - P, P), :], Yb).then_inc(s["y_out"], 16)
            pool.wait_ge(s["yb_ready"], last + 1)
            pool.dma_start(Ys[ds(P * last, P), :], Yb).then_inc(s["y_out"], 16)
            pool.wait_ge(s["y_stored"], 1)
            for t in range(NT):
                for k in range(2):
                    n = 2 * t + k
                    if n >= 4:
                        pool.wait_ge(s["res_ready" if k else "y_used"], (4 if k else 0) + t - 1)
                    pool.indirect_dma_start(Yg[:, n % 4, :], None, Ys[:, :], bass.IndirectOffsetOnAxis(
                        ap=isml[:, 4 * k + t:4 * k + t + 1], axis=0)).then_inc(s[f"y_back{n % 4}"], 16)

            for k in range(2, 5):
                load_gain(k)
            pool.wait_ge(s["fd_psum"], 16)
            nc.gpsimd.memset(rpbs[0:120, :], 0.0).then_inc(s["rpb_zero"], 1)
            pool.wait_ge(s["rpb_zero"], 1)
            pool.dma_start(rpbs[0:120, 16:47], w["na_rpb_2"][0].rearrange("h a b -> (h a) b")).then_inc(s["rpb_in"], 16)
            pool.wait_ge(s["rpb_in"], 16)
            pool.dma_start(Rp, rpbs[0:120, :]).then_inc(s["rpb_out"], 16)
            pool.wait_ge(s["rpb_out"], 16)
            for h in range(H):
                for r in range(8):
                    src = bass.AP(tensor=Rp.tensor, offset=Rp.offset + 64 * (15 * h + r), ap=[[1, 16], [64, 8], [1, 48]])
                    pool.dma_start(xrev[16 * r:16 * r + 16, h, :].rearrange("p (j u) -> p j u", j=8), src)\
                        .then_inc(s["xrev_in"], 16)
            load_gain(5)
            pool.wait_ge(s["z2_evac"], 12)
            for b, band in enumerate((0, 8, 24, 32)):
                for r in range(8):
                    pool.dma_start(Vband[32 * (r % 4):32 * (r % 4) + 32, b, 512 * (r // 4):512 * (r // 4) + 512],
                                   v2[64 * (r % 2) + band:64 * (r % 2) + band + 32, r // 2, :]).then_inc(s["band_in"], 16)
            attend_pool(pool, na)
            nc.gpsimd.memset(zero_tab, 0.0).then_inc(s["mla_tab"], 1)
            attend_pool(pool, mla)
            load_gain(6)
            load_gain(7)

        @block.tensor
        def _(pe):
            def to_features(k, ready=None):
                for t in range(NT):
                    pe.wait_ge(s["hn_ready"], 4 * k + t + 1)
                    for half_ in range(2):
                        for c in range(4):
                            mm = nc.tensor.transpose(ps[2 * t + half_][:, P * c:P * c + P],
                                                     hn[:, t, P * (4 * half_ + c):P * (4 * half_ + c) + P], ident)
                        mm.then_inc(s["ht_psum"], 1)

            pe.wait_ge(s["const_in"], 16)
            pe.wait_ge(s["pos_in"], 32)
            nc.tensor.transpose(ps[7][:, 0:32], sq[0:32, 0, 0:P], ident[0:32, 0:32]).then_inc(s["pos_psum"], 1)
            pe.wait_ge(s["pos_evac"], 1)
            to_features(0)
            pe.wait_ge(s["ht_ready"], 8)

            def project(n, sem, cols, job):
                arrived(pe, n)
                wv = slot_view(n, 8, cols)
                for t in range(NT):
                    j = job + t
                    if j >= 4:
                        pe.wait_ge(s["z_evac"], j - 3)
                    for c in range(KD):
                        mm = nc.tensor.matmul(ps[j % 4][:, 0:cols], hT[:, c, P * t:P * t + P], wv[:, c, :],
                                              start=c == 0, stop=c == KD - 1)
                    mm.then_inc(sem, 1)

            def heads_to_features(g, src):
                if g < 4:
                    pe.wait_ge(s["head_ready"], g + 1)
                for p_ in range(4 if g < 4 else 2):
                    if g:
                        pe.wait_ge(s["tr_evac"], 4 * (g - 1) + p_ + 1)
                    for t in range(NT):
                        mm = nc.tensor.transpose(ps[4 + p_][:, P * t:P * t + P], src[:, t, P * p_:P * p_ + P], ident)
                    mm.then_inc(s["tr_psum"], 1)

            project(0, s["z_psum"], 512, 0)
            project(1, s["z_psum"], 512, 4)
            heads_to_features(0, zs[0])
            project(2, s["z_psum"], 512, 8)
            heads_to_features(1, zs[1])
            project(3, s["z_psum"], 512, 12)
            project(4, s["z_psum"], 512, 16)
            heads_to_features(2, zs[2])
            project(5, s["z_psum"], 288, 20)
            heads_to_features(3, zk)
            heads_to_features(4, zc)

            pe.wait_ge(s["k2_ready"], 8)
            pe.wait_ge(s["z_evac"], 24)
            for kv in range(2):
                arrived(pe, 6 + kv)
                w1 = slot_view(6 + kv, 16, 256)
                for hc in range(2):
                    k = 2 * kv + hc
                    for c in range(16):
                        nc.tensor.matmul(ps[6][:, k:k + 1], w1[:, c, P * hc:P * hc + P],
                                         posT[:, 16 * kv + c:16 * kv + c + 1], start=c == 0, stop=c == 15)
                    for c in range(16):
                        mm = nc.tensor.matmul(ps[k][:, 0:62], w1[:, c, P * hc:P * hc + P],
                                              view(K2[:, 2 * kv, :], [[T, 2], [16, NCMP]], 2 * c), start=c == 0, stop=c == 15)
                    mm.then_inc(s["cmp_psum"], 1)
            pe.wait_ge(s["lf_ready"], 1)
            for j in range(NT):
                mm = nc.tensor.matmul(ps[4][0:8, :], lf[:, 8 * j:8 * j + 8], upper[:, 384 - P * j:896 - P * j],
                                      start=j == 0, stop=j == NT - 1)
            mm.then_inc(s["cum_psum"], 1)
            pe.wait_ge(s["gelu_done"], 4)
            pe.wait_ge(s["misc_in"], 16 * 9)
            for kv in range(2):
                for g in range(2):
                    for hc in range(2):
                        mm = nc.tensor.matmul(ps[7][0:NCMP, 128 * kv + 64 * g:128 * kv + 64 * g + 64],
                                              hidc[:, kv, hc, NCMP * g:NCMP * g + NCMP], cmp_w2[:, kv, hc, :],
                                              start=hc == 0, stop=hc == 1)
            mm.then_inc(s["cmp2_psum"], 1)
            pe.wait_ge(s["kcn_ready"], 1)
            for g in range(2):
                mm = nc.tensor.transpose(ps[5][:, 32 * g:32 * g + NCMP], kcn[:, P * g:P * g + P], ident[0:NCMP, 0:NCMP])
            mm.then_inc(s["kcn_psum"], 1)
            pe.wait_ge(s["kct_ready"], 1)
            pe.wait_ge(s["gates_ready"], 1)
            pe.wait_ge(s["cum_ready"], 1)

            def fox_table(g):
                if g >= H:
                    return
                if g:
                    pe.wait_ge(s["fox_tab"], g)
                nc.tensor.matmul(ps[7], view(ident[0:8, :], [[0, P]], g), cumT[0:8, :], start=True, stop=True)\
                    .then_inc(s["tab_psum"], 1)

            attend_pe(pe, first, fox_table)

            pe.wait_ge(s["pt_ready"], len(first["steps"]))
            pe.wait_ge(s["o_evac"], 8)

            def mix_job(job, bank, lhs, wv, cols, kc):
                for c in range(kc):
                    mm = nc.tensor.matmul(ps[bank], lhs[:, c, :], wv[:, c, cols:cols + 512], start=c == 0, stop=c == kc - 1)
                mm.then_inc(s["mix_psum"], 1)

            for stage, (blocks_, lhs) in enumerate((((8, 9), hT), ((10,), OaT), ((11, 12), hT), ((13,), ObT))):
                for q in range(8):
                    hf, t = divmod(q, 4)
                    n = blocks_[min(hf, len(blocks_) - 1)]
                    if q in (0, 4):
                        arrived(pe, n)
                    kc = 8 if len(blocks_) == 2 else 4
                    wv = slot_view(n, kc, 512 if kc == 8 else 1024)
                    if stage:
                        sem, value = ((s["mix_sig"], 0), (s["mixed"], 0), (s["mix_sig"], 8))[stage - 1]
                        pe.wait_ge(sem, value + q + 1)
                    mix_job(q, q, lhs[:, :, P * t:P * t + P], wv, 512 * hf if kc == 4 else 0, kc)
            to_features(1)
            pe.wait_ge(s["ht_ready"], 16)
            for hf in range(2):
                arrived(pe, 14 + hf)
                wv = slot_view(14 + hf, 8, 512)
                for t in range(NT):
                    mix_job(0, 4 * hf + t, hT[:, :, P * t:P * t + P], wv, 0, 8)

            pe.wait_ge(s["res_ready"], 4)
            to_features(2)
            pe.wait_ge(s["ht_ready"], 24)
            pe.wait_ge(s["route_in"], 32)
            for t in range(NT):
                for c in range(KD):
                    mm = nc.tensor.matmul(ps[0][:, 20 * t:20 * t + 20], hT[:, c, P * t:P * t + P], w_route[:, c, :],
                                          start=c == 0, stop=c == KD - 1)
            mm.then_inc(s["route_psum"], 1)
            pe.wait_ge(s["chosen"], 1)
            for t in range(NT):
                for j in range(t + 1):
                    nc.tensor.matmul(ps[1][:, 16 * t:16 * t + 16], upper[:, 384 + P * (t - j):512 + P * (t - j)],
                                     rt[:, 16 * j:16 * j + 16], start=j == 0, stop=j == t)
            for j in range(NT):
                mm = nc.tensor.matmul(ps[2][:, 0:16], upper[:, 768:896], rt[:, 16 * j:16 * j + 16], start=j == 0, stop=j == NT - 1)
            mm.then_inc(s["route_psum"], 1)

            def slot_features(b):
                pe.wait_ge(s["x_slot"], 16 * b + 16)
                for h_ in range(2):
                    for c in range(4):
                        mm = nc.tensor.transpose(ps[2 + h_][:, P * c:P * c + P], Xb[:, P * (4 * h_ + c):P * (4 * h_ + c) + P], ident)
                    mm.then_inc(s["xtr_psum"], 1)

            def gate_up(k, i=0):
                for g in range(2):
                    moe_arrived(pe, k + g, i)
                    wv = slot_view(AT_MOE + k + g, 8, 512)
                    for c in range(KD):
                        mm = nc.tensor.matmul(ps[g], XT[:, c, :], wv[:, c, :], start=c == 0, stop=c == KD - 1)
                    mm.then_inc(s["gu_psum"], 1)

            def hidden_features(b):
                pe.wait_ge(s["hb_ready"], b + 1)
                for c in range(4):
                    mm = nc.tensor.transpose(ps[6][:, P * c:P * c + P], hb[:, P * c:P * c + P], ident)
                mm.then_inc(s["htr_psum"], 1)

            def down(k, i=0):
                moe_arrived(pe, k, i)
                wv = slot_view(AT_MOE + k, 4, 1024)
                for hf in range(2):
                    for c in range(4):
                        mm = nc.tensor.matmul(ps[4 + hf], HTs[:, c, :], wv[:, c, 512 * hf:512 * hf + 512], start=c == 0, stop=c == 3)
                    mm.then_inc(s["y_psum"], 1)

            pe.wait_ge(s["routed"], 1)
            slot_features(0)
            pe.wait_ge(s["xt_ready"], 2)
            gate_up(0)
            slot_features(1)
            hidden_features(0)

            def gate_up_and_down(b):
                pe.wait_ge(s["xt_ready"], 2 * b + 2)
                gate_up(2, b - 1)
                slot_features(b + 1)
                pe.wait_ge(s["hts_ready"], b)
                if not (isinstance(b, int) and b == 1):
                    pe.wait_ge(s["yb_ready"], b - 1)
                down(4, b - 1)
                hidden_features(b)

            gate_up_and_down(1)
            last = last_block(pe)
            with pe.Fori(2, last + 1) as b:
                gate_up_and_down(b)
            pe.wait_ge(s["hts_ready"], last + 1)
            pe.wait_ge(s["yb_ready"], last)
            down(2, last)
            pe.wait_ge(s["yb_ready"], last + 1)
            pe.wait_ge(s["xt_ready"], 2 * last + 4)

            def ffn_half(g):
                base = HALF * g
                evac = 24 * (g // 2) + 8 * (g % 2)

                def gate_up_unit(v, i=0):
                    u = UNITS * g + v
                    pe.wait_ge(s["split_lo"], i + (u + 1))
                    if v >= 2:
                        pe.wait_ge(s["ff_hid"], i + (base + v - 1))
                    elif g % 2:
                        pe.wait_ge(s["f_evac"], evac - 8 + 2 * v + 2)
                    for k in range(2):
                        for c in range(KD):
                            col = 1024 * k + P * c
                            mm = products(ps[2 * (v % 2) + k], w_hi[:, u % 2, col:col + P], w_lo[:, u % 2, col:col + P],
                                          hT_hi[:, c, :], hT_lo[:, c, :], c == 0, c == KD - 1)
                    mm.then_inc(s["unit_done"], 1)

                for v in range(3):
                    gate_up_unit(v)
                with pe.Fori(0, 2) as i:
                    for q in range(4):
                        gate_up_unit(3 + q, 4 * i)
                for j in range(0, HALF, 2):
                    v = HALF + j // 2
                    u = UNITS * g + v
                    n = min(2, HALF - j)
                    pe.wait_ge(s["split_lo"], u + 1)
                    if j == 0 and g % 2:
                        pe.wait_ge(s["f_evac"], evac)
                    if j > 0:
                        pe.wait_ge(s["ff_hid"], base + HALF)
                    else:
                        pe.wait_ge(s["ff_hid"], base + HALF - 1)
                    for m in (4, 5, 6, 7, 0, 1, 2, 3) if j == 0 else range(8):
                        t, hf = divmod(m, 2)
                        if j == 0 and m == 0:
                            pe.wait_ge(s["ff_hid"], base + HALF)
                        for c in range(j, j + n):
                            col = 512 * (n * hf + c - j)
                            mm = products(ps[m], hid_hi[:, c, P * t:P * t + P], hid_lo[:, c, P * t:P * t + P],
                                          w_hi[:, u % 2, col:col + 512], w_lo[:, u % 2, col:col + 512],
                                          c == 0, c == HALF - 1)
                        if j + n == HALF:
                            mm.then_inc(s["fd_psum"], 1)
                    if j + n < HALF:
                        mm.then_inc(s["unit_done"], 1)

            to_features(3)
            pe.wait_ge(s["hT_low_ready"], 8)
            ffn_half(0)
            ffn_half(1)
            pe.wait_ge(s["f_evac"], 16)

            to_features(4)
            pe.wait_ge(s["ht_ready"], 40)
            for q in range(16):
                n = AT_MID + q // 4
                if q % 4 == 0:
                    arrived(pe, n)
                cols = 512 if q < 12 else 416
                wv = slot_view(n, 8, cols)
                if q >= 8:
                    pe.wait_ge(s["z2_evac"], q - 7)
                r = q % 4
                for c in range(KD):
                    if q < 8:
                        mm = nc.tensor.matmul(ps[q % 8], wv[:, c, P * r:P * r + P], hT[:, c, :], start=c == 0, stop=c == KD - 1)
                    else:
                        mm = nc.tensor.matmul(ps[q % 8][:, 0:cols], hT[:, c, P * r:P * r + P], wv[:, c, :],
                                              start=c == 0, stop=c == KD - 1)
                mm.then_inc(s["z2_psum"], 1)
            pe.wait_ge(s["z2_evac"], 16)

            def na_table(g):
                if g >= H:
                    return
                if g == 0:
                    pe.wait_ge(s["xrev_in"], 16 * 8 * H)
                if g:
                    pe.wait_ge(s["na_tab"], g)
                nc.tensor.matmul(ps[7][:, 0:384], flip, xrev[:, g, :], start=True, stop=True).then_inc(s["tab_psum"], 1)

            pe.wait_ge(s["band_in"], 16 * 32)
            attend_pe(pe, na, na_table)

            def norm_sums(k, sq_):
                pe.wait_ge(s["o_sq"], 4 * k + 4)
                for t in range(NT):
                    for c in range(4):
                        mm = nc.tensor.matmul(ps[7][:, 4 * k + t:4 * k + t + 1], sq_[:, c, P * t:P * t + P], one_col,
                                              start=c == 0, stop=c == 3)
                mm.then_inc(s["nrm_psum"], 1)

            norm_sums(0, sq_na)
            pe.wait_ge(s["cn_ready"], 1)
            pe.wait_ge(s["pt_ready"], mla["n0"])
            for c in range(3):
                for t in range(NT):
                    mm = nc.tensor.transpose(ps[c][:, P * t:P * t + P], z3[:, t, P * c:P * c + P], ident)
                mm.then_inc(s["cn_psum"], 1)
            pe.wait_ge(s["ct_ready"], 3)
            pe.wait_ge(s["o_evac"], 12)
            n = AT_MID + 4
            arrived(pe, n)
            uq, ukv = slot_view(n, 2, 768), slot_view(n, 1, 1024, 1536)
            for t in range(NT):
                for q in range(4):
                    j = 4 * t + q
                    if j >= 4:
                        pe.wait_ge(s["mla_evac"], j - 3)
                    bank = ps[3 + q]
                    if q < 2:
                        for c in range(2):
                            mm = nc.tensor.matmul(bank[:, 0:384], cT[:, c, P * t:P * t + P], uq[:, c, 384 * q:384 * q + 384],
                                                  start=c == 0, stop=c == 1)
                    else:
                        mm = nc.tensor.matmul(bank, cT[:, 2, P * t:P * t + P], ukv[:, 0, 512 * (q - 2):512 * (q - 1)],
                                              start=True, stop=True)
                    mm.then_inc(s["mla_psum"], 1)
            pe.wait_ge(s["roped"], 2)
            for j in range(16):
                src, h = (qz, j) if j < 8 else (kf, j - 8)
                if j >= 3:
                    pe.wait_ge(s["mt_dve" if (j - 3) % 2 else "mt_act"], (j - 3) // 2 + 1)
                for t in range(NT):
                    mm = nc.tensor.transpose(ps[j % 3][0:96, P * t:P * t + P], src[:, t, 96 * h:96 * h + 96], ident)
                mm.then_inc(s["mt_psum"], 1)
            pe.wait_ge(s["mt_act"], 8)
            pe.wait_ge(s["mt_dve"], 8)
            pe.wait_ge(s["mla_evac"], 16)
            attend_pe(pe, mla)
            norm_sums(1, sq_mla)
            pe.wait_ge(s["pt_ready"], mla["n0"] + len(mla["steps"]))
            pe.wait_ge(s["o_evac"], 16)
            for hf in range(2):
                arrived(pe, AT_MID + 5 + hf)
                wv = slot_view(AT_MID + 5 + hf, 8, 512)
                for t in range(NT):
                    for k in range(2):
                        j = 8 * hf + 2 * t + k
                        bank = j % 6
                        if j >= 6:
                            pe.wait_ge(s["f_evac"], 16 + (j - 6) // 2 + 1)
                        for c in range(4):
                            mm = nc.tensor.matmul(ps[bank], hT[:, 4 * k + c, P * t:P * t + P], wv[:, 4 * k + c, :],
                                                  start=c == 0, stop=c == 3)
                        mm.then_inc(s["o2_psum"], 1)
            pe.wait_ge(s["f_evac"], 24)
            to_features(5)
            pe.wait_ge(s["hT_low_ready"], 16)
            ffn_half(2)
            ffn_half(3)

        @block.scalar
        def _(act):
            steps_done, roots = counter(), counter()

            def chained(ins):
                steps_done[0] += 1
                ins.then_inc(s["act_step"], 1)
                act.wait_ge(s["act_step"], steps_done[0])

            def root(ap):
                roots[0] += 1
                act.wait_ge(s["var_ready"], roots[0])
                nc.scalar.activation(ap, ap, ACT.Sqrt).then_inc(s["root_ready"], 1)

            def norm_squares(k):
                for t in range(NT):
                    if k == 0:
                        act.wait_ge(s["x_in"], 16 * NT)
                    else:
                        act.wait_ge(s["res_ready"], 4 * (k - 1) + t + 1)
                    nc.scalar.activation(hn[:, t, :], xres[:, t, :], ACT.Square, accum_out=ss[:, t:t + 1])\
                        .then_inc(s["sumsq"], 1)
                root(rstd[:, 0:NT])

            def to_hT(k, dst=hT):
                for m in range(8):
                    act.wait_ge(s["ht_psum"], 8 * k + m + 1)
                    t, h_ = divmod(m, 2)
                    nc.scalar.activation(dst[:, 4 * h_:4 * h_ + 4, P * t:P * t + P],
                                         ps[m].rearrange("p (c q) -> p c q", c=4), ACT.Copy).then_inc(s["ht_ready"], 1)

            def post_squares(evacuated):
                for t in range(NT):
                    act.wait_ge(s["f_evac"], evacuated(t))
                    nc.scalar.activation(arena[:, t * D:t * D + D], hn[:, t, :], ACT.Square, accum_out=ss[:, t:t + 1])\
                        .then_inc(s["sumsq"], 1)
                root(rstd[:, 0:NT])

            act.wait_ge(s["pos_evac"], 1)
            norm_squares(0)
            to_hT(0)

            def z_copy(blk, dst, cols):
                for t in range(NT):
                    j = 4 * blk + t
                    act.wait_ge(s["z_psum"], j + 1)
                    nc.scalar.activation(dst[:, t, :], ps[j % 4][:, 0:cols], ACT.Copy).then_inc(s["z_evac"], 1)

            z_copy(0, zs[0], 512)
            z_copy(1, zs[1], 512)
            root(rstd[:, 0:32])
            z_copy(2, vf, 512)
            root(rstd[:, 0:32])
            z_copy(3, zs[2], 512)
            z_copy(4, zc, 512)
            root(rstd[:, 0:32])
            z_copy(5, zd, 288)
            root(rstd[:, 0:16])
            act.wait_ge(s["fox_u"], 1)
            chained(nc.scalar.activation(lf, lf, ACT.Exp))
            nc.scalar.activation(lf, lf, ACT.Ln, bias=one_col).then_inc(s["fox_l"], 1)
            act.wait_ge(s["z_evac"], 24)
            nc.scalar.activation(gates.rearrange("p (t n) -> p t n", t=NT), zd[:, :, 256:280], ACT.Sigmoid)\
                .then_inc(s["gate_raw"], 1)
            act.wait_ge(s["pos_bias_ready"], 1)
            for kv in range(2):
                for hc in range(2):
                    k = 2 * kv + hc
                    act.wait_ge(s["cmp_psum"], k + 1)
                    nc.scalar.activation(hidc[:, kv, hc, :], ps[k][:, 0:62], ACT.Gelu_apprx_tanh,
                                         bias=pos_bias[:, k:k + 1]).then_inc(s["gelu_done"], 1)
            root(rstd[0:NCMP, 0:2])

            def fox_table(g):
                if g >= H:
                    return
                free_tab(act, first, g)
                act.wait_ge(s["tab_psum"], g + 1)
                nc.scalar.activation(tab[:, g % 2, 0:T], ps[7], ACT.Copy).then_inc(s["fox_tab"], 1)

            attend_act(act, first, tables=fox_table)

            for stage in range(2):
                for q in range(8):
                    hf, t = divmod(q, 4)
                    act.wait_ge(s["mix_psum"], 16 * stage + q + 1)
                    if stage:
                        act.wait_ge(s["mixed"], q + 1)
                    nc.scalar.activation(gate_sig[:, t, 512 * hf:512 * hf + 512], ps[q], ACT.Sigmoid)\
                        .then_inc(s["mix_sig"], 1)
            to_hT(1)
            norm_squares(1)
            to_hT(2)
            act.wait_ge(s["exp_in"], 1)
            nc.scalar.activation(rt[:, 1024:1044], rt[:, 1024:1044], ACT.Exp).then_inc(s["exp_out"], 1)

            def slot_copy(b):
                for h_ in range(2):
                    act.wait_ge(s["xtr_psum"], 2 * b + (h_ + 1))
                    nc.scalar.activation(XT[:, 4 * h_:4 * h_ + 4, :], ps[2 + h_].rearrange("p (c q) -> p c q", c=4),
                                         ACT.Copy).then_inc(s["xt_ready"], 1)

            def expert_block(b):
                act.wait_ge(s["gu_psum"], 2 * b + 1)
                if not (isinstance(b, int) and b == 0):
                    act.wait_ge(s["hb_ready"], b)
                nc.scalar.activation(sg, ps[0], ACT.Silu).then_inc(s["silu_done"], 1)
                slot_copy(b + 1)
                act.wait_ge(s["htr_psum"], b + 1)
                nc.scalar.activation(HTs, ps[6].rearrange("p (c q) -> p c q", c=4), ACT.Copy).then_inc(s["hts_ready"], 1)

            act.wait_ge(s["routed"], 1)
            slot_copy(0)
            expert_block(0)
            last = last_block(act)
            with act.Fori(1, last + 1) as b:
                expert_block(b)
            act.wait_ge(s["yb_ready"], last + 1)
            split_high(0, 0)
            norm_squares(2)
            split_high(0, 1)
            to_hT(3, hT_hi)

            def ffn_half(g):
                base = HALF * g

                def chunk(v, i=0):
                    act.wait_ge(s["unit_done"], i + ((UNITS - 1) * g + v + 1))
                    if v >= 2:
                        act.wait_ge(s["ff_hid"], i + (base + v - 1))
                    nc.scalar.activation(sgb[:, v % 2, :], ps[2 * (v % 2)], ACT.Silu).then_inc(s["ff_silu"], 1)
                    split_high(g, v + 2, i)
                    act.wait_ge(s["gated"], i + (base + v + 1))
                    at = hid_hi[:, v, :] if isinstance(i, int) else hid_hi[:, ds(i + v, 1), :].rearrange("p a q -> p (a q)")
                    nc.scalar.activation(at, sgb[:, v % 2, :], ACT.Copy).then_inc(s["hid_high"], 1)

                for v in range(3):
                    chunk(v)
                with act.Fori(0, 2) as i:
                    for q in range(4):
                        chunk(3 + q, 4 * i)
                for v in range(HALF + 2, UNITS):
                    split_high(g, v)
                if g % 2 == 0:
                    split_high(g + 1, 0)
                    for m in range(8):
                        t, hf = divmod(m, 2)
                        act.wait_ge(s["fd_psum"], 8 * g + m + 1)
                        nc.scalar.activation(hn[:, t, 512 * hf:512 * hf + 512], ps[m], ACT.Copy).then_inc(s["f_evac"], 1)
                    split_high(g + 1, 1)

            ffn_half(0)
            ffn_half(1)
            post_squares(lambda t: 8 + 2 * t + 2)
            norm_squares(3)
            to_hT(4)
            for q in range(16):
                act.wait_ge(s["z2_psum"], q + 1)
                r = q % 4
                dst = (qT2, kT2, v2, z3)[q // 4][:, r, :]
                src = ps[q % 8][:, 0:dst.shape[1]]
                if q < 4:
                    dst = dst.rearrange("p (b r c) -> p r b c", b=4, r=8)
                    src = src.rearrange("p (r b c) -> p r b c", r=8, b=4)
                nc.scalar.activation(dst, src, ACT.Copy, scale=0.125 if q < 4 else 1.0)\
                    .then_inc(s["z2_evac"], 1)

            def squares(ph, dst):
                def evac(u):
                    unit = ph["units"][u]
                    bank = ps[5 + (ph["p0"] + unit["pair"]) % 2]
                    act.wait_ge(s["pv_psum"], ph["u0"] + u + 1)
                    o, i = dst[:, unit["pair"], :], bank
                    if ph is na:
                        o = o.rearrange("p (r b c) -> p b r c", r=8, b=4)
                        i = i.rearrange("p (b r c) -> p b r c", b=4, r=8)
                    nc.scalar.activation(o, i, ACT.Square).then_inc(s["o_sq"], 1)
                return evac

            root(rstd[:, 16:24])
            attend_act(act, na, squares(na, sq_na))
            root(rstd[:, 24:28])
            for c in range(3):
                act.wait_ge(s["cn_psum"], c + 1)
                nc.scalar.activation(cT[:, c, :], ps[c], ACT.Copy).then_inc(s["ct_ready"], 1)
            for t in range(NT):
                for q in range(4):
                    act.wait_ge(s["mla_psum"], 4 * t + q + 1)
                    if q < 2:
                        nc.scalar.activation(qz[:, t, 384 * q:384 * q + 384], ps[3 + q][:, 0:384], ACT.Copy,
                                             scale=float(96 ** -0.5)).then_inc(s["mla_evac"], 1)
                    else:
                        kv = ps[3 + q].rearrange("p (h n) -> p h n", h=4)
                        h = 4 * (q - 2)
                        nc.scalar.activation(kf[:, t, :].rearrange("p (h n) -> p h n", h=H)[:, h:h + 4, 0:64],
                                             kv[:, :, 0:64], ACT.Copy)
                        nc.scalar.activation(vm[:, t, :].rearrange("p (h n) -> p h n", h=H)[:, h:h + 4, :],
                                             kv[:, :, 64:128], ACT.Copy).then_inc(s["mla_evac"], 1)
            for j in range(0, 16, 2):
                act.wait_ge(s["mt_psum"], j + 1)
                dst = qTm if j < 8 else kTm
                nc.scalar.activation(dst[0:96, j % 8, :], ps[j % 3][0:96], ACT.Copy).then_inc(s["mt_act"], 1)
            attend_act(act, mla, squares(mla, sq_mla))
            root(rstd[:, 28:32])
            post_squares(lambda t: 16 + 4 + t + 1)
            split_high(2, 0)
            norm_squares(4)
            split_high(2, 1)
            to_hT(5, hT_hi)
            ffn_half(2)
            ffn_half(3)
            post_squares(lambda t: 32 + 2 * t + 2)

        @block.vector
        def _(dve):
            steps_done, roots, gains_used, norms = counter(), counter(), counter(), counter()
            V = nc.vector

            def chained(ins):
                steps_done[0] += 1
                ins.then_inc(s["dve_step"], 1)
                dve.wait_ge(s["dve_step"], steps_done[0])

            def variance(dst, src, n):
                return V.tensor_scalar(dst, src, 1.0 / n, 1e-6, ALU.mult, ALU.add)

            def inverse_root(ap):
                roots[0] += 1
                dve.wait_ge(s["root_ready"], roots[0])
                chained(V.reciprocal(ap, ap))

            def row_rstd():
                norms[0] += 1
                dve.wait_ge(s["sumsq"], 4 * norms[0])
                variance(rstd[:, 0:NT], ss[:, 0:NT], D).then_inc(s["var_ready"], 1)
                inverse_root(rstd[:, 0:NT])

            def norm_rows():
                row_rstd()
                k = gains_used[0]
                dve.wait_ge(s[f"gain_in{k % 2}"], 16 * (k // 2 + 1))
                for t in range(NT):
                    V.scalar_tensor_tensor(out=hn[:, t, :], in0=xres[:, t, :], scalar=rstd[:, t:t + 1], in1=gain[:, k % 2, :],
                                           op0=ALU.mult, op1=ALU.mult).then_inc(s["hn_ready"], 1)
                gains_used[0] += 1

            def free_gain(value):
                dve.wait_ge(s["hn_ready"], value)
                V.memset(nmax[:, 0:1], 0.0).then_inc(s["gain_used"], 1)

            def post_norm(factor):
                row_rstd()
                k = gains_used[0]
                dve.wait_ge(s[f"gain_in{k % 2}"], 16 * (k // 2 + 1))
                for t in range(NT):
                    chained(V.scalar_tensor_tensor(out=hn[:, t, :], in0=hn[:, t, :], scalar=rstd[:, t:t + 1],
                                                   in1=gain[:, k % 2, :], op0=ALU.mult, op1=ALU.mult))
                    V.scalar_tensor_tensor(out=xres[:, t, :], in0=hn[:, t, :], scalar=factor, in1=xres[:, t, :],
                                           op0=ALU.mult, op1=ALU.add).then_inc(s["res_ready"], 1)
                gains_used[0] += 1
                V.memset(nmax[:, 0:1], 0.0).then_inc(s["gain_used"], 1)

            dve.wait_ge(s["pos_psum"], 1)
            V.tensor_copy(posT, ps[7][:, 0:32]).then_inc(s["pos_evac"], 1)
            norm_rows()
            free_gain(4)

            dve.wait_ge(s["head_gain_in"], 16 * 8)

            def head_norm(g):
                n = 32 if g < 3 else 16
                src = sq if g < 3 else sq[:, :, 0:256]
                dve.wait_ge(s["sq_done"], g + 1)
                ins = V.tensor_reduce(ss[:, 0:n].rearrange("p (t h) -> p t h", t=NT),
                                      src.rearrange("p t (h d) -> p t h d", d=DH), AX.X, ALU.add)
                ins.then_inc(s["sq_used"], 1)
                dve.wait_ge(s["sq_used"], g + 1)
                variance(rstd[:, 0:n], ss[:, 0:n], DH).then_inc(s["var_ready"], 1)
                inverse_root(rstd[:, 0:n])
                if g < 3:
                    z = zs[g].rearrange("p t (h d) -> p (t h) d", d=DH)
                    V.tensor_tensor(z, z, rstd[:, 0:32].unsqueeze(2).to_broadcast([P, 32, DH]), ALU.mult)\
                        .then_inc(s["head_ready"], 1)
                else:
                    out_ = zk.rearrange("p t (s two d) -> p t s two d", two=2, d=DH)
                    r = rstd[:, 0:16].rearrange("p (t s) -> p t s", t=NT)
                    for k in range(2):
                        src = (zc[:, :, 256:384], zd[:, :, 0:P])[k].rearrange("p t (g d) -> p t g d", d=DH)
                        for two in range(2):
                            ins = V.tensor_tensor(out_[:, :, 2 * k:2 * k + 2, two, :], src,
                                                  r[:, :, 2 * k:2 * k + 2].unsqueeze(3).to_broadcast([P, NT, 2, DH]), ALU.mult)
                    ins.then_inc(s["head_ready"], 1)

            def head_copy(g):
                dst, col, factor = ((qT, 0, 0.125), (kT, 1, 1.0), (nqT, 2, 0.125), (kkT, 3, 1.0))[g]
                for p_ in range(4):
                    dve.wait_ge(s["tr_psum"], 4 * g + p_ + 1)
                    V.tensor_scalar(dst[:, p_, :], ps[4 + p_], gcol[:, col:col + 1], factor, ALU.mult, ALU.mult)\
                        .then_inc(s["tr_evac"], 1)

            head_norm(0)
            head_copy(0)
            head_norm(1)
            head_copy(1)
            head_norm(2)
            head_copy(2)
            head_norm(3)
            head_copy(3)
            dve.wait_ge(s["misc_in"], 16 * 9)
            u = tmp32.rearrange("p (t h) -> p t h", t=NT)
            chained(V.tensor_tensor(u, zd[:, :, 280:288], view(forget, [[0, NT], [1, H]]), ALU.add))
            V.scalar_tensor_tensor(out=lf, in0=tmp32, scalar=-1.0, in1=tmp32, op0=ALU.mult, op1=ALU.min).then_inc(s["fox_u"], 1)
            for kv in range(2):
                dve.wait_ge(s["tr_psum"], 16 + kv + 1)
                for g in range(2):
                    V.tensor_copy(K2[0:64, 2 * kv + g, :], ps[4 + kv][64 * g:64 * g + 64, :]).then_inc(s["k2_ready"], 1)
                    V.tensor_copy(K2[64:128, 2 * kv + g, 0:T - 1], ps[4 + kv][64 * g:64 * g + 64, 1:T])\
                        .then_inc(s["k2_ready"], 1)
            dve.wait_ge(s["fox_l"], 1)
            V.scalar_tensor_tensor(out=lf, in0=tmp32, scalar=0.0, in1=lf, op0=ALU.min, op1=ALU.subtract)\
                .then_inc(s["lf_ready"], 1)
            dve.wait_ge(s["gate_raw"], 1)
            g0 = view(gates, [[3, H]])
            V.tensor_scalar(g0, g0, c_("cmp_valid"), None, ALU.mult).then_inc(s["gates_ready"], 1)
            dve.wait_ge(s["cmp_psum"], 4)
            V.tensor_copy(pos_bias, ps[6][:, 0:4]).then_inc(s["pos_bias_ready"], 1)
            dve.wait_ge(s["cum_psum"], 1)
            V.tensor_scalar(cumT[0:8, :], ps[4][0:8, :], -1.0, None, ALU.mult).then_inc(s["cum_ready"], 1)
            dve.wait_ge(s["cmp2_psum"], 1)
            V.tensor_copy(vcmp, ps[7][0:NCMP, P:2 * P])
            chained(V.tensor_copy(kcs, ps[7][0:NCMP, 0:P]))
            chained(V.tensor_tensor(kcs_sq, kcs, kcs, ALU.mult))
            chained(V.tensor_reduce(ss[0:NCMP, 0:2], kcs_sq.rearrange("p (g d) -> p g d", g=2), AX.X, ALU.add))
            variance(rstd[0:NCMP, 0:2], ss[0:NCMP, 0:2], DH).then_inc(s["var_ready"], 1)
            inverse_root(rstd[0:NCMP, 0:2])
            for two in range(2):
                ins = V.tensor_tensor(kcn.rearrange("p (g two d) -> p g two d", g=2, two=2)[:, :, two, :],
                                      kcs.rearrange("p (g d) -> p g d", g=2),
                                      rstd[0:NCMP, 0:2].unsqueeze(2).to_broadcast([NCMP, 2, DH]), ALU.mult)
            ins.then_inc(s["kcn_ready"], 1)
            dve.wait_ge(s["kcn_psum"], 1)
            V.tensor_scalar(kcT, ps[5][:, 0:64].rearrange("p (g n) -> p g n", g=2)[:, :, 0:NCMP], gcol[:, 3:4], None, ALU.mult)\
                .then_inc(s["kct_ready"], 1)

            def copy_out(ph, dst, gains_=None):
                def evac(u):
                    unit = ph["units"][u]
                    pair = unit["pair"]
                    bank = ps[5 + (ph["p0"] + pair) % 2]
                    dve.wait_ge(s["pv_psum"], ph["u0"] + u + 1)
                    if gains_ is None:
                        o = (OaT if pair < 4 else ObT)[:, pair % 4, :]
                        V.tensor_copy(o, bank).then_inc(s["o_evac"], 1)
                        return
                    dve.wait_ge(s["o_sq"], ph["p0"] - 8 + pair + 1)
                    o, i = dst[:, pair, :], bank
                    if ph is na:
                        o = o.rearrange("p (r b c) -> p b r c", r=8, b=4)
                        i = i.rearrange("p (b r c) -> p b r c", b=4, r=8)
                    V.tensor_scalar(o, i, small[:, gains_ + pair:gains_ + pair + 1], None, ALU.mult).then_inc(s["o_evac"], 1)
                return evac

            attend_dve(dve, first, copy_out(first, None))

            for q in range(8):
                hf, t = divmod(q, 4)
                dve.wait_ge(s["mix_psum"], 8 + q + 1)
                dve.wait_ge(s["mix_sig"], q + 1)
                V.tensor_tensor(hn[:, t, 512 * hf:512 * hf + 512], ps[q], gate_sig[:, t, 512 * hf:512 * hf + 512], ALU.mult)\
                    .then_inc(s["mixed"], 1)
            for q in range(8):
                hf, t = divmod(q, 4)
                dve.wait_ge(s["mix_psum"], 24 + q + 1)
                dve.wait_ge(s["mix_sig"], 8 + q + 1)
                chained(V.tensor_tensor(mixtmp[:, q % 2, :], ps[q], gate_sig[:, t, 512 * hf:512 * hf + 512], ALU.mult))
                V.tensor_tensor(hn[:, t, 512 * hf:512 * hf + 512], mixtmp[:, q % 2, :], hn[:, t, 512 * hf:512 * hf + 512],
                                ALU.add).then_inc(s["hn_ready" if hf else "mixed"], 1)
            for q in range(8):
                hf, t = divmod(q, 4)
                dve.wait_ge(s["mix_psum"], 32 + q + 1)
                x_ = xres[:, t, 512 * hf:512 * hf + 512]
                ins = V.tensor_tensor(x_, ps[q], x_, ALU.add)
                if hf:
                    ins.then_inc(s["res_ready"], 1)

            norm_rows()
            free_gain(12)
            dve.wait_ge(s["route_psum"], 1)
            R = NT

            def r3(at, n):
                return rt[:, at:at + R * n].rearrange("p (t n) -> p t n", t=R)

            logits, gl = r3(64, 20), None
            bias20 = small[:, 526:546]
            chained(V.tensor_tensor(logits, ps[0][:, 0:80].rearrange("p (t n) -> p t n", t=R), view(bias20, [[0, R], [1, 20]]), ALU.add))
            iota = view(c_("iota4"), [[0, R], [1, 4]])

            def bc(ap, n):
                return ap.unsqueeze(2).to_broadcast([P, R, n])

            def first_max(src, top, onehot, scratch, low):
                chained(V.tensor_reduce(top, src, AX.X, ALU.max))
                chained(V.tensor_tensor(scratch, src, bc(top, 4), ALU.is_equal))
                chained(V.tensor_tensor(scratch, scratch, iota, ALU.mult))
                chained(V.tensor_reduce(low, scratch, AX.X, ALU.min))
                chained(V.tensor_tensor(onehot, iota, bc(low, 4), ALU.is_equal))

            top_g, top1, top2, low = rt[:, 160:164], rt[:, 164:168], rt[:, 168:172], rt[:, 172:176]
            oh_g, oh1, oh2, scr = r3(176, 4), r3(192, 4), r3(208, 4), r3(224, 4)
            e_in = r3(240, 4)
            prod = rt[:, 256:320]
            first_max(logits[:, :, 0:4], top_g, oh_g, scr, low)
            lg = view(rt, [[20, R], [4, 4], [1, 4]], 68)
            chained(V.tensor_tensor(prod.rearrange("p (t g e) -> p t g e", t=R, g=4), lg,
                                    oh_g.unsqueeze(3).to_broadcast([P, R, 4, 4]), ALU.mult))
            chained(V.tensor_reduce(e_in, prod.rearrange("p (t g e) -> p t e g", t=R, g=4), AX.X, ALU.add))
            first_max(e_in, top1, oh1, scr, low)
            chained(V.scalar_tensor_tensor(out=e_in, in0=oh1, scalar=-3e38, in1=e_in, op0=ALU.mult, op1=ALU.add))
            first_max(e_in, top2, oh2, scr, low)
            M = [rt[:, 320:384], rt[:, 384:448]]
            for k, oh in enumerate((oh1, oh2)):
                chained(V.tensor_tensor(M[k].rearrange("p (t g e) -> p t g e", t=R, g=4),
                                        oh_g.unsqueeze(3).to_broadcast([P, R, 4, 4]),
                                        oh.unsqueeze(2).to_broadcast([P, R, 4, 4]), ALU.mult))
            V.tensor_tensor(rt[:, 0:64], M[0], M[1], ALU.add).then_inc(s["chosen"], 1)
            gd = rt[:, 1024:1040].rearrange("p (t n) -> p t n", t=R)
            chained(V.tensor_tensor(gd, logits[:, :, 0:4], bc(top_g, 4), ALU.subtract))
            V.tensor_tensor(rt[:, 1040:1044], top2, top1, ALU.subtract).then_inc(s["exp_in"], 1)
            dve.wait_ge(s["exp_out"], 1)
            den, wts = rt[:, 1044:1048], rt[:, 1048:1056]
            chained(V.tensor_reduce(den, gd, AX.X, ALU.add))
            chained(V.tensor_scalar(rt[:, 1056:1060], rt[:, 1040:1044], 1.0, None, ALU.add))
            chained(V.tensor_tensor(den, den, rt[:, 1056:1060], ALU.mult))
            chained(V.reciprocal(wts[:, 0:4], den))
            chained(V.tensor_tensor(wts[:, 4:8], wts[:, 0:4], rt[:, 1040:1044], ALU.mult))
            dve.wait_ge(s["route_psum"], 2)
            count, nblk, off = rt[:, 448:464], rt[:, 464:480], rt[:, 480:496]
            chained(V.tensor_copy(count, ps[2][:, 0:16]))
            chained(V.tensor_scalar(nblk, count, 0.0, None, ALU.is_gt))
            for k in range(1, NT):
                chained(V.scalar_tensor_tensor(out=nblk, in0=count, scalar=float(P * k), in1=nblk, op0=ALU.is_gt, op1=ALU.add))
            tri = rt[:, 512:768].rearrange("p (a b) -> p a b", a=16)
            chained(V.tensor_tensor(tri, c_("tri16").rearrange("p (a b) -> p a b", a=16),
                                    view(nblk, [[0, 16], [1, 16]]), ALU.mult))
            chained(V.tensor_reduce(off, tri, AX.X, ALU.add))
            before = rt[:, 768:1152][:, 0:16]
            chained(V.tensor_tensor(before, off, nblk, ALU.subtract))
            chained(V.tensor_scalar(before, before, float(P), -1.0, ALU.mult, ALU.add))
            slot = rt[:, 800:864]
            chained(V.tensor_tensor(slot.rearrange("p (t e) -> p t e", t=R), ps[1][:, 0:64].rearrange("p (t e) -> p t e", t=R),
                                    view(before, [[0, R], [1, 16]]), ALU.add))
            pos = rt[:, 864:872]
            for k in range(2):
                chained(V.tensor_tensor(rt[:, 880:944], slot, M[k], ALU.mult))
                chained(V.tensor_reduce(pos[:, 4 * k:4 * k + 4], rt[:, 880:944].rearrange("p (t e) -> p t e", t=R), AX.X, ALU.add))
            chained(V.tensor_copy(isml[:, 0:8], pos))
            nmax_blocks = 24
            cmp_ = rt[:, 1152:1152 + 16 * nmax_blocks].rearrange("p (b e) -> p b e", b=nmax_blocks)
            chained(V.tensor_tensor(cmp_, view(off, [[0, nmax_blocks], [1, 16]]),
                                    c_("iota_block").unsqueeze(2).to_broadcast([P, nmax_blocks, 16]), ALU.is_le))
            eb = rt[:, 1600:1600 + nmax_blocks]
            chained(V.tensor_reduce(eb, cmp_, AX.X, ALU.add))
            chained(V.tensor_scalar(eb, eb, float(NE - 1), None, ALU.min))
            V.tensor_scalar(isml[:, 32:33], off[:, 15:16], -1.0, None, ALU.add)
            V.tensor_copy(isml[:, 8:8 + nmax_blocks], eb).then_inc(s["routed"], 1)

            def hidden(b):
                dve.wait_ge(s["silu_done"], b + 1)
                dve.wait_ge(s["gu_psum"], 2 * b + 2)
                V.tensor_tensor(hb, ps[1], sg, ALU.mult).then_inc(s["hb_ready"], 1)

            def y_copy(b):
                dve.wait_ge(s["y_psum"], 2 * b + 2)
                if not (isinstance(b, int) and b == 0):
                    dve.wait_ge(s["y_out"], 16 * b)
                V.tensor_copy(Yb, psum[:, 4:6, :].rearrange("p a b -> p (a b)")).then_inc(s["yb_ready"], 1)

            hidden(0)
            hidden(1)
            y_copy(0)
            last = last_block(dve)
            with dve.Fori(2, last + 1) as b:
                hidden(b)
                y_copy(b - 1)
            y_copy(last)
            dve.wait_ge(s["y_out"], 16 * last + 16)
            V.tensor_copy(Yb[0:1, 0:1], psum[0:1, 4, 0:1]).then_inc(s["y_stored"], 1)
            for t in range(NT):
                for k in range(2):
                    n = 2 * t + k
                    dve.wait_ge(s[f"y_back{n % 4}"], 16 * (n // 4 + 1))
                    if k:
                        dve.wait_ge(s["y_used"], t + 1)
                    V.scalar_tensor_tensor(out=xres[:, t, :], in0=Yg[:, n % 4, :], scalar=wts[:, 4 * k + t:4 * k + t + 1],
                                           in1=xres[:, t, :], op0=ALU.mult, op1=ALU.add)\
                        .then_inc(s["res_ready" if k else "y_used"], 1)
            split_low(0, 0)
            norm_rows()
            free_gain(16)
            split_low(0, 1)

            def low_features(k):
                for m in range(8):
                    t, h_ = divmod(m, 2)
                    part = slice(4 * h_, 4 * h_ + 4), slice(P * t, P * t + P)
                    dve.wait_ge(s["ht_ready"], 8 * k + m + 1)
                    V.tensor_tensor(hT_lo[:, part[0], part[1]], ps[m].rearrange("p (c q) -> p c q", c=4),
                                    hT_hi[:, part[0], part[1]].bitcast(f32), ALU.subtract).then_inc(s["hT_low_ready"], 1)

            low_features(3)

            def ffn_half(g):
                base = HALF * g

                def chunk(v, i=0):
                    dve.wait_ge(s["ff_silu"], i + (base + v + 1))
                    V.tensor_tensor(sgb[:, v % 2, :], ps[2 * (v % 2) + 1], sgb[:, v % 2, :], ALU.mult).then_inc(s["gated"], 1)
                    split_low(g, v + 2, i)
                    dve.wait_ge(s["hid_high"], i + (base + v + 1))
                    lo, hi = (a[:, v, :] if isinstance(i, int) else a[:, ds(i + v, 1), :].rearrange("p a q -> p (a q)")
                              for a in (hid_lo, hid_hi))
                    V.tensor_tensor(lo, sgb[:, v % 2, :], hi.bitcast(f32), ALU.subtract).then_inc(s["ff_hid"], 1)

                for v in range(3):
                    chunk(v)
                with dve.Fori(0, 2) as i:
                    for q in range(4):
                        chunk(3 + q, 4 * i)
                for v in range(HALF + 2, UNITS):
                    split_low(g, v)
                if g % 2 == 0:
                    split_low(g + 1, 0)
                    split_low(g + 1, 1)
                else:
                    for m in range(8):
                        t, hf = divmod(m, 2)
                        part = hn[:, t, 512 * hf:512 * hf + 512]
                        dve.wait_ge(s["fd_psum"], 8 * g + m + 1)
                        V.tensor_tensor(part, ps[m], part, ALU.add).then_inc(s["f_evac"], 1)

            ffn_half(0)
            ffn_half(1)
            post_norm(0.5)
            norm_rows()
            free_gain(20)
            dve.wait_ge(s["z2_evac"], 16)
            zsq = carve(20672, 256)
            for t in range(NT):
                for k, (a, b_) in enumerate(((0, 256), (256, 384))):
                    ins = V.tensor_tensor_reduce(out=zsq[:, 0:b_ - a], in0=z3[:, t, a:b_], in1=z3[:, t, a:b_], scale=1.0,
                                                 scalar=0.0, op0=ALU.mult, op1=ALU.add, accum_out=ss[:, 16 + 4 * k + t:17 + 4 * k + t])
                    chained(ins)
            chained(variance(rstd[:, 16:20], ss[:, 16:20], 256))
            variance(rstd[:, 20:24], ss[:, 20:24], 128).then_inc(s["var_ready"], 1)
            inverse_root(rstd[:, 16:24])
            for t in range(NT):
                for k, (a, b_) in enumerate(((0, 256), (256, 384))):
                    chained(V.scalar_tensor_tensor(out=z3[:, t, a:b_], in0=z3[:, t, a:b_], scalar=rstd[:, 16 + 4 * k + t:17 + 4 * k + t],
                                                   in1=small[:, 600 + a:600 + b_], op0=ALU.mult, op1=ALU.mult))
            V.memset(nmax[:, 0:1], 0.0).then_inc(s["cn_ready"], 1)

            def na_table(g):
                if g >= H:
                    return
                dve.wait_ge(s["tab_psum"], H + g + 1)
                free_tab(dve, na, g)
                src = ps[7][:, 0:384].rearrange("p (j u) -> p j u", j=8)
                for v, off_ in enumerate((0, 8, 16)):
                    ins = V.tensor_tensor(tab2[:, g % 2, 256 * v:256 * v + 256].rearrange("p (j c) -> p j c", j=8),
                                          src[:, :, 16 - off_:48 - off_],
                                          c_("na_mask")[:, 256 * v:256 * v + 256].rearrange("p (j c) -> p j c", j=8), ALU.add)
                ins.then_inc(s["na_tab"], 1)

            attend_dve(dve, na, copy_out(na, hT[:, 0:4, :], 984), na_table)
            dve.wait_ge(s["nrm_psum"], 1)
            variance(rstd[:, 24:28], ps[7][:, 0:4], 512).then_inc(s["var_ready"], 1)
            inverse_root(rstd[:, 24:28])

            def rope(x1, x2, cos, sin, shape, n):
                t1, t2 = (ropes[:, k, 0:n] for k in range(2))
                if len(shape) == 4:
                    t1, t2 = (a.rearrange("p (t h f) -> p t h f", t=shape[1], h=shape[2]) for a in (t1, t2))
                    t3, t4 = (a.rearrange("p (t h f) -> p t h f", t=shape[1], h=shape[2])
                              for a in (hn[:, 1, 0:n], hn[:, 1, 512:512 + n]))
                else:
                    t1, t2 = (a.rearrange("p (t f) -> p t f", t=shape[1]) for a in (t1, t2))
                    t3, t4 = (a.rearrange("p (t f) -> p t f", t=shape[1]) for a in (hn[:, 1, 0:n], hn[:, 1, 512:512 + n]))
                V.tensor_tensor(t1, x1, cos, ALU.mult)
                V.tensor_tensor(t2, x2, sin, ALU.mult)
                V.tensor_tensor(t3, x2, cos, ALU.mult)
                chained(V.tensor_tensor(t4, x1, sin, ALU.mult))
                V.tensor_tensor(x1, t1, t2, ALU.subtract)
                chained(V.tensor_tensor(x2, t3, t4, ALU.add))

            dve.wait_ge(s["cn_psum"], 3)
            cos3, sin3 = (c_(n).rearrange("p (t f) -> p t f", t=NT) for n in ("cos", "sin"))
            rope(z3[:, :, 384:400], z3[:, :, 400:416], cos3, sin3, [P, NT, 16], 64)
            for t in range(NT):
                dve.wait_ge(s["mla_evac"], 4 * t + 4)
                ins = V.tensor_copy(kf[:, t, :].rearrange("p (h n) -> p h n", h=H)[:, :, 64:96],
                                    view(z3[:, t, 384:416], [[0, H], [1, 32]]))
            ins.then_inc(s["roped"], 1)
            for t in range(NT):
                q_ = qz[:, t, :].rearrange("p (h n) -> p h n", h=H)
                ct, st_ = (view(c_(n), [[0, H], [1, 16]], 16 * t) for n in ("cos", "sin"))
                rope(q_[:, :, 64:80], q_[:, :, 80:96], ct, st_, [P, H, 16], 128)
            V.memset(nmax[:, 0:1], 0.0).then_inc(s["roped"], 1)
            for j in range(1, 16, 2):
                dve.wait_ge(s["mt_psum"], j + 1)
                dst = qTm if j < 8 else kTm
                V.tensor_copy(dst[0:96, j % 8, :], ps[j % 3][0:96]).then_inc(s["mt_dve"], 1)
            dve.wait_ge(s["mla_tab"], 1)
            attend_dve(dve, mla, copy_out(mla, hT[:, 4:8, :], 988))
            dve.wait_ge(s["nrm_psum"], 2)
            variance(rstd[:, 28:32], ps[7][:, 4:8], 512).then_inc(s["var_ready"], 1)
            inverse_root(rstd[:, 28:32])
            for q in range(8):
                hf, t = divmod(q, 4)
                f_ = hn[:, t, 512 * hf:512 * hf + 512]
                dve.wait_ge(s["o2_psum"], 2 * q + 1)
                chained(V.tensor_scalar(f_, ps[(2 * q) % 6], rstd[:, 24 + t:25 + t], None, ALU.mult))
                dve.wait_ge(s["o2_psum"], 2 * q + 2)
                V.scalar_tensor_tensor(out=f_, in0=ps[(2 * q + 1) % 6], scalar=rstd[:, 28 + t:29 + t], in1=f_,
                                       op0=ALU.mult, op1=ALU.add).then_inc(s["f_evac"], 1)
            post_norm(1.0)
            split_low(2, 0)
            norm_rows()
            free_gain(24)
            split_low(2, 1)
            low_features(5)
            ffn_half(2)
            ffn_half(3)
            post_norm(0.5)


_INS = ["x", "norm_mix_g", "w_in", "b_forget", "fox_q_g", "fox_k_g", "nsa_q_g", "nsa_k_g", "cmp_k_w1", "cmp_k_w2",
        "cmp_k_pos", "cmp_v_w1", "cmp_v_w2", "cmp_v_pos", "w_fox_up", "w_nsa_up", "w_out", "norm_ffn_g", "w_group",
        "b_group", "w_router", "b_router", "w_gate", "w_up", "w_down", "ffn1_pre_g_2", "ffn1_w_gu_2", "ffn1_w_down_2",
        "ffn1_post_g_2", "mix_pre_g_2", "w_in_2", "na_rpb_2", "mla_q_norm_g_2", "mla_w_uq_2", "mla_kv_norm_g_2",
        "mla_w_ukv_2", "na_out_norm_g_2", "mla_out_norm_g_2", "w_out_2", "mix_post_g_2", "ffn2_pre_g_2",
        "ffn2_w_gu_2", "ffn2_w_down_2", "ffn2_post_g_2"]


def kernel(**inputs):
    import numpy as _np
    import concourse.bacc as _bacc
    from concourse import mybir as _mybir
    from concourse.bass_utils import run_bass_kernel_spmd as _run

    nc = _bacc.Bacc("TRN2", target_bir_lowering=False, num_devices=1)
    arrays, w = {}, {}
    arrays["in_consts"] = shape_constants()
    w["consts"] = nc.dram_tensor("in_consts", arrays["in_consts"].shape, _mybir.dt.float32, kind="ExternalInput").ap()
    for name in _INS:
        a = _np.ascontiguousarray(inputs[name])
        arrays["in_" + name] = a
        w[name] = nc.dram_tensor("in_" + name, a.shape, _mybir.dt.from_np(a.dtype), kind="ExternalInput").ap()
    out = nc.dram_tensor("out_0", (1, T, D), _mybir.dt.float32, kind="ExternalOutput").ap()
    build_blocks(nc, w, out)
    r = _run(nc, [arrays], core_ids=[0])
    return r.results[0]["out_0"]
```
